# Optimizing a Trainium2 kernel written in Bass

```python
import math
import jax, jax.numpy as jnp
from jax import lax
import numpy as np
import jax
import jax.numpy as jnp

D_MODEL = 1024
BATCH = 1
SEQ = 256
DEPTH = 2

MLA_HEADS = 8
MLA_NOPE = 64
MLA_ROPE = 32
MLA_V = 64
MLA_QK = MLA_NOPE + MLA_ROPE
MLA_Q_RANK = 256
MLA_KV_RANK = 128
ROPE_THETA = 10000.0
Q_BLOCK = 128
MOBA_HEADS = 8
MOBA_HEAD_DIM = 64
MOBA_W = MOBA_HEADS * MOBA_HEAD_DIM
MOBA_BLOCK = 256
MOBA_TOPK = 3
MOBA_Q_CHUNK = 16
S5_GROUP = 16
S5_GROUPS = D_MODEL // S5_GROUP
S5_STATE = 64
S5_CHUNK = 128
DT_MIN = 1e-3
DT_MAX = 1e-1
D_FF = 4 * D_MODEL
EPS = 1e-6

N_EVEN = (DEPTH + 1) // 2
N_ODD = DEPTH // 2
IN_SIZES = [MLA_Q_RANK, MLA_KV_RANK, MLA_ROPE, MOBA_W, MOBA_W, MOBA_W]
IN_COLS = sum(IN_SIZES)
IN_SPLITS = [int(v) for v in np.cumsum(IN_SIZES)[:-1]]
MIX_WIDTH = MLA_HEADS * MLA_V + MOBA_W


def rms_norm(x, g):
    xf = x.astype(jnp.float32)
    y = xf * lax.rsqrt(jnp.mean(xf * xf, axis=-1, keepdims=True) + EPS)
    return (y * g.astype(jnp.float32)).astype(x.dtype)

def apply_rope(x, pos):
    half = x.shape[-1] // 2
    inv = ROPE_THETA ** (-jnp.arange(half, dtype=jnp.float32) / half)
    ang = pos.astype(jnp.float32)[:, None] * inv[None, :]
    cos = jnp.cos(ang).astype(x.dtype)
    sin = jnp.sin(ang).astype(x.dtype)
    x1, x2 = x[..., :half], x[..., half:]
    return jnp.concatenate([x1 * cos - x2 * sin, x1 * sin + x2 * cos], axis=-1)

def causal_attention_blocks(q, k, v):
    S = q.shape[2]
    outs = []
    for i in range(S // Q_BLOCK):
        lo, hi = i * Q_BLOCK, (i + 1) * Q_BLOCK
        s = jnp.einsum('bhqd,bhkd->bhqk', q[:, :, lo:hi], k[:, :, :hi]).astype(jnp.float32)
        mask = jnp.arange(hi)[None, :] <= jnp.arange(lo, hi)[:, None]
        p = jax.nn.softmax(jnp.where(mask, s, -jnp.inf), axis=-1).astype(v.dtype)
        outs.append(jnp.einsum('bhqk,bhkd->bhqd', p, v[:, :, :hi]))
    return jnp.concatenate(outs, axis=2)

def moba_attention(q, k, v):
    B, H, S, d = q.shape
    nb = -(-S // MOBA_BLOCK)
    pad = nb * MOBA_BLOCK - S
    kp = jnp.pad(k, ((0, 0), (0, 0), (0, pad), (0, 0)))
    vp = jnp.pad(v, ((0, 0), (0, 0), (0, pad), (0, 0)))
    k_blocks = kp.reshape(B, H, nb, MOBA_BLOCK, d)
    kv_blocks = jnp.concatenate([k_blocks, vp.reshape(B, H, nb, MOBA_BLOCK, d)], axis=-1)
    k_mean = jnp.mean(k_blocks.astype(jnp.float32), axis=3).astype(k.dtype)
    n_sel = min(MOBA_TOPK, nb - 1)
    b_idx = jnp.arange(B)[:, None, None, None]
    h_idx = jnp.arange(H)[None, :, None, None]
    blk_pos = jnp.arange(MOBA_BLOCK)

    def chunk(c):
        t0 = c * MOBA_Q_CHUNK
        qc = lax.dynamic_slice_in_dim(q, t0, MOBA_Q_CHUNK, axis=2)
        t = t0 + jnp.arange(MOBA_Q_CHUNK)
        cur = t0 // MOBA_BLOCK
        kv_own = lax.dynamic_index_in_dim(kv_blocks, cur, axis=2, keepdims=False)
        s_own = jnp.einsum('bhqd,bhld->bhql', qc, kv_own[..., :d]).astype(jnp.float32)
        s_own = jnp.where(cur * MOBA_BLOCK + blk_pos[None, :] <= t[:, None], s_own, -jnp.inf)
        if n_sel == 0:
            p = jax.nn.softmax(s_own, axis=-1).astype(v.dtype)
            return jnp.einsum('bhql,bhld->bhqd', p, kv_own[..., d:])
        gate = jnp.einsum('bhqd,bhnd->bhqn', qc, k_mean).astype(jnp.float32)
        gate = jnp.where(jnp.arange(nb) < cur, gate, -jnp.inf)
        _, sel = lax.top_k(gate, n_sel)
        sel_ok = jnp.arange(n_sel) < cur
        kv_sel = kv_blocks[b_idx, h_idx, sel]
        s_sel = jnp.einsum('bhqd,bhqnld->bhqnl', qc, kv_sel[..., :d]).astype(jnp.float32)
        s_sel = jnp.where(sel_ok[:, None], s_sel, -jnp.inf)
        s_sel = s_sel.reshape(B, H, MOBA_Q_CHUNK, n_sel * MOBA_BLOCK)
        p = jax.nn.softmax(jnp.concatenate([s_sel, s_own], axis=-1), axis=-1).astype(v.dtype)
        p_sel = p[..., :n_sel * MOBA_BLOCK].reshape(B, H, MOBA_Q_CHUNK, n_sel, MOBA_BLOCK)
        p_own = p[..., n_sel * MOBA_BLOCK:]
        return (jnp.einsum('bhqnl,bhqnld->bhqd', p_sel, kv_sel[..., d:])
                + jnp.einsum('bhql,bhld->bhqd', p_own, kv_own[..., d:]))

    outs = lax.map(chunk, jnp.arange(S // MOBA_Q_CHUNK))
    return outs.transpose(1, 2, 0, 3, 4).reshape(B, H, S, d)

def attn_mixer(h, w_in, g_cq, w_uq, g_ckv, w_ukv, g_qn_mla, g_kn_mla, g_qn_moba, g_kn_moba, w_o):
    B, S, _ = h.shape
    pos = jnp.arange(S)
    c_q, c_kv, k_r, q_b, k_b, v_b = jnp.split(h @ w_in, IN_SPLITS, axis=-1)
    q = (rms_norm(c_q, g_cq) @ w_uq).reshape(B, S, MLA_HEADS, MLA_QK).transpose(0, 2, 1, 3)
    kv = (rms_norm(c_kv, g_ckv) @ w_ukv).reshape(B, S, MLA_HEADS, MLA_NOPE + MLA_V).transpose(0, 2, 1, 3)
    k_nope, v = kv[..., :MLA_NOPE], kv[..., MLA_NOPE:]
    q = jnp.concatenate([q[..., :MLA_NOPE], apply_rope(q[..., MLA_NOPE:], pos)], axis=-1)
    k_rope = jnp.broadcast_to(apply_rope(k_r, pos)[:, None], (B, MLA_HEADS, S, MLA_ROPE))
    k = jnp.concatenate([k_nope, k_rope], axis=-1)
    q = rms_norm(q, g_qn_mla) * (MLA_QK ** -0.5)
    k = rms_norm(k, g_kn_mla)
    o_mla = causal_attention_blocks(q, k, v)
    def heads(t):
        return t.reshape(B, S, MOBA_HEADS, MOBA_HEAD_DIM).transpose(0, 2, 1, 3)
    qm = rms_norm(heads(q_b), g_qn_moba) * (MOBA_HEAD_DIM ** -0.5)
    km = rms_norm(heads(k_b), g_kn_moba)
    o_moba = moba_attention(qm, km, heads(v_b))
    o = jnp.concatenate([o_mla.transpose(0, 2, 1, 3).reshape(B, S, MLA_HEADS * MLA_V),
                         o_moba.transpose(0, 2, 1, 3).reshape(B, S, MOBA_W)], axis=-1)
    return o @ w_o

def s5_mixer(h, lam_re, lam_im, log_dt, b_re, b_im, c_re, c_im, d_skip, w_glu):
    B, S, D = h.shape
    f32 = jnp.float32
    u = h.astype(f32)
    lam = lax.complex(lam_re.astype(f32), lam_im.astype(f32))
    dt = jnp.exp(log_dt.astype(f32))[:, None]
    a_bar = jnp.exp(lam * dt)
    b_bar = ((a_bar - 1.0) / lam)[..., None] * lax.complex(b_re.astype(f32), b_im.astype(f32))
    cmat = lax.complex(c_re.astype(f32), c_im.astype(f32))
    nc = S // S5_CHUNK
    u_chunks = u.reshape(B, nc, S5_CHUNK, S5_GROUPS, S5_GROUP).transpose(1, 2, 0, 3, 4)
    steps = jnp.arange(1, S5_CHUNK + 1, dtype=f32)
    a_pow = jnp.exp(lam[None] * dt[None] * steps[:, None, None])
    a_el = jnp.broadcast_to(a_bar, (S5_CHUNK, 1, S5_GROUPS, S5_STATE))

    def combine(e1, e2):
        a1, b1 = e1
        a2, b2 = e2
        return a1 * a2, a2 * b1 + b2

    def step(state, uc):
        bu = jnp.einsum('gpi,lbgi->lbgp', b_bar, uc.astype(jnp.complex64))
        _, hs = lax.associative_scan(combine, (a_el, bu), axis=0)
        hs = hs + a_pow[:, None] * state[None]
        y = jnp.einsum('gop,lbgp->lbgo', cmat, hs).real
        return hs[-1], y

    state0 = jnp.zeros((B, S5_GROUPS, S5_STATE), jnp.complex64)
    _, ys = lax.scan(step, state0, u_chunks)
    y = ys.transpose(2, 0, 1, 3, 4).reshape(B, S, D) + d_skip.astype(f32) * u
    g = jax.nn.gelu(y).astype(h.dtype)
    val, gate = jnp.split(g @ w_glu, 2, axis=-1)
    return val * jax.nn.sigmoid(gate)

def sq_relu_mlp(h, w1, w2):
    return jnp.square(jax.nn.relu(h @ w1)) @ w2

def first_inputs(seed: int = 0) -> dict:
    key = jax.random.key(seed)
    ks = iter(jax.random.split(key, 32))
    f32 = jnp.float32

    def nrm(shape, scale):
        return jax.random.normal(next(ks), shape, f32) * scale

    def gain(shape):
        return 1.0 + 0.02 * jax.random.normal(next(ks), shape, f32)

    n_idx = jnp.arange(S5_STATE, dtype=f32)
    return {
        "x": nrm((BATCH, SEQ, D_MODEL), 1.0),
        "mix_norm_g": gain((DEPTH, D_MODEL)),
        "ffn_norm_g": gain((DEPTH, D_MODEL)),
        "w_in": nrm((N_EVEN, D_MODEL, IN_COLS), D_MODEL ** -0.5),
        "g_cq": gain((N_EVEN, MLA_Q_RANK)),
        "w_uq": nrm((N_EVEN, MLA_Q_RANK, MLA_HEADS * MLA_QK), MLA_Q_RANK ** -0.5),
        "g_ckv": gain((N_EVEN, MLA_KV_RANK)),
        "w_ukv": nrm((N_EVEN, MLA_KV_RANK, MLA_HEADS * (MLA_NOPE + MLA_V)), MLA_KV_RANK ** -0.5),
        "g_qn_mla": gain((N_EVEN, MLA_QK)),
        "g_kn_mla": gain((N_EVEN, MLA_QK)),
        "g_qn_moba": gain((N_EVEN, MOBA_HEAD_DIM)),
        "g_kn_moba": gain((N_EVEN, MOBA_HEAD_DIM)),
        "w_o": nrm((N_EVEN, MIX_WIDTH, D_MODEL), MIX_WIDTH ** -0.5),
        "lam_re": -0.5 + nrm((N_ODD, S5_GROUPS, S5_STATE), 0.01),
        "lam_im": math.pi * n_idx + nrm((N_ODD, S5_GROUPS, S5_STATE), 0.01),
        "log_dt": jax.random.uniform(next(ks), (N_ODD, S5_GROUPS), f32, math.log(DT_MIN), math.log(DT_MAX)),
        "b_re": nrm((N_ODD, S5_GROUPS, S5_STATE, S5_GROUP), (2 * S5_GROUP) ** -0.5),
        "b_im": nrm((N_ODD, S5_GROUPS, S5_STATE, S5_GROUP), (2 * S5_GROUP) ** -0.5),
        "c_re": nrm((N_ODD, S5_GROUPS, S5_GROUP, S5_STATE), (2 * S5_STATE) ** -0.5),
        "c_im": nrm((N_ODD, S5_GROUPS, S5_GROUP, S5_STATE), (2 * S5_STATE) ** -0.5),
        "d_skip": nrm((N_ODD, D_MODEL), 1.0),
        "w_glu": nrm((N_ODD, D_MODEL, 2 * D_MODEL), D_MODEL ** -0.5),
        "w_ff1": nrm((DEPTH, D_MODEL, D_FF), D_MODEL ** -0.5),
        "w_ff2": nrm((DEPTH, D_FF, D_MODEL), D_FF ** -0.5),
    }

def first_block(x, mix_norm_g, ffn_norm_g, w_in, g_cq, w_uq, g_ckv, w_ukv, g_qn_mla, g_kn_mla,
              g_qn_moba, g_kn_moba, w_o, lam_re, lam_im, log_dt, b_re, b_im, c_re, c_im,
              d_skip, w_glu, w_ff1, w_ff2):
    for layer in range(DEPTH):
        h = rms_norm(x, mix_norm_g[layer])
        i = layer // 2
        if layer % 2 == 0:
            x = x + attn_mixer(h, w_in[i], g_cq[i], w_uq[i], g_ckv[i], w_ukv[i], g_qn_mla[i],
                               g_kn_mla[i], g_qn_moba[i], g_kn_moba[i], w_o[i])
        else:
            x = x + s5_mixer(h, lam_re[i], lam_im[i], log_dt[i], b_re[i], b_im[i], c_re[i],
                             c_im[i], d_skip[i], w_glu[i]).astype(x.dtype)
        x = x + sq_relu_mlp(rms_norm(x, ffn_norm_g[layer]), w_ff1[layer], w_ff2[layer])
    return x


DEPTH_2 = 1

D_MIX = D_MODEL
CONV_CH = D_MIX // 2
CONV_GROUPS = 8
CONV_K = 3
N_HEADS = 8
N_KV_HEADS = 2
HEAD_DIM = 64
ATTN_WIDTH = N_HEADS * HEAD_DIM
KV_WIDTH = N_KV_HEADS * HEAD_DIM
IN_WIDTH = 3 * CONV_CH + ATTN_WIDTH + 2 * KV_WIDTH
WINDOW = 128
BLOCK = 128
N_BUCKETS = 32
MAX_DISTANCE = 128
PEER_HEADS = 8
PEER_NKEYS = 128
PEER_EXPERTS = PEER_NKEYS * PEER_NKEYS
PEER_DK = 128
PEER_TOPK = 16
PEER_CHUNK = 128


def rms_norm_2(x, g):
    xf = x.astype(jnp.float32)
    y = xf * lax.rsqrt(jnp.mean(xf * xf, axis=-1, keepdims=True) + EPS)
    return (y * g.astype(jnp.float32)).astype(x.dtype)

def group_rms_norm(y, g, n_groups):
    w = y.shape[-1]
    yg = y.reshape(y.shape[:-1] + (n_groups, w // n_groups))
    return rms_norm_2(yg, g.reshape(n_groups, w // n_groups)).reshape(y.shape)

def t5_bucket(dist):
    max_exact = N_BUCKETS // 2
    d = jnp.maximum(dist, 1).astype(jnp.float32)
    large = max_exact + (jnp.log(d / max_exact) / math.log(MAX_DISTANCE / max_exact)
                         * (N_BUCKETS - max_exact)).astype(jnp.int32)
    large = jnp.minimum(large, N_BUCKETS - 1)
    return jnp.where(dist < max_exact, dist, large)

def short_conv(b_gate, c_gate, h, conv_w):
    u = c_gate * h
    s = u.shape[1]
    up = jnp.pad(u, ((0, 0), (CONV_K - 1, 0), (0, 0)))
    y = conv_w[0] * up[:, 0:s]
    for j in range(1, CONV_K):
        y = y + conv_w[j] * up[:, j:j + s]
    return b_gate * y

def window_attention(q, k, v, rel_bias, sinks):
    bsz, s = q.shape[0], q.shape[1]
    nb = s // BLOCK
    grp = N_HEADS // N_KV_HEADS
    qb = q.reshape(bsz, nb, BLOCK, N_KV_HEADS, grp, HEAD_DIM)
    kb = k.reshape(bsz, nb, BLOCK, N_KV_HEADS, HEAD_DIM)
    vb = v.reshape(bsz, nb, BLOCK, N_KV_HEADS, HEAD_DIM)

    def with_prev(t):
        prev = jnp.concatenate([jnp.zeros_like(t[:, :1]), t[:, :-1]], axis=1)
        return jnp.concatenate([prev, t], axis=2)

    kw = with_prev(kb)
    vw = with_prev(vb)
    scores = jnp.einsum('bnqkgd,bnjkd->bnkgqj', qb, kw).astype(jnp.float32) * (HEAD_DIM ** -0.5)

    qi = jnp.arange(BLOCK)[:, None]
    kj = jnp.arange(2 * BLOCK)[None, :]
    dist = qi + BLOCK - kj
    bias = rel_bias.astype(jnp.float32)[t5_bucket(jnp.maximum(dist, 0))]
    bias = bias.transpose(2, 0, 1).reshape(N_KV_HEADS, grp, BLOCK, 2 * BLOCK)
    blk = jnp.arange(nb)[:, None, None]
    valid = (dist >= 0) & (dist < WINDOW) & (blk * BLOCK - BLOCK + kj >= 0)
    scores = jnp.where(valid[None, :, None, None], scores + bias, -jnp.inf)

    sink = sinks.astype(jnp.float32).reshape(N_KV_HEADS, grp)[None, None, :, :, None]
    m = jnp.maximum(scores.max(axis=-1), sink)
    p = jnp.exp(scores - m[..., None])
    denom = p.sum(axis=-1) + jnp.exp(sink - m)
    o = jnp.einsum('bnkgqj,bnjkd->bnkgqd', p, vw.astype(jnp.float32)) / denom[..., None]
    o = o.transpose(0, 1, 4, 2, 3, 5).reshape(bsz, s, ATTN_WIDTH)
    return o.astype(q.dtype)

def peer_ffn(h, wq, keys, u_tab, v_tab):
    bsz, s, d = h.shape

    def chunk(ht):
        t = ht.shape[0]
        q = (ht @ wq).reshape(t, PEER_HEADS, 2, PEER_DK)
        sa = jnp.einsum('thd,hnd->thn', q[:, :, 0], keys[0]).astype(jnp.float32)
        sb = jnp.einsum('thd,hnd->thn', q[:, :, 1], keys[1]).astype(jnp.float32)
        va, ia = lax.top_k(sa, PEER_TOPK)
        vb, ib = lax.top_k(sb, PEER_TOPK)
        cand = (va[..., :, None] + vb[..., None, :]).reshape(t, PEER_HEADS, PEER_TOPK * PEER_TOPK)
        cidx = (ia[..., :, None] * PEER_NKEYS + ib[..., None, :]).reshape(t, PEER_HEADS, PEER_TOPK * PEER_TOPK)
        top, pos = lax.top_k(cand, PEER_TOPK)
        eidx = jnp.take_along_axis(cidx, pos, axis=-1)
        g = jax.nn.softmax(top, axis=-1).astype(ht.dtype)
        u = u_tab[eidx]
        v = v_tab[eidx]
        a = jax.nn.gelu(jnp.einsum('thkd,td->thk', u, ht))
        return jnp.einsum('thk,thkd->td', g * a, v)

    out = lax.map(chunk, h.reshape(-1, PEER_CHUNK, d))
    return out.reshape(bsz, s, d)

def second_inputs(seed: int = 0) -> dict:
    key = jax.random.key(seed)
    ks = jax.random.split(key, 20)
    f32 = jnp.float32
    nrm = lambda k, shp, sc: jax.random.normal(k, shp, f32) * sc
    return {
        'x': nrm(ks[0], (BATCH, SEQ, D_MODEL), 1.0),
        'c': nrm(ks[1], (BATCH, D_MODEL), 1.0),
        'w_ada': nrm(ks[2], (DEPTH_2, D_MODEL, 6 * D_MODEL), 0.5 * D_MODEL ** -0.5),
        'b_ada': nrm(ks[3], (DEPTH_2, 6 * D_MODEL), 0.02),
        'norm1_g': 1.0 + nrm(ks[4], (DEPTH_2, D_MODEL), 0.1),
        'w_in': nrm(ks[5], (DEPTH_2, D_MODEL, IN_WIDTH), D_MODEL ** -0.5),
        'conv_w': nrm(ks[6], (DEPTH_2, CONV_K, CONV_CH), CONV_K ** -0.5),
        'q_norm_g': 1.0 + nrm(ks[7], (DEPTH_2, HEAD_DIM), 0.1),
        'k_norm_g': 1.0 + nrm(ks[8], (DEPTH_2, HEAD_DIM), 0.1),
        'sinks': nrm(ks[9], (DEPTH_2, N_HEADS), 0.5),
        'rel_bias': nrm(ks[10], (N_BUCKETS, N_HEADS), 0.5),
        'conv_out_g': 1.0 + nrm(ks[11], (DEPTH_2, CONV_CH), 0.1),
        'attn_out_g': 1.0 + nrm(ks[12], (DEPTH_2, ATTN_WIDTH), 0.1),
        'w_out': nrm(ks[13], (DEPTH_2, D_MIX, D_MODEL), D_MIX ** -0.5),
        'norm2_g': 1.0 + nrm(ks[14], (DEPTH_2, D_MODEL), 0.1),
        'peer_wq': nrm(ks[15], (DEPTH_2, D_MODEL, PEER_HEADS * 2 * PEER_DK), D_MODEL ** -0.5),
        'peer_keys': nrm(ks[16], (DEPTH_2, 2, PEER_HEADS, PEER_NKEYS, PEER_DK), PEER_DK ** -0.5),
        'peer_u': nrm(ks[17], (DEPTH_2, PEER_EXPERTS, D_MODEL), D_MODEL ** -0.5),
        'peer_v': nrm(ks[18], (DEPTH_2, PEER_EXPERTS, D_MODEL), 0.5),
    }

def second_block(x, c, w_ada, b_ada, norm1_g, w_in, conv_w, q_norm_g, k_norm_g, sinks, rel_bias,
              conv_out_g, attn_out_g, w_out, norm2_g, peer_wq, peer_keys, peer_u, peer_v):
    bsz, s, _ = x.shape
    cond = jax.nn.silu(c)
    splits = [CONV_CH, 2 * CONV_CH, 3 * CONV_CH, 3 * CONV_CH + ATTN_WIDTH,
              3 * CONV_CH + ATTN_WIDTH + KV_WIDTH]
    for l in range(DEPTH_2):
        mod = cond @ w_ada[l] + b_ada[l]
        sh1, sc1, g1, sh2, sc2, g2 = jnp.split(mod, 6, axis=-1)

        h = rms_norm_2(x, norm1_g[l]) * (1.0 + sc1[:, None]) + sh1[:, None]
        proj = h @ w_in[l]
        b_gate, c_gate, hc, q, k, v = jnp.split(proj, splits, axis=-1)
        y_conv = short_conv(b_gate, c_gate, hc, conv_w[l])
        q = rms_norm_2(q.reshape(bsz, s, N_HEADS, HEAD_DIM), q_norm_g[l])
        k = rms_norm_2(k.reshape(bsz, s, N_KV_HEADS, HEAD_DIM), k_norm_g[l])
        v = v.reshape(bsz, s, N_KV_HEADS, HEAD_DIM)
        y_attn = window_attention(q, k, v, rel_bias, sinks[l])
        mixed = jnp.concatenate([group_rms_norm(y_conv, conv_out_g[l], CONV_GROUPS),
                                 group_rms_norm(y_attn, attn_out_g[l], N_HEADS)], axis=-1)
        x = x + g1[:, None] * (mixed @ w_out[l])

        h2 = rms_norm_2(x, norm2_g[l]) * (1.0 + sc2[:, None]) + sh2[:, None]
        x = x + g2[:, None] * peer_ffn(h2, peer_wq[l], peer_keys[l], peer_u[l], peer_v[l])
    return x


def setup_inputs(seed=0):
    out = dict(first_inputs(seed))
    for name, value in second_inputs(seed + 1).items():
        if name != "x":
            out[name + "_2"] = value
    return out


def reference(
    x, mix_norm_g, ffn_norm_g, w_in, g_cq, w_uq, g_ckv, w_ukv, g_qn_mla, g_kn_mla, g_qn_moba,
    g_kn_moba, w_o, lam_re, lam_im, log_dt, b_re, b_im, c_re, c_im, d_skip, w_glu, w_ff1, w_ff2,
    c_2, w_ada_2, b_ada_2, norm1_g_2, w_in_2, conv_w_2, q_norm_g_2, k_norm_g_2, sinks_2,
    rel_bias_2, conv_out_g_2, attn_out_g_2, w_out_2, norm2_g_2, peer_wq_2, peer_keys_2,
    peer_u_2, peer_v_2,
):
    x = first_block(
        x, mix_norm_g, ffn_norm_g, w_in, g_cq, w_uq, g_ckv, w_ukv, g_qn_mla, g_kn_mla,
        g_qn_moba, g_kn_moba, w_o, lam_re, lam_im, log_dt, b_re, b_im, c_re, c_im, d_skip,
        w_glu, w_ff1, w_ff2,
    )
    return second_block(
        x, c_2, w_ada_2, b_ada_2, norm1_g_2, w_in_2, conv_w_2, q_norm_g_2, k_norm_g_2, sinks_2,
        rel_bias_2, conv_out_g_2, attn_out_g_2, w_out_2, norm2_g_2, peer_wq_2, peer_keys_2,
        peer_u_2, peer_v_2,
    )


_drawn_inputs = setup_inputs


def setup_inputs(seed=0):
    import zlib

    import numpy as np

    out = dict(_drawn_inputs(seed))
    spreads = {}
    factors = {'mix_norm_g': 5.642,
     'g_cq': 8.0,
     'g_ckv': 8.0,
     'g_qn_mla': 8.0,
     'g_kn_mla': 8.0,
     'g_qn_moba': 8.0,
     'g_kn_moba': 8.0,
     'lam_re': 64.0,
     'lam_im': 30.368,
     'log_dt': 34.544,
     'b_re': 40.392,
     'b_im': 41.152,
     'c_re': 42.0,
     'c_im': 40.736,
     'b_ada_2': 3.953,
     'norm1_g_2': 2.674,
     'q_norm_g_2': 8.0,
     'k_norm_g_2': 8.0,
     'sinks_2': 200.0,
     'rel_bias_2': 11.591,
     'conv_out_g_2': 102.439,
     'attn_out_g_2': 100.492,
     'norm2_g_2': 30.16,
     'ffn_norm_g': 4.872,
     'peer_wq_2': 3.788,
     'peer_keys_2': 3.868,
     'peer_u_2': 4.853,
     'peer_v_2': 3.876}
    for name, (base, spread) in spreads.items():
        noise = np.random.default_rng([zlib.crc32(name.encode()), seed]).standard_normal(out[name].shape)
        drawn = base * np.exp(spread * noise) if base else spread * noise
        out[name] = jnp.asarray(drawn.astype(out[name].dtype))
    for name, factor in factors.items():
        out[name] = (out[name] * factor).astype(out[name].dtype)
    return out
```

```python
import math
from contextlib import ExitStack

import concourse.bass as bass
from concourse import mybir
import numpy as np

ALU = mybir.AluOpType
ACT = mybir.ActivationFunctionType
AX = mybir.AxisListType
F32 = mybir.dt.float32
U32 = mybir.dt.uint32
I32 = mybir.dt.int32

NEG = -1.0e30
EPS = 1e-6
PIECE = 2048
NSLOT = 5
NGA = 64

OFF_X = 0
OFF_RING = 32768
OFF_XR = OFF_RING + NSLOT * PIECE
OFF_HT = OFF_XR + 2048
OFF_GB = OFF_HT + 2048
OFF_HN = OFF_GB + 2048
OFF_SM = OFF_HN + 2048


def small_layout():
    cols = [("ident", 128), ("cmask", 128), ("iota", 128), ("bones", 128), ("ones", 128),
            ("cos", 32), ("sin", 32), ("hpar", 2), ("iota16", 16),
            ("mixg", 16), ("ffng", 16), ("n1g", 8), ("n2g", 8), ("gcq", 2), ("gckv", 1),
            ("gqmla", 1), ("gkmla", 1), ("gqmoba", 1), ("gkmoba", 1), ("qng", 1), ("kng", 1),
            ("c", 8), ("bada", 32), ("convw", 12), ("convg", 4), ("attng", 4), ("dskip", 8),
            ("sinks", 8), ("lre", 32), ("lim", 32), ("ldt", 32)]
    at, out = 0, {}
    for name, n in cols:
        out[name] = (at, n)
        at += n
    return out, at


SML, SMN = small_layout()
OFF_ST = OFF_SM + SMN
NST = 53200 - OFF_ST


class Line:

    def __init__(self, eng, sem):
        self.eng, self.sem, self.n, self.todo, self.seen = eng, sem, 0, [], {}
        self.prev = None

    def wait(self, *after):
        for tok in after:
            if tok is None:
                continue
            if isinstance(tok, list):
                self.wait(*tok)
                continue
            sem, val = tok
            if self.seen.get(id(sem), 0) < val:
                self.seen[id(sem)] = val
                self.todo.append(lambda s=sem, v=val: self.eng.wait_ge(s, v))

    def __call__(self, fn, *after, inc=True):
        self.wait(*after)
        if inc:
            self.n += 1
            self.todo.append(lambda: fn(self.eng).then_inc(self.sem, 1))
            self.prev = (self.sem, self.n)
            return self.prev
        self.todo.append(lambda: fn(self.eng))
        return None

    def dma(self, fn, sem, *after):
        self.wait(*after)
        self.todo.append(lambda: fn(self.eng).then_inc(sem, 16))

    def run(self):
        for t in self.todo:
            t()


def build(nc, T, out):
    ctx = ExitStack()
    with ctx:
        ar = ctx.enter_context(nc.sbuf_tensor("arena", [128, 53200], F32))
        ps = [ctx.enter_context(nc.psum_tensor(f"ps{i}", [128, 512], F32)) for i in range(8)]
        sem = lambda n: ctx.enter_context(nc.semaphore(n))
        P = Line(nc.tensor, sem("pe_done"))
        D = Line(nc.vector, sem("dve_done"))
        A = Line(nc.scalar, sem("act_done"))
        G = Line(nc.gpsimd, sem("pool_done"))
        ring_sem = [sem(f"ring{i}") for i in range(NSLOT)]
        in_sem = sem("inputs")
        out_sem = sem("outputs")
        key_sem = sem("bias_in")

        def V(off, *dims, p0=0, p1=128):
            n = 1
            for d in dims:
                n *= d
            ap = ar[p0:p1, off:off + n]
            if len(dims) == 2:
                ap = ap.rearrange("p (a b) -> p a b", a=dims[0])
            elif len(dims) == 3:
                ap = ap.rearrange("p (a b c) -> p a b c", a=dims[0], b=dims[1])
            return ap

        def sm(name, p1=128):
            o, n = SML[name]
            return ar[0:p1, OFF_SM + o:OFF_SM + o + n]

        def B(ap, shape):
            return ap.to_broadcast(list(shape))

        def bank(i, *dims, off=0):
            n = 1
            for d in dims:
                n *= d
            ap = ps[i][:, off:off + n]
            if len(dims) == 2:
                ap = ap.rearrange("p (a b) -> p a b", a=dims[0])
            elif len(dims) == 3:
                ap = ap.rearrange("p (a b c) -> p a b c", a=dims[0], b=dims[1])
            return ap

        fr = [[] for _ in range(8)]

        st_at = [0]

        def stat(n):
            assert st_at[0] + n <= NST - 32
            o = OFF_ST + st_at[0]
            st_at[0] += n
            return o

        items = []
        release = {}

        def get(ap, words=PIECE):
            i = len(items)
            items.append((ap, words))
            slot = i % NSLOT
            return i, OFF_RING + slot * PIECE, (ring_sem[slot], 16 * (i // NSLOT + 1))

        def mms(lst, after=()):
            tok = None
            for k, (o, l, r, s, e) in enumerate(lst):
                tok = P(lambda eng, o=o, l=l, r=r, s=s, e=e: eng.matmul(o, l, r, start=s, stop=e),
                        *(after if k == 0 else ()), inc=(k == len(lst) - 1))
            return tok

        def tps(lst, after=()):
            tok = None
            for k, (o, i, idn) in enumerate(lst):
                tok = P(lambda eng, o=o, i=i, idn=idn: eng.transpose(o, i, idn),
                        *(after if k == 0 else ()), inc=(k == len(lst) - 1))
            return tok

        ident = sm("ident")
        xr = V(OFF_XR, 2, 1024)
        hT = V(OFF_HT, 8, 256)
        hn = V(OFF_HN, 2, 1024)

        def tt(o, a, b, op):
            return lambda e: e.tensor_tensor(o, a, b, op)

        def ts(o, a, s1, s2, op0, op1=None):
            if op1 is None:
                return lambda e: e.tensor_scalar(o, a, s1, None, op0)
            return lambda e: e.tensor_scalar(o, a, s1, s2, op0, op1)

        def stt(o, a, s, b, op0, op1):
            return lambda e: e.scalar_tensor_tensor(out=o, in0=a, scalar=s, in1=b, op0=op0, op1=op1)

        def act(o, a, f, **k):
            return lambda e: e.activation(o, a, f, **k)

        def cp(o, a):
            return lambda e: e.tensor_copy(o, a)

        def rstd(ss, n, dst, *after):
            D(ts(dst, ss, 1.0 / n, EPS, ALU.mult, ALU.add), *after)
            A(act(dst, dst, ACT.Sqrt), D.prev)
            return D(lambda e: e.reciprocal(dst, dst), A.prev)

        def norm_T(gain, ready, shift=None, extra=None):
            toks = []
            for t in range(2):
                so = stat(1)
                ss = ar[:, so:so + 1]
                A(act(hn[:, t, :], xr[:, t, :], ACT.Square, accum_out=ss), ready[t], extra)
                rstd(ss, 1024, ss, A.prev)
                hd = D(ts(hn[:, t, :], xr[:, t, :], ss, None, ALU.mult), D.prev, A.prev)
                for b in range(2):
                    bk = 6 + b
                    tp = tps([(bank(bk, 4, 128)[:, k, :], hn[:, t, (4 * b + k) * 128:(4 * b + k + 1) * 128], ident)
                              for k in range(4)], [hd, fr[bk]])
                    dst = hT[:, 4 * b:4 * b + 4, t * 128:(t + 1) * 128]
                    g = gain[:, 4 * b:4 * b + 4]
                    D(tt(dst, bank(bk, 4, 128), B(g.unsqueeze(2), [128, 4, 128]), ALU.mult), tp)
                    fr[bk] = [D.prev]
                    if shift is not None:
                        h = shift[:, 4 * b:4 * b + 4]
                        D(tt(dst, dst, B(h.unsqueeze(2), [128, 4, 128]), ALU.add), D.prev)
                toks.append(D.prev)
            return toks

        A.dma(lambda e: e.dma_start(V(OFF_SM, SMN), T["small"]), in_sem)
        A.dma(lambda e: e.dma_start(xr, T["x"].rearrange("(t p) d -> p t d", p=128)), in_sem)
        A.dma(lambda e: e.dma_start(V(OFF_GB, 2048), T["gb"]), in_sem)
        got_in = (in_sem, 48)

        for n, d in (("gqmla", 96), ("gqmoba", 64), ("qng", 64)):
            qg_r = D(ts(sm(n), sm(n), float(d) ** -0.5, None, ALU.mult), got_in)
        hT_r = norm_T(sm("mixg")[:, 0:8], [got_in, got_in])
        PROJ, QM, KV, KF, OO = 0, 3904, 5440, 7488, 9024
        QT1, KT1, QT2, KT2, SC = 11072, 13120, 15168, 17216, 19264
        proj = V(PROJ, 2, 1952)
        pj_tok = []
        nb = 0
        for j in range(8):
            n = 256 if j < 7 else 160
            i, so, landed = get(T["w_in"][j], 8 * n)
            w = V(so, 8, n)
            bk = j % 2
            tk = mms([(bank(bk, 2, 256)[:, t, 0:n], hT[:, k, t * 128:(t + 1) * 128], w[:, k, :], k == 0, k == 7)
                      for t in range(2) for k in range(8)], [landed, hT_r, fr[bk]])
            release[i] = tk
            A(act(proj[:, :, 256 * j:256 * j + n], bank(bk, 2, 256)[:, :, 0:n], ACT.Copy), tk)
            fr[bk] = [A.prev]
            pj_tok.append(A.prev)

        def head_rstd(src, n, d, scratch, ready, eng=None):
            so = stat(n)
            r = ar[:, so:so + n]
            D(tt(scratch, src, src, ALU.mult), ready)
            D(lambda e: e.tensor_reduce(r, scratch, AX.X, ALU.add), D.prev)
            return r, rstd(r, d, r, D.prev)

        ctok = None
        cT = V(SC, 3, 256)
        last = None
        for t in range(2):
            so = stat(2)
            s2 = ar[:, so:so + 2]
            A(act(V(SC + 768, 256), proj[:, t, 0:256], ACT.Square, accum_out=s2[:, 0:1]), pj_tok[1], A.prev)
            A(act(V(SC + 1024, 128), proj[:, t, 256:384], ACT.Square, accum_out=s2[:, 1:2]), A.prev)
            D(ts(s2[:, 0:1], s2[:, 0:1], 1.0 / 256, EPS, ALU.mult, ALU.add), A.prev)
            D(ts(s2[:, 1:2], s2[:, 1:2], 1.0 / 128, EPS, ALU.mult, ALU.add), A.prev)
            A(act(s2, s2, ACT.Sqrt), D.prev)
            D(lambda e, s2=s2: e.reciprocal(s2, s2), A.prev)
            D(ts(proj[:, t, 0:256], proj[:, t, 0:256], s2[:, 0:1], None, ALU.mult), D.prev)
            D(ts(proj[:, t, 256:384], proj[:, t, 256:384], s2[:, 1:2], None, ALU.mult), D.prev)
            tk = tps([(bank(2, 4, 128)[:, k, :], proj[:, t, k * 128:(k + 1) * 128], ident) for k in range(3)],
                     [D.prev, fr[2]])
            gc = ar[:, OFF_SM + SML["gcq"][0]:OFF_SM + SML["gcq"][0] + 3]
            D(tt(cT[:, :, t * 128:(t + 1) * 128], bank(2, 4, 128)[:, 0:3, :], B(gc.unsqueeze(2), [128, 3, 128]),
                 ALU.mult), tk)
            fr[2] = [D.prev]
        ctok = D.prev
        qm = V(QM, 2, 768)
        kv = V(KV, 2, 1024)
        i, so, landed = get(T["w_uq"], 1536)
        w = V(so, 2, 768)
        for t in range(2):
            for hf in range(2):
                bk = 3 + hf
                tk = mms([(bank(bk, 384), cT[:, k, t * 128:(t + 1) * 128], w[:, k, hf * 384:(hf + 1) * 384], k == 0, k == 1)
                          for k in range(2)], [landed, ctok, fr[bk]])
                A(act(qm[:, t, hf * 384:(hf + 1) * 384], bank(bk, 384), ACT.Copy), tk)
                fr[bk] = [A.prev]
        release[i] = tk
        q_r = A.prev
        i, so, landed = get(T["w_ukv"], 1024)
        w = V(so, 1024)
        for t in range(2):
            for hf in range(2):
                bk = 5 + hf
                tk = mms([(bank(bk, 512), cT[:, 2, t * 128:(t + 1) * 128], w[:, hf * 512:(hf + 1) * 512], True, True)],
                         [landed, fr[bk]])
                A(act(kv[:, t, hf * 512:(hf + 1) * 512], bank(bk, 512), ACT.Copy), tk)
                fr[bk] = [A.prev]
        release[i] = tk
        kv_r = A.prev

        cosv = sm("cos").rearrange("p (t a d) -> p t a d", t=2, a=1)
        sinv = sm("sin").rearrange("p (t a d) -> p t a d", t=2, a=1)
        rtmp = [V(SC + 2048 + 256 * m, 2, 8, 16) for m in range(4)]

        def rope(src, dst, nh, ready, war=None):
            c, s = B(cosv, [128, 2, nh, 16]), B(sinv, [128, 2, nh, 16])
            x1, x2 = src[:, :, :, 0:16], src[:, :, :, 16:32]
            m = [r[:, :, 0:nh, :] for r in rtmp]
            D(tt(m[0], x1, c, ALU.mult), ready, war)
            D(tt(m[1], x2, s, ALU.mult))
            D(tt(m[2], x1, s, ALU.mult))
            D(tt(m[3], x2, c, ALU.mult))
            D(tt(dst[:, :, :, 0:16], m[0], m[1], ALU.subtract), D.prev)
            return D(tt(dst[:, :, :, 16:32], m[2], m[3], ALU.add), D.prev)

        q4 = qm.rearrange("p t (h d) -> p t h d", h=8)
        rope(q4[:, :, :, 64:96], q4[:, :, :, 64:96], 8, q_r)
        kf4 = V(KF, 2, 8, 96)
        kr4 = proj[:, :, 384:416].rearrange("p t (a d) -> p t a d", a=1)
        rope(kr4, kr4, 1, [pj_tok[1], D.prev])
        kv4 = kv.rearrange("p t (h d) -> p t h d", h=8)
        for t in range(2):
            D(cp(kf4[:, t, :, 64:96], B(kr4[:, t, :, :], [128, 8, 32])), D.prev)
            D(cp(kf4[:, t, :, 0:64], kv4[:, t, :, 0:64]), kv_r)

        sq = V(SC + 3072, 1536)

        def scale_heads(src, n, d, ready):
            r, _ = head_rstd(src, n, d, sq[:, 0:n * d].rearrange("p (a b) -> p a b", a=n), ready)
            return D(tt(src, src, B(r.unsqueeze(2), [128, n, d]), ALU.mult), D.prev)

        def heads_T(src, nh, d, t, dst, gain, ready):
            for b in range((nh + 3) // 4):
                bk = 2 + (hrot[0] % 4)
                hrot[0] += 1
                m = min(4, nh - 4 * b)
                tk = tps([(ps[bk][0:d, k * 128:(k + 1) * 128], src[:, (4 * b + k) * d:(4 * b + k + 1) * d], ident)
                          for k in range(m)], [ready, fr[bk]])
                A(act(dst[0:d, 4 * b:4 * b + m, t * 128:(t + 1) * 128],
                      ps[bk][0:d, 0:m * 128].rearrange("p (a b) -> p a b", a=m), ACT.Copy, scale=gain), tk, qg_r)
                fr[bk] = [A.prev]
            return A.prev

        hrot = [0]
        qt1, kt1, qt2, kt2 = V(QT1, 8, 256), V(KT1, 8, 256), V(QT2, 8, 256), V(KT2, 8, 256)
        qtk = scale_heads(V(QM, 16, 96), 16, 96, D.prev)
        ktk = scale_heads(V(KF, 16, 96), 16, 96, D.prev)
        for t in range(2):
            heads_T(V(QM + 768 * t, 768), 8, 96, t, qt1, sm("gqmla", 96), qtk)
            r1 = heads_T(V(KF + 768 * t, 768), 8, 96, t, kt1, sm("gkmla", 96), ktk)
        for t in range(2):
            for which, dst, g in ((0, qt2, "gqmoba"), (1, kt2, "gkmoba")):
                src = proj[:, t, 416 + 512 * which:928 + 512 * which]
                tk = scale_heads(src.rearrange("p (a b) -> p a b", a=8), 8, 64, [pj_tok[7], D.prev])
                r2 = heads_T(src, 8, 64, t, dst, sm(g, 64), tk)

        def attention(units, ready):
            n = len(units)
            tok = [dict() for _ in units]
            st_off = [(OFF_HN + 512 * (u % 2), OFF_HN + 1024 + 512 * (u % 2)) for u in range(n)]
            dn = [stat(0) for _ in units]
            DN = V(ATT_ST, n, 2)
            NM = V(ATT_ST + 2 * n, n, 2)
            SE = V(ATT_ST + 4 * n, n, 2)
            for step in range(n + 3):
                u = step
                if u < n:
                    c = units[u]
                    K = c["K"]
                    bk = u % 2
                    tok[u]["s"] = mms([(bank(bk, 2, K)[:, h, :], c["q"][h], c["k"][h], True, True) for h in range(2)],
                                      [ready, fr[bk]])
                u = step - 2
                if 0 <= u < n:
                    c = units[u]
                    K = c["K"]
                    nk = K // 128
                    bk = 2 + u % 2
                    sv = V(st_off[u][0], 2, K)
                    tok[u]["t"] = tps([(bank(bk, 2 * nk, 128)[:, h * nk + kb, :], sv[:, h, kb * 128:(kb + 1) * 128], ident)
                                       for h in range(2) for kb in range(nk)], [tok[u]["e"], fr[bk]])
                u = step - 3
                if 0 <= u < n:
                    c = units[u]
                    nk = c["K"] // 128
                    bk = 4 + u % 2
                    pt = V(st_off[u][1], 2 * nk, 128)
                    tok[u]["o"] = mms([(bank(bk, 2, 64)[:, h, :], pt[:, h * nk + kb, :], c["v"][h][kb], kb == 0, kb == nk - 1)
                                       for h in range(2) for kb in range(nk)], [tok[u]["pt"], fr[bk]])
                u = step
                if u < n:
                    c = units[u]
                    K = c["K"]
                    bk = u % 2
                    sv = V(st_off[u][0], 2, K)
                    sp = bank(bk, 2, K)
                    war = [tok[u - 2]["t"]] if u >= 2 else []
                    if c["bias"] is not None:
                        D(tt(sv, sp, c["bias"], ALU.add), tok[u]["s"], war)
                    elif K == 128:
                        D(tt(sv, sp, B(sm("cmask").unsqueeze(1), [128, 2, 128]), ALU.add), tok[u]["s"], war)
                    else:
                        D(tt(sv[:, :, 128:256], sp[:, :, 128:256], B(sm("cmask").unsqueeze(1), [128, 2, 128]), ALU.add),
                          tok[u]["s"], war)
                        D(cp(sv[:, :, 0:128], sp[:, :, 0:128]))
                    fr[bk] = [D.prev]
                    nm = NM[:, u, :]
                    D(lambda e, nm=nm, sv=sv: e.tensor_reduce(nm, sv, AX.X, ALU.max, negate=True), D.prev)
                    if c["sink"] is not None:
                        se = SE[:, u, :]
                        D(stt(nm, c["sink"], -1.0, nm, ALU.mult, ALU.min), D.prev)
                        D(tt(se, c["sink"], nm, ALU.add), D.prev)
                    dt = D.prev
                    for h in range(2):
                        A(act(sv[:, h, :], sv[:, h, :], ACT.Exp, bias=nm[:, h:h + 1], accum_out=DN[:, u, h:h + 1]), dt)
                    if c["sink"] is not None:
                        A(act(se, se, ACT.Exp), dt)
                    tok[u]["e"] = A.prev
                u = step - 2
                if 0 <= u < n:
                    c = units[u]
                    nk = c["K"] // 128
                    bk = 2 + u % 2
                    pt = V(st_off[u][1], 2 * nk, 128)
                    war = [tok[u - 2]["o"]] if u >= 2 else []
                    A(act(pt, bank(bk, 2 * nk, 128), ACT.Copy), tok[u]["t"], war)
                    tok[u]["pt"] = A.prev
                    fr[bk] = [A.prev]
                    dn = DN[:, u, :]
                    if c["sink"] is not None:
                        D(tt(dn, dn, SE[:, u, :], ALU.add), tok[u]["e"])
                    D(lambda e, dn=dn: e.reciprocal(dn, dn), tok[u]["e"], D.prev)
                    tok[u]["r"] = D.prev
                u = step - 3
                if 0 <= u < n:
                    c = units[u]
                    bk = 4 + u % 2
                    D(tt(c["o"], bank(bk, 2, 64), B(DN[:, u, :].unsqueeze(2), [128, 2, 64]), ALU.mult),
                      tok[u]["o"], tok[u]["r"])
                    fr[bk] = [D.prev]
            return D.prev

        ATT_ST = SC
        oo = V(OO, 2, 1024)
        units = []
        for fam in range(2):
            qt, kt, d = ((qt1, kt1, 96), (qt2, kt2, 64))[fam]
            for hp in range(4):
                for t in range(2):
                    K = 128 * (t + 1)
                    hs = (2 * hp, 2 * hp + 1)
                    if fam == 0:
                        vv = [[kv4[:, kb, h, 64:128] for kb in range(2)] for h in hs]
                    else:
                        vv = [[proj[:, kb, 1440 + 64 * h:1504 + 64 * h] for kb in range(2)] for h in hs]
                    units.append(dict(K=K, q=[qt[0:d, h, t * 128:(t + 1) * 128] for h in hs],
                                      k=[kt[0:d, h, 0:K] for h in hs], v=vv, bias=None, sink=None,
                                      o=oo[:, t, 512 * fam + 128 * hp:512 * fam + 128 * (hp + 1)].rearrange(
                                          "p (a b) -> p a b", a=2)))
        att = attention(units, [r1, r2, kv_r, pj_tok[7], got_in])

        def to_T(src_of, dst, ready, gain=None, nchunk=8, c0=0):
            for t in range(2):
                for b in range(nchunk // 4):
                    bk = 6 + b % 2
                    tk = tps([(bank(bk, 4, 128)[:, k, :], src_of(t)[:, (4 * b + k) * 128:(4 * b + k + 1) * 128], ident)
                              for k in range(4)], [ready, fr[bk]])
                    d = dst[:, c0 + 4 * b:c0 + 4 * b + 4, t * 128:(t + 1) * 128]
                    if gain is None:
                        A(act(d, bank(bk, 4, 128), ACT.Copy), tk)
                        fr[bk] = [A.prev]
                    else:
                        D(tt(d, bank(bk, 4, 128), B(gain[:, 4 * b:4 * b + 4].unsqueeze(2), [128, 4, 128]), ALU.mult), tk)
                        fr[bk] = [D.prev]
            return A.prev if gain is None else D.prev

        def mix_out(wname, ready, gate=None):
            toks = None
            for j in range(4):
                i, so, landed = get(T[wname][j])
                w = V(so, 8, 256)
                bk = j % 2
                tk = mms([(bank(bk, 2, 256)[:, t, :], hT[:, k, t * 128:(t + 1) * 128], w[:, k, :], k == 0, k == 7)
                          for t in range(2) for k in range(8)], [landed, ready, fr[bk]])
                release[i] = tk
                xs = xr[:, :, 256 * j:256 * (j + 1)]
                if gate is None:
                    D(tt(xs, bank(bk, 2, 256), xs, ALU.add), tk)
                else:
                    tmp = V(OFF_HN + 512 * (j % 2), 2, 256)
                    D(tt(tmp, bank(bk, 2, 256), B(gate[:, 256 * j:256 * (j + 1)].unsqueeze(1), [128, 2, 256]), ALU.mult), tk)
                    fr[bk] = [D.prev]
                    D(tt(xs, tmp, xs, ALU.add), D.prev)
                fr[bk] = [D.prev]
            return [D.prev, D.prev]

        oT_r = to_T(lambda t: oo[:, t, :], hT, att)
        x_r = mix_out("w_o", oT_r)

        CO = stat(16)
        cond = ar[:, CO:CO + 8]
        ct2 = ar[:, CO + 8:CO + 16]
        MT = OFF_ST + NST - 32
        modT = V(MT, 4, 8)
        gb = V(OFF_GB, 2, 1024)

        def ada_setup():
            A(act(ct2, sm("c"), ACT.Exp, scale=-1.0), got_in)
            D(ts(ct2, ct2, 1.0, None, ALU.add), A.prev)
            D(lambda e: e.reciprocal(ct2, ct2), D.prev)
            D(tt(cond, ct2, sm("c"), ALU.mult), D.prev)

        ADA = [OFF_X + 15872, OFF_X + 16128]
        ada_mm = [None, None]
        ada_state = dict(pending=None)

        def ada_load(n):
            i, so, landed = get(T["w_ada"][n])
            w = V(so, 8, 256)
            acc = V(ADA[n % 2], 256)
            D(ts(acc, w[:, 0, :], cond[:, 0:1], None, ALU.mult), landed, ada_mm[n % 2], D.prev)
            for k in range(1, 8):
                D(stt(acc, w[:, k, :], cond[:, k:k + 1], acc, ALU.mult, ALU.add), D.prev)
            release[i] = D.prev
            ada_state["pending"] = (n, acc, D.prev)

        def ada_use():
            if ada_state["pending"] is None:
                return
            n, acc, tok = ada_state["pending"]
            ada_state["pending"] = None
            part, j = n // 4, n % 4
            if part in (2, 5):
                tk = mms([(bank(7, 256), sm("ones"), acc, True, True)], [tok, fr[7]])
                g = gb[:, 0 if part == 2 else 1, 256 * j:256 * (j + 1)]
                D(tt(g, bank(7, 256), g, ALU.add), tk, got_in)
            else:
                row = {0: 0, 1: 1, 3: 2, 4: 3}[part]
                tk = mms([(ps[7][:, m:m + 1], acc[:, 128 * m:128 * (m + 1)], sm("ones")[:, 0:1], True, True)
                          for m in range(2)], [tok, fr[7]])
                b0 = OFF_SM + SML["bada"][0] + 8 * row + 2 * j
                D(tt(modT[:, row, 2 * j:2 * j + 2], ps[7][:, 0:2], ar[:, b0:b0 + 2], ALU.add), tk)
            fr[7] = [D.prev]
            ada_mm[n % 2] = tk

        def ffn(layer, x_ready, war, ada=False):
            hr = norm_T(sm("ffng")[:, 8 * layer:8 * layer + 8], x_ready)
            aT = V(0, 32, 256)
            done = []
            n_ada = 0
            for j in range(16):
                i, so, landed = get(T["w_ff1"][layer, j])
                w = V(so, 8, 256)
                bk = j % 2
                tk = mms([(bank(bk, 2, 256)[:, m, :], w[:, k, 128 * m:128 * (m + 1)], hT[:, k, :], k == 0, k == 7)
                          for m in range(2) for k in range(8)], [landed, hr, fr[bk]])
                release[i] = tk
                d = aT[:, 2 * j:2 * j + 2, :]
                A(act(d, bank(bk, 2, 256), ACT.Relu), tk, war)
                fr[bk] = [A.prev]
                D(tt(d, d, d, ALU.mult), A.prev)
                done.append(D.prev)
                if ada:
                    ada_use()
                    if n_ada < 24:
                        ada_load(n_ada)
                        n_ada += 1
            for j in range(16):
                i, so, landed = get(T["w_ff2"][layer, j])
                w = V(so, 2, 1024)
                tk = mms([(bank(2 + 2 * t + hf, 512), aT[:, 2 * j + m, t * 128:(t + 1) * 128],
                           w[:, m, 512 * hf:512 * (hf + 1)], j == 0 and m == 0, j == 15 and m == 1)
                          for m in range(2) for t in range(2) for hf in range(2)],
                         [landed, done[j]] + ([fr[2], fr[3], fr[4], fr[5]] if j == 0 else []))
                release[i] = tk
                if ada:
                    ada_use()
                    if n_ada < 24:
                        ada_load(n_ada)
                        n_ada += 1
            toks = []
            for t in range(2):
                for hf in range(2):
                    b = 2 + 2 * t + hf
                    xs = xr[:, t, 512 * hf:512 * (hf + 1)]
                    D(tt(xs, bank(b, 512), xs, ALU.add), tk)
                    fr[b] = [D.prev]
                toks.append(D.prev)
            return toks, tk

        ada_setup()

        EO, BO, WO, CI = 16384, 8192, 10240, 13312
        Er, Ei = V(EO, 32, 256), V(EO + 8192, 32, 256)
        s5t = V(CI + 1024, 40, 32)
        row = lambda k: s5t[:, k, :]

        def s5_tables(war):
            L, LI, LT = sm("lre"), sm("lim"), sm("ldt")
            (dt, xx, nn, rr, pp, s2n, em, ex, th, kk, sn, cs, hs, cm1, are, aim, den, cr, ci, t1, t2, pr, pi) = [
                row(k) for k in range(23)]
            LOG2E = 1.0 / math.log(2.0)

            def expo(x, want_em):
                D(ts(x, x, -87.0, 88.0, ALU.max, ALU.min), D.prev, war)
                D(ts(nn, x, LOG2E, 12582912.0, ALU.mult, ALU.add), D.prev)
                D(ts(nn, nn, 12582912.0, None, ALU.subtract), D.prev)
                D(stt(rr, nn, -0.693359375, x, ALU.mult, ALU.add), D.prev)
                D(stt(rr, nn, 2.12194440e-4, rr, ALU.mult, ALU.add), D.prev)
                D(ts(pp, rr, 1.0 / 5040, 1.0 / 720, ALU.mult, ALU.add), D.prev)
                for c in (1.0 / 120, 1.0 / 24, 1.0 / 6, 0.5, 1.0):
                    D(tt(pp, pp, rr, ALU.mult), D.prev)
                    D(ts(pp, pp, c, None, ALU.add), D.prev)
                D(tt(pp, pp, rr, ALU.mult), D.prev)
                D(ts(nn, nn, 127.0, 8388608.0, ALU.add, ALU.mult), D.prev)
                D(cp(s2n.bitcast(I32), nn), D.prev)
                D(tt(pp, pp, s2n, ALU.mult), D.prev)
                D(tt(ex, pp, s2n, ALU.add), D.prev)
                if want_em:
                    D(ts(em, s2n, 1.0, None, ALU.subtract))
                    D(tt(em, em, pp, ALU.add), D.prev)

            D(cp(xx, LT), got_in, D.prev, war)
            expo(xx, False)
            D(cp(dt, ex), D.prev)
            D(tt(xx, L, dt, ALU.mult), D.prev)
            expo(xx, True)
            D(tt(th, LI, dt, ALU.mult), D.prev)
            D(ts(kk, th, 1.0 / (2 * math.pi), 12582912.0, ALU.mult, ALU.add), D.prev)
            D(ts(kk, kk, 12582912.0, None, ALU.subtract), D.prev)
            c1 = 6.28125
            c2 = float(np.float32(2 * math.pi - c1))
            c3 = 2 * math.pi - c1 - c2
            for c in (c1, c2, c3):
                D(stt(th, kk, -c, th, ALU.mult, ALU.add), D.prev)
            D(ts(th, th, -3.1415925, 3.1415925, ALU.max, ALU.min), D.prev)
            D(stt(t1, th, -1.0, th, ALU.mult, ALU.max), D.prev)
            D(ts(t1, t1, -1.0, math.pi / 2, ALU.mult, ALU.add), D.prev)
            D(ts(t2, th, 0.5, None, ALU.mult), D.prev)
            A(act(sn, th, ACT.Sin), D.prev)
            A(act(cs, t1, ACT.Sin))
            A(act(hs, t2, ACT.Sin))
            D(tt(cm1, hs, hs, ALU.mult), A.prev)
            D(ts(cm1, cm1, -2.0, None, ALU.mult), D.prev)
            D(tt(are, em, cs, ALU.mult), D.prev)
            D(tt(are, are, cm1, ALU.add), D.prev)
            D(tt(aim, ex, sn, ALU.mult))
            D(tt(den, L, L, ALU.mult))
            D(tt(t1, LI, LI, ALU.mult))
            D(tt(den, den, t1, ALU.add), D.prev)
            D(lambda e: e.reciprocal(den, den), D.prev)
            D(tt(cr, are, L, ALU.mult))
            D(tt(t1, aim, LI, ALU.mult), D.prev)
            D(tt(cr, cr, t1, ALU.add), D.prev)
            D(tt(cr, cr, den, ALU.mult), D.prev)
            D(tt(ci, aim, L, ALU.mult))
            D(tt(t2, are, LI, ALU.mult), D.prev)
            D(tt(ci, ci, t2, ALU.subtract), D.prev)
            base = D(tt(ci, ci, den, ALU.mult), D.prev)
            G(lambda e: e.memset(Er[:, :, 0:1], 1.0), war)
            G(lambda e: e.memset(Ei[:, :, 0:1], 0.0))
            G(cp(pr, cs), base)
            G(cp(pi, sn))
            n = 1
            qr, qi, q1 = row(23), row(24), row(25)
            while n < 256:
                a, b = B(pr.unsqueeze(2), [128, 32, n]), B(pi.unsqueeze(2), [128, 32, n])
                tm = TMPE(n)
                G(tt(tm, Ei[:, :, 0:n], b, ALU.mult), G.prev)
                G(tt(Er[:, :, n:2 * n], Er[:, :, 0:n], a, ALU.mult))
                G(tt(Er[:, :, n:2 * n], Er[:, :, n:2 * n], tm, ALU.subtract), G.prev)
                G(tt(tm, Er[:, :, 0:n], b, ALU.mult), G.prev)
                G(tt(Ei[:, :, n:2 * n], Ei[:, :, 0:n], a, ALU.mult))
                G(tt(Ei[:, :, n:2 * n], Ei[:, :, n:2 * n], tm, ALU.add), G.prev)
                G(tt(qr, pr, pr, ALU.mult))
                G(tt(q1, pi, pi, ALU.mult))
                G(tt(qi, pr, pi, ALU.mult))
                G(tt(pr, qr, q1, ALU.subtract), G.prev)
                G(tt(pi, qi, qi, ALU.add), G.prev)
                n *= 2
            return base, G.prev, ex, cr, ci

        def TMPE(n):
            return V(0, 32, n)

        BTr, BTi = V(BO, 8, 128), V(BO + 1024, 8, 128)
        W1, W1n, W2 = V(WO, 32, 32), V(WO + 1024, 32, 32), V(WO + 2048, 32, 32)

        x_r, ff_last = ffn(0, x_r, att, ada=True)

        base, e_ready, r_ap, cr_ap, ci_ap = s5_tables([ff_last, D.prev, x_r[1]])
        bl = V(4096, 2, 8, 64)
        cl = V(5120, 2, 32, 16)
        A.dma(lambda e: e.dma_start(V(4096, 1024), T["b5"]), key_sem, ff_last)
        A.dma(lambda e: e.dma_start(V(5120, 1024), T["c5"]), key_sem)
        bc_r = (key_sem, 32)
        hp = sm("hpar")
        for ri, dst in ((0, BTr), (1, BTi)):
            for h in range(2):
                D(ts(dst[:, :, 64 * h:64 * h + 64], bl[:, ri, :, :], hp[:, h:h + 1], None, ALU.mult), bc_r, ff_last)
        m1, m2 = V(6144, 32, 16), V(6656, 32, 16)
        c1, c2 = V(7168, 32, 16), V(7680, 32, 16)
        crb, cib = B(cr_ap.unsqueeze(2), [128, 32, 16]), B(ci_ap.unsqueeze(2), [128, 32, 16])
        D(tt(m1, cl[:, 0], crb, ALU.mult), bc_r, base)
        D(tt(m2, cl[:, 1], cib, ALU.mult))
        D(tt(c1, m1, m2, ALU.subtract), D.prev)
        D(tt(m1, cl[:, 0], cib, ALU.mult), D.prev)
        D(tt(m2, cl[:, 1], crb, ALU.mult), D.prev)
        D(tt(c2, m1, m2, ALU.add), D.prev)
        for h in range(2):
            D(ts(W1[:, :, 16 * h:16 * h + 16], c1, sm("bones")[:, 64 * h:64 * h + 1], 64.0, ALU.mult, ALU.mult), D.prev)
            D(ts(W1n[:, :, 16 * h:16 * h + 16], c1, sm("bones")[:, 64 * h:64 * h + 1], -64.0, ALU.mult, ALU.mult), D.prev)
            D(ts(W2[:, :, 16 * h:16 * h + 16], c2, sm("bones")[:, 64 * h:64 * h + 1], -64.0, ALU.mult, ALU.mult), D.prev)
        tab_r = D.prev

        hr = norm_T(sm("mixg")[:, 8:16], x_r)
        def sc5(q, k):
            return V(512 * 0 + (q % 2) * 2048 + 256 * k, 256)
        pe_c = {}
        gT = V(4096, 8, 256)
        ybank = [4, 5]
        bu = {}

        def s5_bu(q):
            c, j = q // 4, q % 4
            bk = q % 4
            rows = slice(32 * j, 32 * j + 32)
            bu[q] = mms([(bank(bk, 2, 256)[:, 0, :], BTr[rows, c, :], hT[rows, c, :], True, True),
                         (bank(bk, 2, 256)[:, 1, :], BTi[rows, c, :], hT[rows, c, :], True, True)],
                        [hr, tab_r, fr[bk]])

        g_tok = None
        for q in range(2):
            s5_bu(q)
        for q in range(32):
            if q + 2 < 32:
                s5_bu(q + 2)
            c, j = q // 4, q % 4
            bk = q % 4
            er, ei = Er[:, q, :], Ei[:, q, :]
            br, bi = bank(bk, 2, 256)[:, 0, :], bank(bk, 2, 256)[:, 1, :]
            a1, a2, a3, a4, v1, v2, h1, h2 = [sc5(q, k) for k in range(8)]
            war = pe_c.get(q - 2)
            D(tt(a1, br, er, ALU.mult), bu[q], e_ready, war)
            D(tt(a2, bi, ei, ALU.mult))
            D(tt(a3, bi, er, ALU.mult))
            D(tt(a4, br, ei, ALU.mult))
            fr[bk] = [D.prev]
            dm = D.prev
            G(tt(v1, a1, a2, ALU.add), dm, war)
            G(tt(v2, a3, a4, ALU.subtract))
            rb = B(r_ap[:, q:q + 1], [128, 256])
            D(lambda e, h1=h1, rb=rb, v1=v1: e.tensor_tensor_scan(h1, rb, v1, 0.0, ALU.mult, ALU.add), G.prev)
            D(lambda e, h2=h2, rb=rb, v2=v2: e.tensor_tensor_scan(h2, rb, v2, 0.0, ALU.mult, ALU.add))
            sc = D.prev
            D(tt(a1, h1, er, ALU.mult), sc, G.prev)
            D(tt(a4, h2, er, ALU.mult))
            dd = D.prev
            G(tt(a2, h2, ei, ALU.mult), sc)
            G(tt(a3, h1, ei, ALU.mult))
            yb = ybank[c % 2]
            yo = ps[yb][32 * j:32 * j + 32, 0:256]
            pe_c[q] = mms([(yo, W1[:, q, :], a1, True, False), (yo, W1n[:, q, :], a2, False, False),
                           (yo, W2[:, q, :], a3, False, False), (yo, W2[:, q, :], a4, False, True)],
                          [dd, G.prev, fr[yb] if j == 0 else None])
            if j == 3:
                ds = sm("dskip")[:, c:c + 1]
                D(stt(gT[:, c, :], hT[:, c, :], ds, ps[yb][:, 0:256], ALU.mult, ALU.add), pe_c[q])
                fr[yb] = [D.prev]
                A(act(gT[:, c, :], gT[:, c, :], ACT.Gelu_apprx_tanh), D.prev)
                g_tok = A.prev
        glu_free = {}
        for j in range(4):
            iv, sv, lv = get(T["w_glu"][j])
            ig, sg, lg = get(T["w_glu"][4 + j])
            for t in range(2):
                bk = 2 * (j % 2) + t
                lst = []
                for half, so in ((0, sv), (1, sg)):
                    w = V(so, 8, 256)
                    lst += [(bank(bk, 2, 256)[:, half, :], gT[:, k, t * 128:(t + 1) * 128], w[:, k, :], k == 0, k == 7)
                            for k in range(8)]
                tk = mms(lst, [lv, lg, g_tok, fr[bk]])
                sg_t = V(OFF_HN + 256 * (2 * (j % 2) + t), 256)
                A(act(sg_t, bank(bk, 2, 256)[:, 1, :], ACT.Sigmoid), tk, glu_free.get(bk))
                D(tt(sg_t, bank(bk, 2, 256)[:, 0, :], sg_t, ALU.mult), A.prev)
                fr[bk] = [D.prev]
                xs = xr[:, t, 256 * j:256 * (j + 1)]
                D(tt(xs, xs, sg_t, ALU.add), D.prev)
                glu_free[bk] = D.prev
            release[iv] = tk
            release[ig] = tk
        x_r, ff_last = ffn(1, [D.prev, D.prev], [tk, D.prev])

        gs = stat(8)
        gsc = ar[:, gs:gs + 8]
        D(stt(gsc, modT[:, 1, :], 1.0, sm("n1g"), ALU.add, ALU.mult), D.prev)
        hr = norm_T(gsc, x_r, shift=modT[:, 0, :], extra=D.prev)
        WB = 16384
        A.dma(lambda e: e.dma_start(V(WB, 2048), T["wbias"]), key_sem, ff_last, x_r)
        A.dma(lambda e: e.dma_start(V(WB + 2048, 256), T["wmask"]), key_sem)
        wb_in = (key_sem, 64)
        wb = V(WB, 8, 256)
        wb_r = D(tt(wb, wb, B(V(WB + 2048, 256).unsqueeze(1), [128, 8, 256]), ALU.add), wb_in)
        CV = 0
        cw = sm("convw").rearrange("p (j c) -> p j c", j=3)
        cps = []
        cvT = V(CV, 12, 256)
        for j in range(6):
            i, so, landed = get(T["w_in2"][j])
            w = V(so, 8, 256)
            bk = j % 2
            tk = mms([(bank(bk, 2, 256)[:, m, :], w[:, k, 128 * m:128 * (m + 1)], hT[:, k, :], k == 0, k == 7)
                      for m in range(2) for k in range(8)], [landed, hr, fr[bk]])
            release[i] = tk
            A(act(cvT[:, 2 * j:2 * j + 2, :], bank(bk, 2, 256), ACT.Copy), tk, ff_last, x_r)
            fr[bk] = [A.prev]
            cps.append(A.prev)
        pj2 = V(4096, 2, 768)
        pj2_t = []
        for j in range(3):
            i, so, landed = get(T["w_in2"][6 + j])
            w = V(so, 8, 256)
            bk = j % 2
            tk = mms([(bank(bk, 2, 256)[:, t, :], hT[:, k, t * 128:(t + 1) * 128], w[:, k, :], k == 0, k == 7)
                      for t in range(2) for k in range(8)], [landed, fr[bk]])
            release[i] = tk
            A(act(pj2[:, :, 256 * j:256 * (j + 1)], bank(bk, 2, 256), ACT.Copy), tk)
            fr[bk] = [A.prev]
            pj2_t.append(A.prev)
        hT_free = tk
        sq = V(12288, 1536)
        sq_ = sq
        KT3, QT3 = 6144, 7168
        qt3, kt3 = V(QT3, 8, 256), V(KT3, 2, 256)
        for t in range(2):
            src = pj2[:, t, 0:512]
            tk = scale_heads(src.rearrange("p (a b) -> p a b", a=8), 8, 64, [pj2_t[1], D.prev])
            heads_T(src, 8, 64, t, qt3, sm("qng", 64), tk)
            src = pj2[:, t, 512:640]
            tk = scale_heads(src.rearrange("p (a b) -> p a b", a=2), 2, 64, [pj2_t[2], D.prev])
            r3 = heads_T(src, 2, 64, t, kt3, sm("kng", 64), tk)
        OO2 = 9216
        oo2 = V(OO2, 2, 512)
        ATT_ST = 11264
        units = []
        for hp in range(4):
            for t in range(2):
                K = 128 * (t + 1)
                hs = (2 * hp, 2 * hp + 1)
                kh = hp // 2
                so = OFF_SM + SML["sinks"][0] + 2 * hp
                units.append(dict(K=K, q=[qt3[0:64, h, t * 128:(t + 1) * 128] for h in hs],
                                  k=[kt3[0:64, kh, 0:K]] * 2,
                                  v=[[pj2[:, kb, 640 + 64 * kh:704 + 64 * kh] for kb in range(2)]] * 2,
                                  bias=wb[:, 2 * hp:2 * hp + 2, 128 * (1 - t):256], sink=ar[:, so:so + 2],
                                  o=oo2[:, t, 128 * hp:128 * (hp + 1)].rearrange("p (a b) -> p a b", a=2)))
        att = attention(units, [r3, wb_r, hr])
        cv = lambda k: cvT[:, k, :]
        YC = 14336
        yT = V(YC, 4, 256)
        for c in range(4):
            cg, hh, bg = cv(3 * c), cv(3 * c + 1), cv(3 * c + 2)
            y = yT[:, c, :]
            D(tt(cg, cg, hh, ALU.mult), cps[5], D.prev)
            D(ts(y, cg, cw[:, 2, c:c + 1], None, ALU.mult), D.prev)
            D(stt(y[:, 1:256], cg[:, 0:255], cw[:, 1, c:c + 1], y[:, 1:256], ALU.mult, ALU.add), D.prev)
            D(stt(y[:, 2:256], cg[:, 0:254], cw[:, 0, c:c + 1], y[:, 2:256], ALU.mult, ALU.add), D.prev)
            D(tt(y, y, bg, ALU.mult), D.prev)
            D(tt(cg, y, y, ALU.mult), D.prev)
            bk = c % 2
            tk = mms([(bank(bk, 256), sm("bones"), cg, True, True)], [D.prev, fr[bk]])
            D(ts(hh, bank(bk, 256), 1.0, EPS, ALU.mult, ALU.add), tk)
            fr[bk] = [D.prev]
            A(act(hh, hh, ACT.Sqrt), D.prev)
            D(lambda e, hh=hh: e.reciprocal(hh, hh), A.prev)
            D(tt(y, y, hh, ALU.mult), D.prev)
            D(ts(hT[:, c, :], y, sm("convg")[:, c:c + 1], None, ALU.mult), D.prev, hT_free)
        tk = scale_heads(V(OO2, 16, 64), 16, 64, [att, D.prev])
        to_T(lambda t: oo2[:, t, :], hT, [tk, hT_free], gain=sm("attng"), nchunk=4, c0=4)
        x_r = mix_out("w_out", [D.prev], gate=gb[:, 0, :])

        gs = stat(8)
        gsc = ar[:, gs:gs + 8]
        D(stt(gsc, modT[:, 3, :], 1.0, sm("n2g"), ALU.add, ALU.mult), D.prev)
        hr = norm_T(gsc, x_r, shift=modT[:, 2, :], extra=D.prev)
        X = V(0, 128, 256)
        QP, SCO = 28672, 24576
        qp = V(QP, 16, 256)
        scs = V(SCO, 2, 16, 128)
        att_all = [D.prev, A.prev, P.prev]
        for j in range(8):
            i, so, landed = get(T["peer_wq"][j])
            w = V(so, 8, 256)
            bk = j % 2
            tk = mms([(bank(bk, 2, 256)[:, m, :], w[:, k, 128 * m:128 * (m + 1)], hT[:, k, :], k == 0, k == 7)
                      for m in range(2) for k in range(8)], [landed, hr, fr[bk]])
            release[i] = tk
            A(act(qp[:, 2 * j:2 * j + 2, :], bank(bk, 2, 256), ACT.Copy), tk, att_all)
            fr[bk] = [A.prev]
        qp_r = A.prev
        i, so, landed = get(T["keys"])
        kw = V(so, 16, 128)
        sc_t = []
        for t in range(2):
            for b in range(4):
                bk = 2 + (4 * t + b) % 4
                tk = mms([(bank(bk, 4, 128)[:, m, :], qp[:, 4 * b + m, t * 128:(t + 1) * 128], kw[:, 4 * b + m, :], True, True)
                          for m in range(4)], [landed, qp_r, fr[bk]])
                A(act(scs[:, t, 4 * b:4 * b + 4, :], bank(bk, 4, 128), ACT.Copy), tk)
                fr[bk] = [A.prev]
            sc_t.append(A.prev)
        release[i] = tk

        u_tok = {}
        u_scr = {}

        def u_piece(j, p_ready=None):
            i, so, landed = get(T["peer_u"][j])
            w = V(so, 2, 8, 128)
            bk = j % 2
            tk = mms([(bank(bk, 2, 256)[:, m, :], w[:, m, k, :], hT[:, k, :], k == 0, k == 7)
                      for m in range(2) for k in range(8)], [landed, hr, fr[bk]])
            release[i] = tk
            if p_ready is None:
                A(act(X[:, 2 * j:2 * j + 2, :], bank(bk, 2, 256), ACT.Gelu_apprx_tanh), tk, att_all)
                fr[bk] = [A.prev]
                u_tok[j] = A.prev
            else:
                s = V(OFF_HN + 512 * (j % 2), 2, 256)
                A(act(s, bank(bk, 2, 256), ACT.Gelu_apprx_tanh), tk, p_ready, u_scr.get(j - 2))
                fr[bk] = [A.prev]
                xs = X[:, 2 * j:2 * j + 2, :]
                D(tt(xs, xs, s, ALU.mult), A.prev)
                u_scr[j] = D.prev
                u_tok[j] = D.prev

        SEL = 16384
        TVa, TIa, TIf = V(SEL, 2, 16, 16), V(SEL + 512, 2, 16, 16), V(SEL + 1024, 2, 16, 16)
        CAND = V(SEL + 1536, 8, 16, 16)
        CAND2 = V(SEL + 1536, 8, 256)
        EQ = V(SEL + 3584, 128, 16)
        EQ4 = V(SEL + 3584, 8, 256).rearrange("p h (k i) -> p h k i", k=16)
        TV, TI = V(SEL + 5632, 8, 16), V(SEL + 5760, 8, 16)
        PI, PJ = V(SEL + 5888, 128), V(SEL + 6016, 128)
        PIf, PJf = V(SEL + 6144, 128), V(SEL + 6272, 128)
        RIA = [V(SEL + 6400 + 128 * m, 128) for m in range(3)]
        SUM = V(SEL + 6784, 8)
        TMP = [V(SEL + 6912 + 256 * m, 256) for m in range(2)]
        IT = [V(OFF_GB + 256 * m, 2, 128) for m in range(3)]

        def top16(src, tv, ti, tmp, *after):
            D(lambda e: e.max(tv[:, 0:8], src), *after)
            D(lambda e: e.max_index(ti[:, 0:8].bitcast(U32), tv[:, 0:8], src), D.prev)
            D(lambda e: e.match_replace(tmp, tv[:, 0:8], src, NEG * 10), D.prev)
            D(lambda e: e.max(tv[:, 8:16], tmp), D.prev)
            D(lambda e: e.max_index(ti[:, 8:16].bitcast(U32), tv[:, 8:16], tmp), D.prev)

        for t in range(2):
            for m in range(16):
                top16(scs[:, t, m, :], TVa[:, t, m, :], TIa[:, t, m, :], TMP[m % 2][:, 0:128], sc_t[t], D.prev, att_all)
            D(cp(TIf[:, t], TIa[:, t].bitcast(U32)), D.prev)
            va = TVa[:, t].rearrange("p (h a) k -> p h a k", a=2)
            D(lambda e, va=va: e.tensor_tensor(
                CAND, B(va[:, :, 0, :].unsqueeze(3), [128, 8, 16, 16]), B(va[:, :, 1, :].unsqueeze(2), [128, 8, 16, 16]),
                ALU.add), D.prev)
            for h in range(8):
                top16(CAND2[:, h, :], TV[:, h, :], TI[:, h, :], TMP[h % 2], D.prev)
            tiu = V(SEL + 5760, 128).bitcast(U32)
            D(lambda e: e.tensor_scalar(PI.bitcast(U32), tiu, 4, None, ALU.logical_shift_right), D.prev)
            D(lambda e: e.tensor_scalar(PJ.bitcast(U32), tiu, 15, None, ALU.bitwise_and))
            D(cp(PIf, PI.bitcast(U32)), D.prev)
            D(cp(PJf, PJ.bitcast(U32)), D.prev)
            fi = TIf[:, t].rearrange("p (h a) k -> p h a k", a=2)
            for which, pf in ((0, PIf), (1, PJf)):
                D(tt(EQ, B(pf.unsqueeze(2), [128, 128, 16]), B(sm("iota16").unsqueeze(1), [128, 128, 16]), ALU.is_equal),
                  D.prev)
                D(tt(EQ4, EQ4, B(fi[:, :, which, :].unsqueeze(2), [128, 8, 16, 16]), ALU.mult), D.prev)
                D(lambda e, which=which: e.tensor_reduce(RIA[which], EQ, AX.X, ALU.add), D.prev)
            R3 = RIA[2].rearrange("p (h k) -> p h k", h=8)
            D(tt(R3, TV, B(TV[:, :, 0:1], [128, 8, 16]), ALU.subtract), D.prev)
            sub = D.prev
            for j in range(*((0, 12), (12, 26))[t]):
                u_piece(j)
            A(act(R3, R3, ACT.Exp), sub)
            D(lambda e, R3=R3: e.tensor_reduce(SUM, R3, AX.X, ALU.add), A.prev)
            D(lambda e: e.reciprocal(SUM, SUM), D.prev)
            D(tt(R3, R3, B(SUM.unsqueeze(2), [128, 8, 16]), ALU.mult), D.prev)
            sel_done = D.prev
            tk = tps([(bank(6, 4, 128)[:, m, :], RIA[m], ident) for m in range(3)], [sel_done, fr[6]])
            itv = V(OFF_GB, 3, 256)[:, :, t * 128:(t + 1) * 128]
            D(cp(itv, bank(6, 4, 128)[:, 0:3, :]), tk, att_all)
            fr[6] = [D.prev]
        it_r = D.prev
        for j in range(26, NGA // 2):
            u_piece(j)
        iaT, ibT, gT_ = V(OFF_GB, 256), V(OFF_GB + 256, 256), V(OFF_GB + 512, 256)
        iota = sm("iota")
        oh_free = {}
        u_all = [u_tok[j] for j in range(NGA // 2)]
        for s in range(64):
            oa = V(OFF_HN + 1024 * (s % 2), 4, 128)
            ob = V(OFF_HN + 1024 * (s % 2) + 512, 4, 128)
            for k in range(4):
                tkn = 4 * s + k
                G(ts(oa[:, k, :], iota, iaT[:, tkn:tkn + 1], None, ALU.is_equal), it_r, oh_free.get(s - 2), hr)
                D(ts(ob[:, k, :], iota, ibT[:, tkn:tkn + 1], gT_[:, tkn:tkn + 1], ALU.is_equal, ALU.mult),
                  it_r, oh_free.get(s - 2), hr)
            bk = 2 + s % 4
            tk = mms([(bank(bk, 4, 128)[:, k, :], oa[:, k, :], ob[:, k, :], True, True) for k in range(4)],
                     [G.prev, D.prev, fr[bk]])
            oh_free[s] = tk
            gv = bank(bk, 4, 128).rearrange("p t b -> p b t")
            xs = X[:, 0:NGA, 4 * s:4 * s + 4]
            D(tt(xs, gv[:, 0:NGA, :], xs, ALU.mult), tk, u_all)
            A(act(X[:, NGA:128, 4 * s:4 * s + 4], gv[:, NGA:128, :], ACT.Copy), D.prev, sel_done)
            fr[bk] = [A.prev]
        spread = [D.prev, A.prev]
        for j in range(NGA // 2, 64):
            u_piece(j, spread)
        for j in range(64):
            i, so, landed = get(T["peer_v"][j])
            w = V(so, 2, 1024)
            tk = mms([(bank(2 + 2 * t + hf, 512), X[:, 2 * j + m, t * 128:(t + 1) * 128],
                       w[:, m, 512 * hf:512 * (hf + 1)], j == 0 and m == 0, j == 63 and m == 1)
                      for m in range(2) for t in range(2) for hf in range(2)],
                     [landed, u_tok[j] if j >= NGA // 2 else spread] + ([fr[2], fr[3], fr[4], fr[5]] if j == 0 else []))
            release[i] = tk
        outd = out.rearrange("a (t p) d -> p (a t) d", p=128)
        for t in range(2):
            for hf in range(2):
                b = 2 + 2 * t + hf
                xs = xr[:, t, 512 * hf:512 * (hf + 1)]
                tmp = V(OFF_HN + 512 * (2 * t + hf), 512)
                D(tt(tmp, bank(b, 512), gb[:, 1, 512 * hf:512 * (hf + 1)], ALU.mult), tk, u_all, u_tok[63])
                D(tt(xs, tmp, xs, ALU.add), D.prev)
            A.dma(lambda e, t=t: e.dma_start(outd[:, t, :], xr[:, t, :]), out_sem, D.prev)
        A.wait((out_sem, 32))

        ring_line = Line(nc.sync, None)
        for i, (ap, words) in enumerate(items):
            slot = i % NSLOT
            after = [release[i - NSLOT]] if i >= NSLOT else []
            ring_line.dma(lambda e, ap=ap, words=words, slot=slot: e.dma_start(V(OFF_RING + slot * PIECE, words), ap),
                          ring_sem[slot], *after)

        block = ctx.enter_context(nc.Block())

        @block.sync
        def _(e):
            ring_line.run()

        @block.scalar
        def _(e):
            A.run()

        @block.gpsimd
        def _(e):
            G.run()

        @block.vector
        def _(e):
            D.run()

        @block.tensor
        def _(e):
            P.run()



def _cols(v, n):
    return np.ascontiguousarray(v.reshape(n, 128).T)


def _rows(v):
    o = np.zeros((128, 1), np.float32)
    o[:len(v), 0] = v
    return o


def _pieces(w, order=None):
    n = w.shape[1] // 256
    return np.ascontiguousarray(w.reshape(8, 128, n, 256).transpose(2, 1, 0, 3)).reshape(n, 128, 2048)


def _bucket(dist):
    d = np.maximum(dist, 1).astype(np.float32)
    large = 16 + (np.log(d / np.float32(16)) / np.float32(math.log(8.0)) * np.float32(16)).astype(np.int32)
    return np.where(dist < 16, dist, np.minimum(large, 31))


def _arrays(a):
    f = np.float32
    p = np.arange(128)
    sml = {}
    sml["ident"] = np.eye(128, dtype=f)
    sml["cmask"] = np.where(p[None, :] <= p[:, None], 0.0, NEG).astype(f)
    sml["iota"] = np.broadcast_to(p.astype(f), (128, 128))
    sml["bones"] = np.where(p[None, :] // 64 == p[:, None] // 64, 1.0 / 64, 0.0).astype(f)
    sml["ones"] = np.ones((128, 128), f)
    inv = f(10000.0) ** (-np.arange(16, dtype=f) / f(16))
    ang = np.arange(256, dtype=f)[:, None] * inv[None, :]
    for n, fn in (("cos", np.cos), ("sin", np.sin)):
        sml[n] = fn(ang).astype(f).reshape(2, 128, 16).transpose(1, 0, 2).reshape(128, 32)
    h = (p // 16) % 2
    sml["hpar"] = np.stack([h == 0, h == 1], 1).astype(f)
    sml["iota16"] = np.broadcast_to(np.arange(16, dtype=f), (128, 16))
    sml["mixg"] = np.concatenate([_cols(a["mix_norm_g"][l], 8) for l in range(2)], 1)
    sml["ffng"] = np.concatenate([_cols(a["ffn_norm_g"][l], 8) for l in range(2)], 1)
    sml["n1g"] = _cols(a["norm1_g_2"][0], 8)
    sml["n2g"] = _cols(a["norm2_g_2"][0], 8)
    sml["gcq"] = _cols(a["g_cq"][0], 2)
    sml["gckv"] = _cols(a["g_ckv"][0], 1)
    for n, k in (("gqmla", "g_qn_mla"), ("gkmla", "g_kn_mla"), ("gqmoba", "g_qn_moba"), ("gkmoba", "g_kn_moba"),
                 ("qng", "q_norm_g_2"), ("kng", "k_norm_g_2")):
        sml[n] = _rows(a[k][0])
    sml["c"] = _cols(a["c_2"][0], 8)
    ba = a["b_ada_2"][0].reshape(6, 1024)
    sml["bada"] = np.concatenate([_cols(ba[r], 8) for r in (0, 1, 3, 4)], 1)
    sml["convw"] = np.concatenate([_cols(a["conv_w_2"][0][j], 4) for j in range(3)], 1)
    sml["convg"] = _cols(a["conv_out_g_2"][0], 4)
    sml["attng"] = _cols(a["attn_out_g_2"][0], 4)
    sml["dskip"] = _cols(a["d_skip"][0], 8)
    sml["sinks"] = np.broadcast_to(a["sinks_2"][0], (128, 8))
    st = lambda v: v.reshape(32, 128).T
    sml["lre"] = st(a["lam_re"][0])
    sml["lim"] = st(a["lam_im"][0])
    sml["ldt"] = st(np.repeat(a["log_dt"][0][:, None], 64, 1))
    small = np.concatenate([np.broadcast_to(sml[n], (128, w)).astype(f) for n, (_, w) in SML.items()], 1)
    r = {"small": small, "x": a["x"][0]}
    r["gb"] = np.broadcast_to(np.concatenate([ba[2], ba[5]]), (128, 2048))
    w = a["w_in"][0]
    r["w_in"] = _pieces(w[:, :1792])
    r["w_in_last"] = w[:, 1792:].reshape(8, 128, 160).transpose(1, 0, 2).reshape(128, 1280)
    r["w_uq"] = a["w_uq"][0].reshape(2, 128, 768).transpose(1, 0, 2).reshape(128, 1536)
    r["w_ukv"] = a["w_ukv"][0]
    r["w_o"] = _pieces(a["w_o"][0])
    r["w_ff1"] = np.stack([_pieces(a["w_ff1"][l]) for l in range(2)])
    r["w_ff2"] = a["w_ff2"].reshape(2, 16, 2, 128, 1024).transpose(0, 1, 3, 2, 4).reshape(2, 16, 128, 2048)
    r["w_ada"] = _pieces(a["w_ada_2"][0])
    r["w_glu"] = _pieces(a["w_glu"][0])
    b = np.stack([a["b_re"][0], a["b_im"][0]])
    r["b5"] = b.reshape(2, 8, 4, 2, 64, 16).transpose(2, 3, 5, 0, 1, 4).reshape(128, 1024)
    c = np.stack([a["c_re"][0], a["c_im"][0]])
    r["c5"] = c.reshape(2, 32, 2, 16, 64).transpose(2, 4, 0, 1, 3).reshape(128, 1024)
    w = a["w_in_2"][0]
    order = [w[:, off + 128 * k:off + 128 * k + 128] for k in range(4) for off in (512, 1024, 0)]
    r["w_in2"] = _pieces(np.concatenate(order + [w[:, 1536:]], 1))
    r["w_out"] = _pieces(a["w_out_2"][0])
    dist = p[:, None] + 128 - np.arange(256)[None, :]
    r["wbias"] = a["rel_bias_2"][_bucket(np.maximum(dist, 0))].transpose(0, 2, 1).reshape(128, 2048)
    r["wmask"] = np.where((dist >= 0) & (dist < 128), 0.0, NEG).astype(f)
    r["peer_wq"] = _pieces(a["peer_wq_2"][0])
    r["keys"] = a["peer_keys_2"][0].transpose(3, 1, 0, 2).reshape(128, 2048)
    u = a["peer_u_2"][0].reshape(128, 64, 2, 8, 128)
    r["peer_u"] = np.ascontiguousarray(u.transpose(1, 4, 2, 3, 0)).reshape(64, 128, 2048)
    v = a["peer_v_2"][0].reshape(128, 64, 2048)
    r["peer_v"] = v.transpose(1, 0, 2)
    return {k: np.ascontiguousarray(v) for k, v in r.items()}


def kernel(**inputs):
    import concourse.bacc as _bacc
    from concourse import mybir as _mybir
    from concourse.bass_utils import run_bass_kernel_spmd as _run

    nc = _bacc.Bacc("TRN2", target_bir_lowering=False, num_devices=1)
    arrays = _arrays({k: np.asarray(v) for k, v in inputs.items()})
    T = {}
    feed = {}
    for name, v in arrays.items():
        feed[f"in_{name}"] = v
        T[name] = nc.dram_tensor(f"in_{name}", v.shape, _mybir.dt.from_np(v.dtype), kind="ExternalInput").ap()
    T["w_in"] = [T["w_in"][j] for j in range(7)] + [T["w_in_last"]]
    out = nc.dram_tensor("out_0", (1, 256, 1024), F32, kind="ExternalOutput").ap()
    build(nc, T, out)
    r = _run(nc, [feed], core_ids=[0])
    return r.results[0]["out_0"]
```

```python
import math
from contextlib import ExitStack

import concourse.bass as bass
from concourse import mybir
import numpy as np

ALU = mybir.AluOpType
ACT = mybir.ActivationFunctionType
AX = mybir.AxisListType
F32 = mybir.dt.float32
F32R = mybir.dt.float32r
U32 = mybir.dt.uint32
I32 = mybir.dt.int32

NEG = -1.0e30
EPS = 1e-6
UNIT = 1024
NRAW = 4
NHL = 2
NGA = 96

OFF_X = 0
OFF_RING = 32768
OFF_XR = OFF_RING + NRAW * UNIT
OFF_GB = OFF_XR + 2048
OFF_HN = OFF_GB + 2048
OFF_SM = OFF_HN + 2048


def small_layout():
    cols = [("ident", 128), ("cmask", 128), ("iota", 128), ("bones", 128), ("ones", 128),
            ("cos", 32), ("sin", 32), ("hpar", 2), ("iota16", 16),
            ("mixg", 16), ("ffng", 16), ("n1g", 8), ("n2g", 8), ("gcq", 2), ("gckv", 1),
            ("gqmla", 1), ("gkmla", 1), ("gqmoba", 1), ("gkmoba", 1), ("qng", 1), ("kng", 1),
            ("c", 8), ("bada", 32), ("convw", 12), ("convg", 4), ("attng", 4), ("dskip", 8),
            ("sinks", 8), ("lre", 32), ("lim", 32), ("ldt", 32)]
    at, out = 0, {}
    for name, n in cols:
        out[name] = (at, n)
        at += n
    return out, at


SML, SMN = small_layout()
OFF_ST = OFF_SM + SMN
NST = 420
WORDS = OFF_ST + NST


class Line:

    def __init__(self, eng, sem):
        self.eng, self.sem, self.n, self.todo, self.seen = eng, sem, 0, [], {}
        self.prev = None

    def wait(self, *after):
        for tok in after:
            if tok is None:
                continue
            if isinstance(tok, list):
                self.wait(*tok)
                continue
            sem, val = tok
            if self.seen.get(id(sem), 0) < val:
                self.seen[id(sem)] = val
                self.todo.append(lambda s=sem, v=val: self.eng.wait_ge(s, v))

    def __call__(self, fn, *after, inc=True):
        self.wait(*after)
        if inc:
            self.n += 1
            self.todo.append(lambda: fn(self.eng).then_inc(self.sem, 1))
            self.prev = (self.sem, self.n)
            return self.prev
        self.todo.append(lambda: fn(self.eng))
        return None

    def dma(self, fn, sem, *after):
        self.wait(*after)
        self.todo.append(lambda: fn(self.eng).then_inc(sem, 16))

    def run(self):
        for t in self.todo:
            t()


def build(nc, T, out):
    ctx = ExitStack()
    with ctx:
        ar = ctx.enter_context(nc.sbuf_tensor("arena", [128, WORDS], F32))
        hth = ctx.enter_context(nc.sbuf_tensor("act_hi", [128, 2048], F32R))
        htl = ctx.enter_context(nc.sbuf_tensor("act_lo", [128, 2048], F32R))
        wh = ctx.enter_context(nc.sbuf_tensor("w_hi", [128, NHL * UNIT], F32R))
        wl = ctx.enter_context(nc.sbuf_tensor("w_lo", [128, NHL * UNIT], F32R))
        ps = [ctx.enter_context(nc.psum_tensor(f"ps{i}", [128, 512], F32)) for i in range(8)]
        sem = lambda n: ctx.enter_context(nc.semaphore(n))
        P = Line(nc.tensor, sem("pe_done"))
        D = Line(nc.vector, sem("dve_done"))
        A = Line(nc.scalar, sem("act_done"))
        G = Line(nc.gpsimd, sem("pool_done"))
        ring_sem = [sem(f"ring{i}") for i in range(NRAW)]
        in_sem = sem("inputs")
        out_sem = sem("outputs")
        key_sem = sem("bias_in")

        def V(off, *dims, p0=0, p1=128):
            n = 1
            for d in dims:
                n *= d
            ap = ar[p0:p1, off:off + n]
            if len(dims) == 2:
                ap = ap.rearrange("p (a b) -> p a b", a=dims[0])
            elif len(dims) == 3:
                ap = ap.rearrange("p (a b c) -> p a b c", a=dims[0], b=dims[1])
            return ap

        def sm(name, p1=128):
            o, n = SML[name]
            return ar[0:p1, OFF_SM + o:OFF_SM + o + n]

        def B(ap, shape):
            return ap.to_broadcast(list(shape))

        def bank(i, *dims, off=0):
            n = 1
            for d in dims:
                n *= d
            ap = ps[i][:, off:off + n]
            if len(dims) == 2:
                ap = ap.rearrange("p (a b) -> p a b", a=dims[0])
            elif len(dims) == 3:
                ap = ap.rearrange("p (a b c) -> p a b c", a=dims[0], b=dims[1])
            return ap

        fr = [[] for _ in range(8)]

        st_at = [0]

        def stat(n):
            assert st_at[0] + n <= NST - 32
            o = OFF_ST + st_at[0]
            st_at[0] += n
            return o

        plan = []
        for j, n in enumerate((512, 512, 512, 416)):
            plan += [("w_in", T[f"w_in{j}"][u], 2 * n, True) for u in range(4)]
        plan += [("w_uq", T["w_uq"][u], 768, True) for u in range(2)]
        plan += [("w_ukv", T["w_ukv"], 1024, True)]
        plan += [("w_o", T["w_o"][u], UNIT, True) for u in range(8)]
        for layer in range(2):
            ff = [("w_ff1", T["w_ff1"][layer, u], UNIT, True) for u in range(32)]
            ff += [("w_ff2", T["w_ff2"][layer, u], UNIT, True) for u in range(32)]
            for u, item in enumerate(ff):
                plan.append(item)
                if layer == 0 and u < 48:
                    plan.append(("w_ada", T["w_ada"][u], UNIT, False))
            if layer == 0:
                plan += [("w_glu", T["w_glu"][u], UNIT, True) for u in range(16)]
        plan += [("w_conv", T["w_conv"][u], UNIT, True) for u in range(12)]
        plan += [("w_qkv", T["w_qkv0"][u], UNIT, True) for u in range(4)]
        plan += [("w_qkv", T["w_qkv1"][u], 512, True) for u in range(4)]
        plan += [("w_out", T["w_out"][u], UNIT, True) for u in range(8)]
        plan += [("peer_wq", T["peer_wq"][u], UNIT, True) for u in range(16)]
        plan += [("keys", T["keys"][u], UNIT, False) for u in range(2)]
        plan += [("peer_u", T["peer_u"][u], UNIT, True) for u in range(128)]
        plan += [("peer_v", T["peer_v"][u], UNIT, True) for u in range(128)]
        raw_free = {}
        hl_order = [i for i, x in enumerate(plan) if x[3]]
        hl_no = {i: n for n, i in enumerate(hl_order)}
        hl_ready, hl_free = {}, {}
        at = dict(plan=0, cut=0)

        def raw(i):
            o = OFF_RING + (i % NRAW) * UNIT
            return ar[:, o:o + plan[i][2]], (ring_sem[i % NRAW], 16 * (i // NRAW + 1))

        def cut_weights(n):
            i = hl_order[n]
            src, landed = raw(i)
            o = (n % NHL) * UNIT
            w = plan[i][2]
            free = hl_free.get(n - NHL)
            hi, lo = wh[:, o:o + w], wl[:, o:o + w]
            A(act(hi, src, ACT.Copy), landed, free)
            D(tt(lo, src, hi.bitcast(F32), ALU.subtract), A.prev, free)
            raw_free[i] = [D.prev]
            hl_ready[n] = [A.prev, D.prev]

        def take(name):
            i = at["plan"]
            at["plan"] += 1
            assert plan[i][0] == name and plan[i][3], (name, plan[i][0])
            n = hl_no[i]
            while at["cut"] <= min(n + 1, len(hl_order) - 1):
                cut_weights(at["cut"])
                at["cut"] += 1
            o = (n % NHL) * UNIT
            w = plan[i][2]
            return wh[:, o:o + w], wl[:, o:o + w], hl_ready[n], n

        def take_raw(name):
            i = at["plan"]
            at["plan"] += 1
            assert plan[i][0] == name and not plan[i][3], (name, plan[i][0])
            src, landed = raw(i)
            return src, landed, i

        def mms(lst, after=()):
            tok = None
            for k, (o, l, r, s, e) in enumerate(lst):
                tok = P(lambda eng, o=o, l=l, r=r, s=s, e=e: eng.matmul(o, l, r, start=s, stop=e),
                        *(after if k == 0 else ()), inc=(k == len(lst) - 1))
            return tok

        def p3(o, l, r, s, e):
            return [(o, l[0], r[0], s, False), (o, l[0], r[1], False, False), (o, l[1], r[0], False, e)]

        def tps(lst, after=()):
            tok = None
            for k, (o, i, idn) in enumerate(lst):
                tok = P(lambda eng, o=o, i=i, idn=idn: eng.transpose(o, i, idn),
                        *(after if k == 0 else ()), inc=(k == len(lst) - 1))
            return tok

        ident = sm("ident")
        xr = V(OFF_XR, 2, 1024)
        HH = hth[:, :].rearrange("p (a b) -> p a b", a=8)
        HL = htl[:, :].rearrange("p (a b) -> p a b", a=8)
        HQ = [(hth[:, 512 * q:512 * (q + 1)], htl[:, 512 * q:512 * (q + 1)]) for q in range(4)]

        def cut_act(hi, lo, src, *after):
            A(act(hi, src, ACT.Copy), *after)
            D(tt(lo, src, hi.bitcast(F32), ALU.subtract), A.prev, *after)
            return [A.prev, D.prev]

        hn = V(OFF_HN, 2, 1024)

        def tt(o, a, b, op):
            return lambda e: e.tensor_tensor(o, a, b, op)

        def ts(o, a, s1, s2, op0, op1=None):
            if op1 is None:
                return lambda e: e.tensor_scalar(o, a, s1, None, op0)
            return lambda e: e.tensor_scalar(o, a, s1, s2, op0, op1)

        def stt(o, a, s, b, op0, op1):
            return lambda e: e.scalar_tensor_tensor(out=o, in0=a, scalar=s, in1=b, op0=op0, op1=op1)

        def act(o, a, f, **k):
            return lambda e: e.activation(o, a, f, **k)

        def cp(o, a):
            return lambda e: e.tensor_copy(o, a)

        def rstd(ss, n, dst, *after):
            D(ts(dst, ss, 1.0 / n, EPS, ALU.mult, ALU.add), *after)
            A(act(dst, dst, ACT.Sqrt), D.prev)
            return D(lambda e: e.reciprocal(dst, dst), A.prev)

        def norm_T(gain, ready, at_raw, shift=None, extra=None, cut=True):
            hT = V(at_raw, 8, 256)
            free = P.prev
            toks = []
            for t in range(2):
                so = stat(1)
                ss = ar[:, so:so + 1]
                A(act(hn[:, t, :], xr[:, t, :], ACT.Square, accum_out=ss), ready[t], extra)
                rstd(ss, 1024, ss, A.prev)
                hd = D(ts(hn[:, t, :], xr[:, t, :], ss, None, ALU.mult), D.prev, A.prev)
                for b in range(2):
                    bk = 6 + b
                    tp = tps([(bank(bk, 4, 128)[:, k, :], hn[:, t, (4 * b + k) * 128:(4 * b + k + 1) * 128], ident)
                              for k in range(4)], [hd, fr[bk]])
                    sl = (slice(None), slice(4 * b, 4 * b + 4), slice(t * 128, (t + 1) * 128))
                    dst = hT[sl]
                    g = gain[:, 4 * b:4 * b + 4]
                    D(tt(dst, bank(bk, 4, 128), B(g.unsqueeze(2), [128, 4, 128]), ALU.mult), tp, free)
                    fr[bk] = [D.prev]
                    if shift is not None:
                        h = shift[:, 4 * b:4 * b + 4]
                        D(tt(dst, dst, B(h.unsqueeze(2), [128, 4, 128]), ALU.add), D.prev)
                    if cut:
                        toks += cut_act(HH[sl], HL[sl], dst, D.prev, free)
                    else:
                        toks.append(D.prev)
            return toks

        def lin_tok(name, n, lhs, ready, done, b0=0, units=4):
            bks = (b0, b0 + 1)
            for u in range(units):
                h, l, ok, no = take(name)
                h, l = [x.rearrange("p (k n) -> p k n", k=2) for x in (h, l)]
                lst = []
                for kk in range(2):
                    k = 2 * u + kk
                    for t in range(2):
                        lst += p3(bank(bks[t], n), [x[:, k, t * 128:(t + 1) * 128] for x in lhs],
                                  (h[:, kk, :], l[:, kk, :]), k == 0, k == 2 * units - 1)
                tk = mms(lst, [ok, ready] + ([fr[bks[0]], fr[bks[1]]] if u == 0 else []))
                hl_free[no] = tk
            for t in range(2):
                done(t, bks[t], tk)
            return tk

        def lin_T(name, bk, half, ready, free=()):
            h, l, ok, no = take(name)
            h, l = [x.rearrange("p (k n) -> p k n", k=8) for x in (h, l)]
            lst = []
            for k in range(8):
                lst += p3(bank(bk, 2, 256)[:, half, :], (h[:, k, :], l[:, k, :]), (HH[:, k, :], HL[:, k, :]), k == 0, k == 7)
            hl_free[no] = mms(lst, [ok, ready] + list(free))
            return hl_free[no]

        A.dma(lambda e: e.dma_start(V(OFF_SM, SMN), T["small"]), in_sem)
        A.dma(lambda e: e.dma_start(xr, T["x"].rearrange("(t p) d -> p t d", p=128)), in_sem)
        A.dma(lambda e: e.dma_start(V(OFF_GB, 2048), T["gb"]), in_sem)
        got_in = (in_sem, 48)

        for n, d in (("gqmla", 96), ("gqmoba", 64), ("qng", 64)):
            qg_r = D(ts(sm(n), sm(n), float(d) ** -0.5, None, ALU.mult), got_in)
        hT_r = norm_T(sm("mixg")[:, 0:8], [got_in, got_in], 22528)
        PROJ, QM, KV, KF, OO = 0, 3904, 5440, 7488, 9024
        QT1, KT1, QT2, KT2, SC = 11072, 13120, 15168, 17216, 19264
        proj = V(PROJ, 2, 1952)
        pj_tok = []
        for j, n in enumerate((512, 512, 512, 416)):
            def done(t, bk, tk, j=j, n=n):
                A(act(proj[:, t, 512 * j:512 * j + n], bank(bk, n), ACT.Copy), tk)
                fr[bk] = [A.prev]
            lin_tok("w_in", n, (HH, HL), hT_r, done, 2 * (j % 2))
            pj_tok.append(A.prev)

        def head_rstd(src, n, d, scratch, ready, eng=None):
            so = stat(n)
            r = ar[:, so:so + n]
            D(tt(scratch, src, src, ALU.mult), ready)
            D(lambda e: e.tensor_reduce(r, scratch, AX.X, ALU.add), D.prev)
            return r, rstd(r, d, r, D.prev)

        ctok = None
        cT = V(SC, 3, 256)
        last = None
        for t in range(2):
            so = stat(2)
            s2 = ar[:, so:so + 2]
            A(act(V(SC + 768, 256), proj[:, t, 0:256], ACT.Square, accum_out=s2[:, 0:1]), pj_tok[0], A.prev)
            A(act(V(SC + 1024, 128), proj[:, t, 256:384], ACT.Square, accum_out=s2[:, 1:2]), A.prev)
            D(ts(s2[:, 0:1], s2[:, 0:1], 1.0 / 256, EPS, ALU.mult, ALU.add), A.prev)
            D(ts(s2[:, 1:2], s2[:, 1:2], 1.0 / 128, EPS, ALU.mult, ALU.add), A.prev)
            A(act(s2, s2, ACT.Sqrt), D.prev)
            D(lambda e, s2=s2: e.reciprocal(s2, s2), A.prev)
            D(ts(proj[:, t, 0:256], proj[:, t, 0:256], s2[:, 0:1], None, ALU.mult), D.prev)
            D(ts(proj[:, t, 256:384], proj[:, t, 256:384], s2[:, 1:2], None, ALU.mult), D.prev)
            tk = tps([(bank(2, 4, 128)[:, k, :], proj[:, t, k * 128:(k + 1) * 128], ident) for k in range(3)],
                     [D.prev, fr[2]])
            gc = ar[:, OFF_SM + SML["gcq"][0]:OFF_SM + SML["gcq"][0] + 3]
            D(tt(cT[:, :, t * 128:(t + 1) * 128], bank(2, 4, 128)[:, 0:3, :], B(gc.unsqueeze(2), [128, 3, 128]),
                 ALU.mult), tk)
            fr[2] = [D.prev]
        CH = hth[:, 0:768].rearrange("p (a b) -> p a b", a=3)
        CL = htl[:, 0:768].rearrange("p (a b) -> p a b", a=3)
        ctok = cut_act(CH, CL, cT, D.prev, P.prev)
        qm = V(QM, 2, 768)
        kv = V(KV, 2, 1024)
        for k in range(2):
            h, l, ok, no = take("w_uq")
            lst = []
            for t in range(2):
                for hf in range(2):
                    c = slice(hf * 384, (hf + 1) * 384)
                    lst += p3(bank(2 + 2 * t + hf, 384), [x[:, k, t * 128:(t + 1) * 128] for x in (CH, CL)],
                              (h[:, c], l[:, c]), k == 0, k == 1)
            tk = mms(lst, [ok, ctok] + fr[2] + fr[3] + fr[4] + fr[5])
            hl_free[no] = tk
        for t in range(2):
            for hf in range(2):
                bk = 2 + 2 * t + hf
                A(act(qm[:, t, hf * 384:(hf + 1) * 384], bank(bk, 384), ACT.Copy), tk)
                fr[bk] = [A.prev]
        q_r = A.prev
        h, l, ok, no = take("w_ukv")
        for t in range(2):
            lst = []
            for hf in range(2):
                c = slice(hf * 512, (hf + 1) * 512)
                lst += p3(bank(6 * t + hf, 512), [x[:, 2, t * 128:(t + 1) * 128] for x in (CH, CL)],
                          (h[:, c], l[:, c]), True, True)
            b0 = 0 if t == 0 else 6
            tk = mms(lst, [ok, fr[b0], fr[b0 + 1]])
            for hf in range(2):
                A(act(kv[:, t, hf * 512:(hf + 1) * 512], bank(b0 + hf, 512), ACT.Copy), tk)
                fr[b0 + hf] = [A.prev]
        hl_free[no] = tk
        kv_r = A.prev

        cosv = sm("cos").rearrange("p (t a d) -> p t a d", t=2, a=1)
        sinv = sm("sin").rearrange("p (t a d) -> p t a d", t=2, a=1)
        rtmp = [V(SC + 2048 + 256 * m, 2, 8, 16) for m in range(4)]

        def rope(src, dst, nh, ready, war=None):
            c, s = B(cosv, [128, 2, nh, 16]), B(sinv, [128, 2, nh, 16])
            x1, x2 = src[:, :, :, 0:16], src[:, :, :, 16:32]
            m = [r[:, :, 0:nh, :] for r in rtmp]
            D(tt(m[0], x1, c, ALU.mult), ready, war)
            D(tt(m[1], x2, s, ALU.mult))
            D(tt(m[2], x1, s, ALU.mult))
            D(tt(m[3], x2, c, ALU.mult))
            D(tt(dst[:, :, :, 0:16], m[0], m[1], ALU.subtract), D.prev)
            return D(tt(dst[:, :, :, 16:32], m[2], m[3], ALU.add), D.prev)

        q4 = qm.rearrange("p t (h d) -> p t h d", h=8)
        rope(q4[:, :, :, 64:96], q4[:, :, :, 64:96], 8, q_r)
        kf4 = V(KF, 2, 8, 96)
        kr4 = proj[:, :, 384:416].rearrange("p t (a d) -> p t a d", a=1)
        rope(kr4, kr4, 1, [pj_tok[0], D.prev])
        kv4 = kv.rearrange("p t (h d) -> p t h d", h=8)
        for t in range(2):
            D(cp(kf4[:, t, :, 64:96], B(kr4[:, t, :, :], [128, 8, 32])), D.prev)
            D(cp(kf4[:, t, :, 0:64], kv4[:, t, :, 0:64]), kv_r)

        sq = V(SC + 3072, 1536)

        def scale_heads(src, n, d, ready):
            r, _ = head_rstd(src, n, d, sq[:, 0:n * d].rearrange("p (a b) -> p a b", a=n), ready)
            return D(tt(src, src, B(r.unsqueeze(2), [128, n, d]), ALU.mult), D.prev)

        def heads_T(src, nh, d, t, dst, gain, ready):
            for b in range((nh + 3) // 4):
                bk = 2 + (hrot[0] % 4)
                hrot[0] += 1
                m = min(4, nh - 4 * b)
                tk = tps([(ps[bk][0:d, k * 128:(k + 1) * 128], src[:, (4 * b + k) * d:(4 * b + k + 1) * d], ident)
                          for k in range(m)], [ready, fr[bk]])
                A(act(dst[0:d, 4 * b:4 * b + m, t * 128:(t + 1) * 128],
                      ps[bk][0:d, 0:m * 128].rearrange("p (a b) -> p a b", a=m), ACT.Copy, scale=gain), tk, qg_r)
                fr[bk] = [A.prev]
            return A.prev

        hrot = [0]
        qt1, kt1, qt2, kt2 = V(QT1, 8, 256), V(KT1, 8, 256), V(QT2, 8, 256), V(KT2, 8, 256)
        qtk = scale_heads(V(QM, 16, 96), 16, 96, D.prev)
        ktk = scale_heads(V(KF, 16, 96), 16, 96, D.prev)
        for t in range(2):
            heads_T(V(QM + 768 * t, 768), 8, 96, t, qt1, sm("gqmla", 96), qtk)
            r1 = heads_T(V(KF + 768 * t, 768), 8, 96, t, kt1, sm("gkmla", 96), ktk)
        for t in range(2):
            for which, dst, g in ((0, qt2, "gqmoba"), (1, kt2, "gkmoba")):
                src = proj[:, t, 416 + 512 * which:928 + 512 * which]
                tk = scale_heads(src.rearrange("p (a b) -> p a b", a=8), 8, 64, [pj_tok[3], D.prev])
                r2 = heads_T(src, 8, 64, t, dst, sm(g, 64), tk)

        def attention(units, ready):
            n = len(units)
            tok = [dict() for _ in units]
            st_off = [(OFF_HN + 512 * (u % 2), OFF_HN + 1024 + 512 * (u % 2)) for u in range(n)]
            dn = [stat(0) for _ in units]
            DN = V(ATT_ST, n, 2)
            NM = V(ATT_ST + 2 * n, n, 2)
            SE = V(ATT_ST + 4 * n, n, 2)
            for step in range(n + 3):
                u = step
                if u < n:
                    c = units[u]
                    K = c["K"]
                    bk = u % 2
                    tok[u]["s"] = mms([(bank(bk, 2, K)[:, h, :], c["q"][h], c["k"][h], True, True) for h in range(2)],
                                      [ready, fr[bk]])
                u = step - 2
                if 0 <= u < n:
                    c = units[u]
                    K = c["K"]
                    nk = K // 128
                    bk = 2 + u % 2
                    sv = V(st_off[u][0], 2, K)
                    tok[u]["t"] = tps([(bank(bk, 2 * nk, 128)[:, h * nk + kb, :], sv[:, h, kb * 128:(kb + 1) * 128], ident)
                                       for h in range(2) for kb in range(nk)], [tok[u]["e"], fr[bk]])
                u = step - 3
                if 0 <= u < n:
                    c = units[u]
                    nk = c["K"] // 128
                    bk = 4 + u % 2
                    pt = V(st_off[u][1], 2 * nk, 128)
                    tok[u]["o"] = mms([(bank(bk, 2, 64)[:, h, :], pt[:, h * nk + kb, :], c["v"][h][kb], kb == 0, kb == nk - 1)
                                       for h in range(2) for kb in range(nk)], [tok[u]["pt"], fr[bk]])
                u = step
                if u < n:
                    c = units[u]
                    K = c["K"]
                    bk = u % 2
                    sv = V(st_off[u][0], 2, K)
                    sp = bank(bk, 2, K)
                    war = [tok[u - 2]["t"]] if u >= 2 else []
                    if c["bias"] is not None:
                        D(tt(sv, sp, c["bias"], ALU.add), tok[u]["s"], war)
                    elif K == 128:
                        D(tt(sv, sp, B(sm("cmask").unsqueeze(1), [128, 2, 128]), ALU.add), tok[u]["s"], war)
                    else:
                        D(tt(sv[:, :, 128:256], sp[:, :, 128:256], B(sm("cmask").unsqueeze(1), [128, 2, 128]), ALU.add),
                          tok[u]["s"], war)
                        D(cp(sv[:, :, 0:128], sp[:, :, 0:128]))
                    fr[bk] = [D.prev]
                    nm = NM[:, u, :]
                    D(lambda e, nm=nm, sv=sv: e.tensor_reduce(nm, sv, AX.X, ALU.max, negate=True), D.prev)
                    if c["sink"] is not None:
                        se = SE[:, u, :]
                        D(stt(nm, c["sink"], -1.0, nm, ALU.mult, ALU.min), D.prev)
                        D(tt(se, c["sink"], nm, ALU.add), D.prev)
                    dt = D.prev
                    for h in range(2):
                        A(act(sv[:, h, :], sv[:, h, :], ACT.Exp, bias=nm[:, h:h + 1], accum_out=DN[:, u, h:h + 1]), dt)
                    if c["sink"] is not None:
                        A(act(se, se, ACT.Exp), dt)
                    tok[u]["e"] = A.prev
                u = step - 2
                if 0 <= u < n:
                    c = units[u]
                    nk = c["K"] // 128
                    bk = 2 + u % 2
                    pt = V(st_off[u][1], 2 * nk, 128)
                    war = [tok[u - 2]["o"]] if u >= 2 else []
                    A(act(pt, bank(bk, 2 * nk, 128), ACT.Copy), tok[u]["t"], war)
                    tok[u]["pt"] = A.prev
                    fr[bk] = [A.prev]
                    dn = DN[:, u, :]
                    if c["sink"] is not None:
                        D(tt(dn, dn, SE[:, u, :], ALU.add), tok[u]["e"])
                    D(lambda e, dn=dn: e.reciprocal(dn, dn), tok[u]["e"], D.prev)
                    tok[u]["r"] = D.prev
                u = step - 3
                if 0 <= u < n:
                    c = units[u]
                    bk = 4 + u % 2
                    D(tt(c["o"], bank(bk, 2, 64), B(DN[:, u, :].unsqueeze(2), [128, 2, 64]), ALU.mult),
                      tok[u]["o"], tok[u]["r"])
                    fr[bk] = [D.prev]
            return D.prev

        ATT_ST = SC
        oo = V(OO, 2, 1024)
        units = []
        for fam in range(2):
            qt, kt, d = ((qt1, kt1, 96), (qt2, kt2, 64))[fam]
            for hp in range(4):
                for t in range(2):
                    K = 128 * (t + 1)
                    hs = (2 * hp, 2 * hp + 1)
                    if fam == 0:
                        vv = [[kv4[:, kb, h, 64:128] for kb in range(2)] for h in hs]
                    else:
                        vv = [[proj[:, kb, 1440 + 64 * h:1504 + 64 * h] for kb in range(2)] for h in hs]
                    units.append(dict(K=K, q=[qt[0:d, h, t * 128:(t + 1) * 128] for h in hs],
                                      k=[kt[0:d, h, 0:K] for h in hs], v=vv, bias=None, sink=None,
                                      o=oo[:, t, 512 * fam + 128 * hp:512 * fam + 128 * (hp + 1)].rearrange(
                                          "p (a b) -> p a b", a=2)))
        att = attention(units, [r1, r2, kv_r, pj_tok[3], got_in])

        def to_T(src_of, at_raw, ready, gain=None, nchunk=8, c0=0):
            raw_T = V(at_raw, nchunk, 256)
            free = P.prev
            toks = []
            for t in range(2):
                for b in range(nchunk // 4):
                    bk = 6 + b % 2
                    tk = tps([(bank(bk, 4, 128)[:, k, :], src_of(t)[:, (4 * b + k) * 128:(4 * b + k + 1) * 128], ident)
                              for k in range(4)], [ready, fr[bk]])
                    cols = slice(t * 128, (t + 1) * 128)
                    d = raw_T[:, 4 * b:4 * b + 4, cols]
                    if gain is None:
                        D(cp(d, bank(bk, 4, 128)), tk)
                    else:
                        D(tt(d, bank(bk, 4, 128), B(gain[:, 4 * b:4 * b + 4].unsqueeze(2), [128, 4, 128]), ALU.mult), tk)
                    fr[bk] = [D.prev]
                    c = slice(c0 + 4 * b, c0 + 4 * b + 4)
                    toks += cut_act(HH[:, c, cols], HL[:, c, cols], d, D.prev, free)
            return toks

        def mix_out(wname, ready, gate=None):
            for j in range(2):
                def done(t, bk, tk, j=j):
                    xs = xr[:, t, 512 * j:512 * (j + 1)]
                    if gate is None:
                        D(tt(xs, bank(bk, 512), xs, ALU.add), tk)
                    else:
                        tmp = V(OFF_HN + 512 * t, 512)
                        D(tt(tmp, bank(bk, 512), gate[:, 512 * j:512 * (j + 1)], ALU.mult), tk)
                        D(tt(xs, tmp, xs, ALU.add), D.prev)
                    fr[bk] = [D.prev]
                lin_tok(wname, 512, (HH, HL), ready, done, 2 * j)
            return [D.prev, D.prev]

        oT_r = to_T(lambda t: oo[:, t, :], 24576, att)
        x_r = mix_out("w_o", oT_r)

        CO = stat(16)
        cond = ar[:, CO:CO + 8]
        ct2 = ar[:, CO + 8:CO + 16]
        MT = OFF_ST + NST - 32
        modT = V(MT, 4, 8)
        gb = V(OFF_GB, 2, 1024)

        def ada_setup():
            A(act(ct2, sm("c"), ACT.Exp, scale=-1.0), got_in)
            D(ts(ct2, ct2, 1.0, None, ALU.add), A.prev)
            D(lambda e: e.reciprocal(ct2, ct2), D.prev)
            D(tt(cond, ct2, sm("c"), ALU.mult), D.prev)

        ADA = [OFF_X + 15872, OFF_X + 16128]
        ada_mm = [None, None]
        ada_n = [0]
        ada_state = dict(pending=None)

        def ada_load():
            n, half = ada_n[0] // 2, ada_n[0] % 2
            ada_n[0] += 1
            src, landed, i = take_raw("w_ada")
            w = src.rearrange("p (k n) -> p k n", k=4)
            acc = V(ADA[n % 2], 256)
            for k in range(4):
                c = cond[:, 4 * half + k:4 * half + k + 1]
                if half == 0 and k == 0:
                    D(ts(acc, w[:, 0, :], c, None, ALU.mult), landed, ada_mm[n % 2], D.prev)
                else:
                    D(stt(acc, w[:, k, :], c, acc, ALU.mult, ALU.add), landed, D.prev)
            raw_free[i] = [D.prev]
            if half == 1:
                ada_state["pending"] = (n, acc, D.prev)

        def ada_use():
            if ada_state["pending"] is None:
                return
            n, acc, tok = ada_state["pending"]
            ada_state["pending"] = None
            part, j = n // 4, n % 4
            if part in (2, 5):
                tk = mms([(bank(7, 256), sm("ones"), acc, True, True)], [tok, fr[7]])
                g = gb[:, 0 if part == 2 else 1, 256 * j:256 * (j + 1)]
                D(tt(g, bank(7, 256), g, ALU.add), tk, got_in)
            else:
                row = {0: 0, 1: 1, 3: 2, 4: 3}[part]
                tk = mms([(ps[7][:, m:m + 1], acc[:, 128 * m:128 * (m + 1)], sm("ones")[:, 0:1], True, True)
                          for m in range(2)], [tok, fr[7]])
                b0 = OFF_SM + SML["bada"][0] + 8 * row + 2 * j
                D(tt(modT[:, row, 2 * j:2 * j + 2], ps[7][:, 0:2], ar[:, b0:b0 + 2], ALU.add), tk)
            fr[7] = [D.prev]
            ada_mm[n % 2] = tk

        def cut_pair(src, n, *after):
            q = n % 4
            hi, lo = HQ[q]
            tok = cut_act(hi, lo, src, hq_free.get(q), *after)
            return [x.rearrange("p (m t) -> p m t", m=2) for x in (hi, lo)], tok

        hq_free = {}

        def down(name, units, src_of, ready_of, ada=False):
            nxt = None
            for q in range(4):
                hq_free[q] = P.prev
            nxt = cut_pair(src_of(0), 0, ready_of(0))
            for j in range(units // 2):
                (hi, lo), ok2 = nxt
                for m in range(2):
                    h, l, ok, no = take(name)
                    lst = []
                    for t in range(2):
                        for hf in range(2):
                            c = slice(512 * hf, 512 * (hf + 1))
                            lst += p3(bank(2 + 2 * t + hf, 512), [x[:, m, t * 128:(t + 1) * 128] for x in (hi, lo)],
                                      (h[:, c], l[:, c]), j == 0 and m == 0, j == units // 2 - 1 and m == 1)
                    tk = mms(lst, [ok, ok2] + (fr[2] + fr[3] + fr[4] + fr[5] if j == 0 and m == 0 else []))
                    hl_free[no] = tk
                    if m == 0 and j + 1 < units // 2:
                        nxt = cut_pair(src_of(j + 1), j + 1, ready_of(j + 1))
                    if ada:
                        ada_use()
                        if ada_n[0] < 48:
                            ada_load()
                hq_free[j % 4] = tk
            return tk

        def ffn(layer, x_ready, war, ada=False, side=None):
            hr = norm_T(sm("ffng")[:, 8 * layer:8 * layer + 8], x_ready, 0)
            aT = V(0, 32, 256)
            done = {}
            for j in range(16):
                bk = j % 2
                for m in range(2):
                    tk = lin_T("w_ff1", bk, m, hr, fr[bk] if m == 0 else ())
                    if ada:
                        ada_use()
                        ada_load()
                    if side is not None:
                        next(side, None)
                d = aT[:, 2 * j:2 * j + 2, :]
                A(act(d, bank(bk, 2, 256), ACT.Relu), tk, war, hr)
                fr[bk] = [A.prev]
                done[j] = D(tt(d, d, d, ALU.mult), A.prev)
            tk = down("w_ff2", 32, lambda j: V(512 * j, 512), lambda j: done[j], ada)
            toks = []
            for t in range(2):
                for hf in range(2):
                    b = 2 + 2 * t + hf
                    xs = xr[:, t, 512 * hf:512 * (hf + 1)]
                    D(tt(xs, bank(b, 512), xs, ALU.add), tk)
                    fr[b] = [D.prev]
                toks.append(D.prev)
            return toks, tk

        ada_setup()

        EO, BO, WO, CI = 16384, 8192, 10240, 13312
        Er, Ei = V(EO, 32, 256), V(EO + 8192, 32, 256)
        s5t = V(CI + 1024, 40, 32)
        row = lambda k: s5t[:, k, :]

        def s5_prep(war):
            L, LI, LT = sm("lre"), sm("lim"), sm("ldt")
            (dt, xx, nn, rr, pp, s2n, em, ex, th, kk, sn, cs, hs, cm1, are, aim, den, cr, ci, t1, t2, pr, pi) = [
                row(k) for k in range(23)]
            LOG2E = 1.0 / math.log(2.0)

            A.dma(lambda e: e.dma_start(V(4096, 1024), T["b5"]), key_sem, war)
            A.dma(lambda e: e.dma_start(V(5120, 1024), T["c5"]), key_sem)
            bc_r = (key_sem, 32)

            def expo(x, want_em):
                D(ts(x, x, -87.0, 88.0, ALU.max, ALU.min), D.prev, war)
                D(ts(nn, x, LOG2E, 12582912.0, ALU.mult, ALU.add), D.prev)
                D(ts(nn, nn, 12582912.0, None, ALU.subtract), D.prev)
                D(stt(rr, nn, -0.693359375, x, ALU.mult, ALU.add), D.prev)
                D(stt(rr, nn, 2.12194440e-4, rr, ALU.mult, ALU.add), D.prev)
                D(ts(pp, rr, 1.0 / 5040, 1.0 / 720, ALU.mult, ALU.add), D.prev)
                for c in (1.0 / 120, 1.0 / 24, 1.0 / 6, 0.5, 1.0):
                    D(tt(pp, pp, rr, ALU.mult), D.prev)
                    D(ts(pp, pp, c, None, ALU.add), D.prev)
                D(tt(pp, pp, rr, ALU.mult), D.prev)
                D(ts(nn, nn, 127.0, 8388608.0, ALU.add, ALU.mult), D.prev)
                D(cp(s2n.bitcast(I32), nn), D.prev)
                D(tt(pp, pp, s2n, ALU.mult), D.prev)
                D(tt(ex, pp, s2n, ALU.add), D.prev)
                if want_em:
                    D(ts(em, s2n, 1.0, None, ALU.subtract))
                    D(tt(em, em, pp, ALU.add), D.prev)

            D(cp(xx, LT), got_in, D.prev, war)
            expo(xx, False)
            yield
            D(cp(dt, ex), D.prev)
            D(tt(xx, L, dt, ALU.mult), D.prev)
            expo(xx, True)
            yield
            D(tt(th, LI, dt, ALU.mult), D.prev)
            D(ts(kk, th, 1.0 / (2 * math.pi), 12582912.0, ALU.mult, ALU.add), D.prev)
            D(ts(kk, kk, 12582912.0, None, ALU.subtract), D.prev)
            c1 = 6.28125
            c2 = float(np.float32(2 * math.pi - c1))
            c3 = 2 * math.pi - c1 - c2
            for c in (c1, c2, c3):
                D(stt(th, kk, -c, th, ALU.mult, ALU.add), D.prev)
            D(ts(th, th, -3.1415925, 3.1415925, ALU.max, ALU.min), D.prev)
            D(stt(t1, th, -1.0, th, ALU.mult, ALU.max), D.prev)
            yield
            D(ts(t1, t1, -1.0, math.pi / 2, ALU.mult, ALU.add), D.prev)
            D(ts(t2, th, 0.5, None, ALU.mult), D.prev)
            A(act(sn, th, ACT.Sin), D.prev)
            A(act(cs, t1, ACT.Sin))
            A(act(hs, t2, ACT.Sin))
            D(tt(cm1, hs, hs, ALU.mult), A.prev)
            D(ts(cm1, cm1, -2.0, None, ALU.mult), D.prev)
            D(tt(are, em, cs, ALU.mult), D.prev)
            yield
            D(tt(are, are, cm1, ALU.add), D.prev)
            D(tt(aim, ex, sn, ALU.mult))
            D(tt(den, L, L, ALU.mult))
            D(tt(t1, LI, LI, ALU.mult))
            D(tt(den, den, t1, ALU.add), D.prev)
            yield
            D(lambda e: e.reciprocal(den, den), D.prev)
            D(tt(cr, are, L, ALU.mult))
            D(tt(t1, aim, LI, ALU.mult), D.prev)
            D(tt(cr, cr, t1, ALU.add), D.prev)
            D(tt(cr, cr, den, ALU.mult), D.prev)
            yield
            D(tt(ci, aim, L, ALU.mult))
            D(tt(t2, are, LI, ALU.mult), D.prev)
            D(tt(ci, ci, t2, ALU.subtract), D.prev)
            base = D(tt(ci, ci, den, ALU.mult), D.prev)
            G(lambda e: e.memset(Er[:, :, 0:1], 1.0), war)
            G(lambda e: e.memset(Ei[:, :, 0:1], 0.0))
            G(cp(pr, cs), base)
            G(cp(pi, sn))
            qr, qi, q1 = row(23), row(24), row(25)
            n = 1
            while n < 256:
                for o in range(0, n, 64):
                    w = min(64, n)
                    tm = V(OFF_HN, 32, w)
                    a, b = B(pr.unsqueeze(2), [128, 32, w]), B(pi.unsqueeze(2), [128, 32, w])
                    lo, up = slice(o, o + w), slice(n + o, n + o + w)
                    G(tt(tm, Ei[:, :, lo], b, ALU.mult), G.prev)
                    G(tt(Er[:, :, up], Er[:, :, lo], a, ALU.mult))
                    G(tt(Er[:, :, up], Er[:, :, up], tm, ALU.subtract), G.prev)
                    G(tt(tm, Er[:, :, lo], b, ALU.mult), G.prev)
                    G(tt(Ei[:, :, up], Ei[:, :, lo], a, ALU.mult))
                    G(tt(Ei[:, :, up], Ei[:, :, up], tm, ALU.add), G.prev)
                G(tt(qr, pr, pr, ALU.mult))
                G(tt(q1, pi, pi, ALU.mult))
                G(tt(qi, pr, pi, ALU.mult))
                G(tt(pr, qr, q1, ALU.subtract), G.prev)
                G(tt(pi, qi, qi, ALU.add), G.prev)
                n *= 2
            S5["e"] = G.prev
            yield
            bl = V(4096, 2, 8, 64)
            cl = V(5120, 2, 32, 16)
            hp = sm("hpar")
            for ri, dst in ((0, BTr), (1, BTi)):
                for h in range(2):
                    D(ts(dst[:, :, 64 * h:64 * h + 64], bl[:, ri, :, :], hp[:, h:h + 1], None, ALU.mult), bc_r)
                yield
            m1, m2 = V(6144, 32, 16), V(6656, 32, 16)
            c1, c2 = V(7168, 32, 16), V(7680, 32, 16)
            crb, cib = B(cr.unsqueeze(2), [128, 32, 16]), B(ci.unsqueeze(2), [128, 32, 16])
            D(tt(m1, cl[:, 0], crb, ALU.mult), bc_r, base)
            D(tt(m2, cl[:, 1], cib, ALU.mult))
            D(tt(c1, m1, m2, ALU.subtract), D.prev)
            yield
            D(tt(m1, cl[:, 0], cib, ALU.mult), D.prev)
            D(tt(m2, cl[:, 1], crb, ALU.mult), D.prev)
            D(tt(c2, m1, m2, ALU.add), D.prev)
            yield
            for h in range(2):
                mask = sm("bones")[:, 64 * h:64 * h + 1]
                D(ts(W1[:, :, 16 * h:16 * h + 16], c1, mask, 64.0, ALU.mult, ALU.mult), D.prev)
                D(ts(W1n[:, :, 16 * h:16 * h + 16], c1, mask, -64.0, ALU.mult, ALU.mult), D.prev)
                D(ts(W2[:, :, 16 * h:16 * h + 16], c2, mask, -64.0, ALU.mult, ALU.mult), D.prev)
                yield
            S5["tab"] = D.prev
            S5["r"] = ex

        S5 = {}
        BTr, BTi = V(BO, 8, 128), V(BO + 1024, 8, 128)
        W1, W1n, W2 = V(WO, 32, 32), V(WO + 1024, 32, 32), V(WO + 2048, 32, 32)
        side = s5_prep([att, x_r[1]])
        x_r, ff_last = ffn(0, x_r, att, ada=True, side=side)
        assert next(side, None) is None and "tab" in S5
        tab_r, e_ready, r_ap = S5["tab"], S5["e"], S5["r"]

        hr = norm_T(sm("mixg")[:, 8:16], x_r, 6144, extra=e_ready, cut=False)
        hT = V(6144, 8, 256)
        def sc5(q, k):
            return V(512 * 0 + (q % 2) * 2048 + 256 * k, 256)
        pe_c = {}
        gT = V(4096, 8, 256)
        ybank = [4, 5]
        bu = {}

        def s5_bu(q):
            c, j = q // 4, q % 4
            bk = q % 4
            rows = slice(32 * j, 32 * j + 32)
            bu[q] = mms([(bank(bk, 2, 256)[:, 0, :], BTr[rows, c, :], hT[rows, c, :], True, True),
                         (bank(bk, 2, 256)[:, 1, :], BTi[rows, c, :], hT[rows, c, :], True, True)],
                        [hr, tab_r, fr[bk]])

        g_tok = []
        for q in range(2):
            s5_bu(q)
        for q in range(32):
            if q + 2 < 32:
                s5_bu(q + 2)
            c, j = q // 4, q % 4
            bk = q % 4
            er, ei = Er[:, q, :], Ei[:, q, :]
            br, bi = bank(bk, 2, 256)[:, 0, :], bank(bk, 2, 256)[:, 1, :]
            a1, a2, a3, a4, v1, v2, h1, h2 = [sc5(q, k) for k in range(8)]
            war = pe_c.get(q - 2)
            D(tt(a1, br, er, ALU.mult), bu[q], e_ready, war)
            D(tt(a2, bi, ei, ALU.mult))
            D(tt(a3, bi, er, ALU.mult))
            D(tt(a4, br, ei, ALU.mult))
            fr[bk] = [D.prev]
            dm = D.prev
            G(tt(v1, a1, a2, ALU.add), dm, war)
            G(tt(v2, a3, a4, ALU.subtract))
            rb = B(r_ap[:, q:q + 1], [128, 256])
            D(lambda e, h1=h1, rb=rb, v1=v1: e.tensor_tensor_scan(h1, rb, v1, 0.0, ALU.mult, ALU.add), G.prev)
            D(lambda e, h2=h2, rb=rb, v2=v2: e.tensor_tensor_scan(h2, rb, v2, 0.0, ALU.mult, ALU.add))
            sc = D.prev
            D(tt(a1, h1, er, ALU.mult), sc, G.prev)
            D(tt(a4, h2, er, ALU.mult))
            dd = D.prev
            G(tt(a2, h2, ei, ALU.mult), sc)
            G(tt(a3, h1, ei, ALU.mult))
            yb = ybank[c % 2]
            yo = ps[yb][32 * j:32 * j + 32, 0:256]
            pe_c[q] = mms([(yo, W1[:, q, :], a1, True, False), (yo, W1n[:, q, :], a2, False, False),
                           (yo, W2[:, q, :], a3, False, False), (yo, W2[:, q, :], a4, False, True)],
                          [dd, G.prev, fr[yb] if j == 0 else None])
            if j == 3:
                ds = sm("dskip")[:, c:c + 1]
                D(stt(gT[:, c, :], hT[:, c, :], ds, ps[yb][:, 0:256], ALU.mult, ALU.add), pe_c[q])
                fr[yb] = [D.prev]
                A(act(gT[:, c, :], gT[:, c, :], ACT.Gelu_apprx_tanh), D.prev)
                g_tok += cut_act(HH[:, c, :], HL[:, c, :], gT[:, c, :], A.prev)
        glu_free = {}
        for j in range(2):
            keep = {}
            def vals(t, bk, tk):
                keep[t] = (bk, tk)
            def gates(t, bk, tk, j=j):
                s = V(OFF_HN + 512 * t, 512)
                A(act(s, bank(bk, 512), ACT.Sigmoid), tk, glu_free.get(t))
                vb, vt = keep[t]
                D(tt(s, bank(vb, 512), s, ALU.mult), A.prev, vt)
                fr[vb] = [D.prev]
                fr[bk] = [A.prev]
                xs = xr[:, t, 512 * j:512 * (j + 1)]
                D(tt(xs, xs, s, ALU.add), D.prev)
                glu_free[t] = D.prev
            lin_tok("w_glu", 512, (HH, HL), g_tok, vals, 0 if j == 0 else 4)
            tk = lin_tok("w_glu", 512, (HH, HL), g_tok, gates, 2)
        x_r, ff_last = ffn(1, [D.prev, D.prev], [tk, D.prev])

        gs = stat(8)
        gsc = ar[:, gs:gs + 8]
        D(stt(gsc, modT[:, 1, :], 1.0, sm("n1g"), ALU.add, ALU.mult), D.prev)
        hr = norm_T(gsc, x_r, 20480, shift=modT[:, 0, :], extra=D.prev)
        WB = 16384
        A.dma(lambda e: e.dma_start(V(WB, 2048), T["wbias"]), key_sem, ff_last, x_r)
        A.dma(lambda e: e.dma_start(V(WB + 2048, 256), T["wmask"]), key_sem)
        wb_in = (key_sem, 64)
        wb = V(WB, 8, 256)
        wb_r = D(tt(wb, wb, B(V(WB + 2048, 256).unsqueeze(1), [128, 8, 256]), ALU.add), wb_in)
        CV = 0
        cw = sm("convw").rearrange("p (j c) -> p j c", j=3)
        cps = []
        cvT = V(CV, 12, 256)
        for j in range(6):
            bk = j % 2
            for m in range(2):
                tk = lin_T("w_conv", bk, m, hr, fr[bk] if m == 0 else ())
            A(act(cvT[:, 2 * j:2 * j + 2, :], bank(bk, 2, 256), ACT.Copy), tk, ff_last, x_r)
            fr[bk] = [A.prev]
            cps.append(A.prev)
        pj2 = V(4096, 2, 768)
        pj2_t = []
        for j, n in enumerate((512, 256)):
            def done(t, bk, tk, j=j, n=n):
                A(act(pj2[:, t, 512 * j:512 * j + n], bank(bk, n), ACT.Copy), tk)
                fr[bk] = [A.prev]
            hT_free = lin_tok("w_qkv", n, (HH, HL), hr, done, 2 * j)
            pj2_t.append(A.prev)
        sq = V(12288, 1536)
        sq_ = sq
        KT3, QT3 = 6144, 7168
        qt3, kt3 = V(QT3, 8, 256), V(KT3, 2, 256)
        for t in range(2):
            src = pj2[:, t, 0:512]
            tk = scale_heads(src.rearrange("p (a b) -> p a b", a=8), 8, 64, [pj2_t[0], D.prev])
            heads_T(src, 8, 64, t, qt3, sm("qng", 64), tk)
            src = pj2[:, t, 512:640]
            tk = scale_heads(src.rearrange("p (a b) -> p a b", a=2), 2, 64, [pj2_t[1], D.prev])
            r3 = heads_T(src, 2, 64, t, kt3, sm("kng", 64), tk)
        OO2 = 9216
        oo2 = V(OO2, 2, 512)
        ATT_ST = 11264
        units = []
        for hp in range(4):
            for t in range(2):
                K = 128 * (t + 1)
                hs = (2 * hp, 2 * hp + 1)
                kh = hp // 2
                so = OFF_SM + SML["sinks"][0] + 2 * hp
                units.append(dict(K=K, q=[qt3[0:64, h, t * 128:(t + 1) * 128] for h in hs],
                                  k=[kt3[0:64, kh, 0:K]] * 2,
                                  v=[[pj2[:, kb, 640 + 64 * kh:704 + 64 * kh] for kb in range(2)]] * 2,
                                  bias=wb[:, 2 * hp:2 * hp + 2, 128 * (1 - t):256], sink=ar[:, so:so + 2],
                                  o=oo2[:, t, 128 * hp:128 * (hp + 1)].rearrange("p (a b) -> p a b", a=2)))
        att = attention(units, [r3, wb_r, hr])
        cv = lambda k: cvT[:, k, :]
        YC = 14336
        yT = V(YC, 4, 256)
        cv_tok = []
        for c in range(4):
            cg, hh, bg = cv(3 * c), cv(3 * c + 1), cv(3 * c + 2)
            y = yT[:, c, :]
            D(tt(cg, cg, hh, ALU.mult), cps[5], D.prev)
            D(ts(y, cg, cw[:, 2, c:c + 1], None, ALU.mult), D.prev)
            D(stt(y[:, 1:256], cg[:, 0:255], cw[:, 1, c:c + 1], y[:, 1:256], ALU.mult, ALU.add), D.prev)
            D(stt(y[:, 2:256], cg[:, 0:254], cw[:, 0, c:c + 1], y[:, 2:256], ALU.mult, ALU.add), D.prev)
            D(tt(y, y, bg, ALU.mult), D.prev)
            D(tt(cg, y, y, ALU.mult), D.prev)
            bk = c % 2
            tk = mms([(bank(bk, 256), sm("bones"), cg, True, True)], [D.prev, fr[bk]])
            D(ts(hh, bank(bk, 256), 1.0, EPS, ALU.mult, ALU.add), tk)
            fr[bk] = [D.prev]
            A(act(hh, hh, ACT.Sqrt), D.prev)
            D(lambda e, hh=hh: e.reciprocal(hh, hh), A.prev)
            D(tt(y, y, hh, ALU.mult), D.prev)
            D(ts(y, y, sm("convg")[:, c:c + 1], None, ALU.mult), D.prev)
            cv_tok += cut_act(HH[:, c, :], HL[:, c, :], y, D.prev, hT_free)
        tk = scale_heads(V(OO2, 16, 64), 16, 64, [att, D.prev])
        cv_tok += to_T(lambda t: oo2[:, t, :], 20480, [tk, hT_free], gain=sm("attng"), nchunk=4, c0=4)
        x_r = mix_out("w_out", cv_tok, gate=gb[:, 0, :])

        gs = stat(8)
        gsc = ar[:, gs:gs + 8]
        D(stt(gsc, modT[:, 3, :], 1.0, sm("n2g"), ALU.add, ALU.mult), D.prev)
        hr = norm_T(gsc, x_r, 20480, shift=modT[:, 2, :], extra=D.prev)
        X = V(0, 128, 256)
        QP, SCO = 28672, 24576
        qp = V(QP, 16, 256)
        scs = V(SCO, 2, 16, 128)
        att_all = [D.prev, A.prev, P.prev]
        for j in range(8):
            bk = j % 2
            for m in range(2):
                tk = lin_T("peer_wq", bk, m, hr, fr[bk] if m == 0 else ())
            A(act(qp[:, 2 * j:2 * j + 2, :], bank(bk, 2, 256), ACT.Copy), tk, att_all)
            fr[bk] = [A.prev]
        qp_r = A.prev
        kw = [take_raw("keys") for _ in range(2)]
        sc_t = {}
        for b in range(4):
            src, landed, i = kw[b // 2]
            k8 = src.rearrange("p (a b) -> p a b", a=8)
            for t in range(2):
                bk = 2 + (4 * t + b) % 4
                tk = mms([(bank(bk, 4, 128)[:, m, :], qp[:, 4 * b + m, t * 128:(t + 1) * 128], k8[:, 4 * (b % 2) + m, :],
                           True, True) for m in range(4)], [landed, qp_r, fr[bk]])
                A(act(scs[:, t, 4 * b:4 * b + 4, :], bank(bk, 4, 128), ACT.Copy), tk)
                fr[bk] = [A.prev]
                sc_t[t] = A.prev
            raw_free[i] = [tk]
        scores_done = tk

        u_tok = {}
        u_scr = {}

        def u_pair(j, p_ready=None, side=None):
            bk = j % 2
            for m in range(2):
                tk = lin_T("peer_u", bk, m, hr, fr[bk] if m == 0 else ())
                if side is not None:
                    next(side, None)
            if p_ready is None:
                A(act(X[:, 2 * j:2 * j + 2, :], bank(bk, 2, 256), ACT.Gelu_apprx_tanh), tk, att_all)
                fr[bk] = [A.prev]
                u_tok[j] = A.prev
            else:
                s = V(OFF_HN + 512 * (j % 2), 2, 256)
                A(act(s, bank(bk, 2, 256), ACT.Gelu_apprx_tanh), tk, p_ready, u_scr.get(j - 2))
                fr[bk] = [A.prev]
                xs = X[:, 2 * j:2 * j + 2, :]
                D(tt(xs, xs, s, ALU.mult), A.prev)
                u_scr[j] = D.prev
                u_tok[j] = D.prev

        SEL = QP
        TVa, TIa, TIf = V(SEL, 16, 16), V(SEL + 256, 16, 16), V(SEL + 512, 16, 16)
        CAND = V(SEL + 768, 8, 16, 16)
        CAND2 = V(SEL + 768, 8, 256)
        EQ = V(SEL + 768, 128, 16)
        EQ4 = V(SEL + 768, 8, 256).rearrange("p h (k i) -> p h k i", k=16)
        TV, TI = V(SEL + 2816, 8, 16), V(SEL + 2944, 8, 16)
        PI, PJ = V(SEL + 3072, 128), V(SEL + 3200, 128)
        PIf, PJf = V(SEL + 3328, 128), V(SEL + 3456, 128)
        RIA = [V(SEL + 3584 + 128 * m, 128) for m in range(3)]
        SUM = V(SEL + 3968, 8)
        TMP = [V(OFF_HN + 256 * m, 256) for m in range(2)]
        picked = {}

        def top16(src, tv, ti, tmp, *after):
            D(lambda e: e.max(tv[:, 0:8], src), *after)
            D(lambda e: e.max_index(ti[:, 0:8].bitcast(U32), tv[:, 0:8], src), D.prev)
            D(lambda e: e.match_replace(tmp, tv[:, 0:8], src, NEG * 10), D.prev)
            D(lambda e: e.max(tv[:, 8:16], tmp), D.prev)
            D(lambda e: e.max_index(ti[:, 8:16].bitcast(U32), tv[:, 8:16], tmp), D.prev)

        def select():
            for t in range(2):
                for m in range(16):
                    top16(scs[:, t, m, :], TVa[:, m, :], TIa[:, m, :], TMP[m % 2][:, 0:128], sc_t[t], D.prev, scores_done)
                    yield
                D(cp(TIf, TIa.bitcast(U32)), D.prev)
                va = TVa.rearrange("p (h a) k -> p h a k", a=2)
                D(tt(CAND, B(va[:, :, 0, :].unsqueeze(3), [128, 8, 16, 16]),
                     B(va[:, :, 1, :].unsqueeze(2), [128, 8, 16, 16]), ALU.add), D.prev)
                yield
                yield
                for h in range(8):
                    top16(CAND2[:, h, :], TV[:, h, :], TI[:, h, :], TMP[h % 2], D.prev)
                    yield
                tiu = V(SEL + 2944, 128).bitcast(U32)
                D(lambda e: e.tensor_scalar(PI.bitcast(U32), tiu, 4, None, ALU.logical_shift_right), D.prev)
                D(lambda e: e.tensor_scalar(PJ.bitcast(U32), tiu, 15, None, ALU.bitwise_and))
                D(cp(PIf, PI.bitcast(U32)), D.prev)
                D(cp(PJf, PJ.bitcast(U32)), D.prev)
                yield
                fi = TIf.rearrange("p (h a) k -> p h a k", a=2)
                for which, pf in ((0, PIf), (1, PJf)):
                    D(tt(EQ, B(pf.unsqueeze(2), [128, 128, 16]), B(sm("iota16").unsqueeze(1), [128, 128, 16]),
                         ALU.is_equal), D.prev)
                    yield
                    D(tt(EQ4, EQ4, B(fi[:, :, which, :].unsqueeze(2), [128, 8, 16, 16]), ALU.mult), D.prev)
                    yield
                    D(lambda e, which=which: e.tensor_reduce(RIA[which], EQ, AX.X, ALU.add), D.prev,
                      picked.get(t - 1))
                    yield
                R3 = RIA[2].rearrange("p (h k) -> p h k", h=8)
                D(tt(R3, TV, B(TV[:, :, 0:1], [128, 8, 16]), ALU.subtract), D.prev)
                A(act(R3, R3, ACT.Exp), D.prev)
                yield
                D(lambda e, R3=R3: e.tensor_reduce(SUM, R3, AX.X, ALU.add), A.prev)
                D(lambda e: e.reciprocal(SUM, SUM), D.prev)
                D(tt(R3, R3, B(SUM.unsqueeze(2), [128, 8, 16]), ALU.mult), D.prev)
                sel_done = D.prev
                yield
                tk = tps([(bank(6, 4, 128)[:, m, :], RIA[m], ident) for m in range(3)], [sel_done, fr[6]])
                picked[t] = tk
                itv = V(OFF_GB, 3, 256)[:, :, t * 128:(t + 1) * 128]
                D(cp(itv, bank(6, 4, 128)[:, 0:3, :]), tk, att_all)
                fr[6] = [D.prev]
                picked["all"] = D.prev
                yield

        side = select()
        for j in range(NGA // 2):
            u_pair(j, side=side)
        for _ in side:
            pass
        it_r = picked["all"]
        iaT, ibT, gT_ = V(OFF_GB, 256), V(OFF_GB + 256, 256), V(OFF_GB + 512, 256)
        iota = sm("iota")
        oh_free = {}
        spread_q = []

        def evac_g(s, bk, tk):
            gv = bank(bk, 4, 128).rearrange("p t b -> p b t")
            xs = X[:, 0:NGA, 4 * s:4 * s + 4]
            D(tt(xs, gv[:, 0:NGA, :], xs, ALU.mult), tk, u_all)
            A(act(X[:, NGA:128, 4 * s:4 * s + 4], gv[:, NGA:128, :], ACT.Copy), D.prev, it_r)
            fr[bk] = [A.prev]

        u_all = [u_tok[j] for j in range(NGA // 2)]
        for s in range(64):
            oa = V(OFF_HN + 1024 * (s % 2), 4, 128)
            ob = V(OFF_HN + 1024 * (s % 2) + 512, 4, 128)
            for k in range(4):
                tkn = 4 * s + k
                G(ts(oa[:, k, :], iota, iaT[:, tkn:tkn + 1], None, ALU.is_equal), it_r, oh_free.get(s - 2))
                D(ts(ob[:, k, :], iota, ibT[:, tkn:tkn + 1], gT_[:, tkn:tkn + 1], ALU.is_equal, ALU.mult),
                  it_r, oh_free.get(s - 2))
            bk = 2 + s % 4
            tk = mms([(bank(bk, 4, 128)[:, k, :], oa[:, k, :], ob[:, k, :], True, True) for k in range(4)],
                     [G.prev, D.prev, fr[bk]])
            oh_free[s] = tk
            spread_q.append((s, bk, tk))
            if len(spread_q) > 1:
                evac_g(*spread_q.pop(0))
        while spread_q:
            evac_g(*spread_q.pop(0))
        spread = [D.prev, A.prev]
        for j in range(NGA // 2, 64):
            u_pair(j, spread)
        tk = down("peer_v", 128, lambda j: V(512 * j, 512), lambda j: u_tok[j] if j >= NGA // 2 else spread)
        outd = out.rearrange("a (t p) d -> p (a t) d", p=128)
        for t in range(2):
            for hf in range(2):
                b = 2 + 2 * t + hf
                xs = xr[:, t, 512 * hf:512 * (hf + 1)]
                tmp = V(OFF_HN + 512 * (2 * t + hf), 512)
                D(tt(tmp, bank(b, 512), gb[:, 1, 512 * hf:512 * (hf + 1)], ALU.mult), tk, u_all, u_tok[63])
                D(tt(xs, tmp, xs, ALU.add), D.prev)
            A.dma(lambda e, t=t: e.dma_start(outd[:, t, :], xr[:, t, :]), out_sem, D.prev)
        A.wait((out_sem, 32))

        assert at["plan"] == len(plan)
        loads = Line(nc.sync, None)
        for i, (_, ap, words, _) in enumerate(plan):
            loads.dma(lambda e, ap=ap, i=i: e.dma_start(raw(i)[0], ap), ring_sem[i % NRAW], raw_free.get(i - NRAW))

        block = ctx.enter_context(nc.Block())

        @block.sync
        def _(e):
            loads.run()

        @block.scalar
        def _(e):
            A.run()

        @block.gpsimd
        def _(e):
            G.run()

        @block.vector
        def _(e):
            D.run()

        @block.tensor
        def _(e):
            P.run()



def _cols(v, n):
    return np.ascontiguousarray(v.reshape(n, 128).T)


def _rows(v):
    o = np.zeros((128, 1), np.float32)
    o[:len(v), 0] = v
    return o


def _units_T(w):
    n = w.shape[1] // 128
    return w.reshape(8, 128, n, 128).transpose(2, 1, 0, 3).reshape(n, 128, 1024)


def _units_tok(w, width=512):
    n = w.shape[1] // width
    return w.reshape(4, 2, 128, n, width).transpose(3, 0, 2, 1, 4).reshape(4 * n, 128, 2 * width)


def _bucket(dist):
    d = np.maximum(dist, 1).astype(np.float32)
    large = 16 + (np.log(d / np.float32(16)) / np.float32(math.log(8.0)) * np.float32(16)).astype(np.int32)
    return np.where(dist < 16, dist, np.minimum(large, 31))


def _arrays(a):
    f = np.float32
    p = np.arange(128)
    sml = {}
    sml["ident"] = np.eye(128, dtype=f)
    sml["cmask"] = np.where(p[None, :] <= p[:, None], 0.0, NEG).astype(f)
    sml["iota"] = np.broadcast_to(p.astype(f), (128, 128))
    sml["bones"] = np.where(p[None, :] // 64 == p[:, None] // 64, 1.0 / 64, 0.0).astype(f)
    sml["ones"] = np.ones((128, 128), f)
    inv = f(10000.0) ** (-np.arange(16, dtype=f) / f(16))
    ang = np.arange(256, dtype=f)[:, None] * inv[None, :]
    for n, fn in (("cos", np.cos), ("sin", np.sin)):
        sml[n] = fn(ang).astype(f).reshape(2, 128, 16).transpose(1, 0, 2).reshape(128, 32)
    h = (p // 16) % 2
    sml["hpar"] = np.stack([h == 0, h == 1], 1).astype(f)
    sml["iota16"] = np.broadcast_to(np.arange(16, dtype=f), (128, 16))
    sml["mixg"] = np.concatenate([_cols(a["mix_norm_g"][l], 8) for l in range(2)], 1)
    sml["ffng"] = np.concatenate([_cols(a["ffn_norm_g"][l], 8) for l in range(2)], 1)
    sml["n1g"] = _cols(a["norm1_g_2"][0], 8)
    sml["n2g"] = _cols(a["norm2_g_2"][0], 8)
    sml["gcq"] = _cols(a["g_cq"][0], 2)
    sml["gckv"] = _cols(a["g_ckv"][0], 1)
    for n, k in (("gqmla", "g_qn_mla"), ("gkmla", "g_kn_mla"), ("gqmoba", "g_qn_moba"), ("gkmoba", "g_kn_moba"),
                 ("qng", "q_norm_g_2"), ("kng", "k_norm_g_2")):
        sml[n] = _rows(a[k][0])
    sml["c"] = _cols(a["c_2"][0], 8)
    ba = a["b_ada_2"][0].reshape(6, 1024)
    sml["bada"] = np.concatenate([_cols(ba[r], 8) for r in (0, 1, 3, 4)], 1)
    sml["convw"] = np.concatenate([_cols(a["conv_w_2"][0][j], 4) for j in range(3)], 1)
    sml["convg"] = _cols(a["conv_out_g_2"][0], 4)
    sml["attng"] = _cols(a["attn_out_g_2"][0], 4)
    sml["dskip"] = _cols(a["d_skip"][0], 8)
    sml["sinks"] = np.broadcast_to(a["sinks_2"][0], (128, 8))
    st = lambda v: v.reshape(32, 128).T
    sml["lre"] = st(a["lam_re"][0])
    sml["lim"] = st(a["lam_im"][0])
    sml["ldt"] = st(np.repeat(a["log_dt"][0][:, None], 64, 1))
    small = np.concatenate([np.broadcast_to(sml[n], (128, w)).astype(f) for n, (_, w) in SML.items()], 1)
    r = {"small": small, "x": a["x"][0]}
    r["gb"] = np.broadcast_to(np.concatenate([ba[2], ba[5]]), (128, 2048))
    w = a["w_in"][0]
    for j in range(3):
        r[f"w_in{j}"] = _units_tok(w[:, 512 * j:512 * j + 512])
    r["w_in3"] = _units_tok(w[:, 1536:], 416)
    r["w_uq"] = a["w_uq"][0].reshape(2, 128, 768)
    r["w_ukv"] = a["w_ukv"][0]
    r["w_o"] = _units_tok(a["w_o"][0])
    r["w_ff1"] = np.stack([_units_T(a["w_ff1"][l]) for l in range(2)])
    r["w_ff2"] = a["w_ff2"].reshape(2, 32, 128, 1024)
    r["w_ada"] = a["w_ada_2"][0].reshape(2, 4, 128, 24, 256).transpose(3, 0, 2, 1, 4).reshape(48, 128, 1024)
    glu = _units_tok(a["w_glu"][0])
    r["w_glu"] = np.concatenate([glu[4 * n:4 * n + 4] for n in (0, 2, 1, 3)])
    b = np.stack([a["b_re"][0], a["b_im"][0]])
    r["b5"] = b.reshape(2, 8, 4, 2, 64, 16).transpose(2, 3, 5, 0, 1, 4).reshape(128, 1024)
    c = np.stack([a["c_re"][0], a["c_im"][0]])
    r["c5"] = c.reshape(2, 32, 2, 16, 64).transpose(2, 4, 0, 1, 3).reshape(128, 1024)
    w = a["w_in_2"][0]
    order = [w[:, off + 128 * k:off + 128 * k + 128] for k in range(4) for off in (512, 1024, 0)]
    r["w_conv"] = _units_T(np.concatenate(order, 1))
    r["w_qkv0"] = _units_tok(w[:, 1536:2048])
    r["w_qkv1"] = _units_tok(w[:, 2048:], 256)
    r["w_out"] = _units_tok(a["w_out_2"][0])
    dist = p[:, None] + 128 - np.arange(256)[None, :]
    r["wbias"] = a["rel_bias_2"][_bucket(np.maximum(dist, 0))].transpose(0, 2, 1).reshape(128, 2048)
    r["wmask"] = np.where((dist >= 0) & (dist < 128), 0.0, NEG).astype(f)
    r["peer_wq"] = _units_T(a["peer_wq_2"][0])
    r["keys"] = a["peer_keys_2"][0].transpose(3, 1, 0, 2).reshape(128, 2, 1024).transpose(1, 0, 2)
    u = a["peer_u_2"][0].reshape(128, 128, 8, 128)
    r["peer_u"] = u.transpose(1, 3, 2, 0).reshape(128, 128, 1024)
    r["peer_v"] = a["peer_v_2"][0].reshape(128, 128, 1024).transpose(1, 0, 2)
    return {k: np.ascontiguousarray(v) for k, v in r.items()}


def kernel(**inputs):
    import concourse.bacc as _bacc
    from concourse import mybir as _mybir
    from concourse.bass_utils import run_bass_kernel_spmd as _run

    nc = _bacc.Bacc("TRN2", target_bir_lowering=False, num_devices=1)
    arrays = _arrays({k: np.asarray(v) for k, v in inputs.items()})
    T = {}
    feed = {}
    for name, v in arrays.items():
        feed[f"in_{name}"] = v
        T[name] = nc.dram_tensor(f"in_{name}", v.shape, _mybir.dt.from_np(v.dtype), kind="ExternalInput").ap()
    out = nc.dram_tensor("out_0", (1, 256, 1024), F32, kind="ExternalOutput").ap()
    build(nc, T, out)
    r = _run(nc, [feed], core_ids=[0])
    return r.results[0]["out_0"]
```

```python
import math
from contextlib import ExitStack

import concourse.bass as bass
from concourse import mybir
import numpy as np

ALU = mybir.AluOpType
ACT = mybir.ActivationFunctionType
AX = mybir.AxisListType
F32 = mybir.dt.float32
F32R = mybir.dt.float32r
U32 = mybir.dt.uint32
I32 = mybir.dt.int32

NEG = -1.0e30
EPS = 1e-6
UNIT = 1024
NRAW = 4
CUT = 512
NHL = 4
AHEAD = 3
NGA = 84

OFF_X = 0
OFF_RING = 32768
OFF_XR = OFF_RING + NRAW * UNIT
OFF_GB = OFF_XR + 2048
OFF_HN = OFF_GB + 2048
OFF_SM = OFF_HN + 2048


def small_layout():
    cols = [("ident", 128), ("cmask", 128), ("iota", 128), ("bones", 128), ("ones", 128),
            ("cos", 32), ("sin", 32), ("hpar", 2), ("iota16", 16),
            ("mixg", 16), ("ffng", 16), ("n1g", 8), ("n2g", 8), ("gcq", 2), ("gckv", 1),
            ("gqmla", 1), ("gkmla", 1), ("gqmoba", 1), ("gkmoba", 1), ("qng", 1), ("kng", 1),
            ("c", 8), ("bada", 32), ("convw", 12), ("convg", 4), ("attng", 4), ("dskip", 8),
            ("sinks", 8), ("lre", 32), ("lim", 32), ("ldt", 32)]
    at, out = 0, {}
    for name, n in cols:
        out[name] = (at, n)
        at += n
    return out, at


SML, SMN = small_layout()
OFF_ST = OFF_SM + SMN
NST = 420
OFF_SCR = OFF_ST + NST
WORDS = OFF_SCR + 512


class Line:

    def __init__(self, eng, sem):
        self.eng, self.sem, self.n, self.todo, self.seen = eng, sem, 0, [], {}
        self.prev = None

    def wait(self, *after):
        for tok in after:
            if tok is None:
                continue
            if isinstance(tok, list):
                self.wait(*tok)
                continue
            sem, val = tok
            if self.seen.get(id(sem), 0) < val:
                self.seen[id(sem)] = val
                self.todo.append(lambda s=sem, v=val: self.eng.wait_ge(s, v))

    def __call__(self, fn, *after, inc=True):
        self.wait(*after)
        if inc:
            self.n += 1
            self.todo.append(lambda: fn(self.eng).then_inc(self.sem, 1))
            self.prev = (self.sem, self.n)
            return self.prev
        self.todo.append(lambda: fn(self.eng))
        return None

    def dma(self, fn, sem, *after):
        self.wait(*after)
        self.todo.append(lambda: fn(self.eng).then_inc(sem, 16))

    def run(self):
        for t in self.todo:
            t()


def build(nc, T, out):
    ctx = ExitStack()
    with ctx:
        ar = ctx.enter_context(nc.sbuf_tensor("arena", [128, WORDS], F32))
        hth = ctx.enter_context(nc.sbuf_tensor("act_hi", [128, 2048], F32R))
        htl = ctx.enter_context(nc.sbuf_tensor("act_lo", [128, 2048], F32R))
        wh = ctx.enter_context(nc.sbuf_tensor("w_hi", [128, NHL * CUT], F32R))
        wl = ctx.enter_context(nc.sbuf_tensor("w_lo", [128, NHL * CUT], F32R))
        ps = [ctx.enter_context(nc.psum_tensor(f"ps{i}", [128, 512], F32)) for i in range(8)]
        sem = lambda n: ctx.enter_context(nc.semaphore(n))
        P = Line(nc.tensor, sem("pe_done"))
        D = Line(nc.vector, sem("dve_done"))
        A = Line(nc.scalar, sem("act_done"))
        G = Line(nc.gpsimd, sem("pool_done"))
        ring_sem = [sem(f"ring{i}") for i in range(NRAW)]
        in_sem = sem("inputs")
        out_sem = sem("outputs")
        key_sem = sem("bias_in")
        rank_sem = sem("rank_weights")
        gb_sem = sem("gate_bias")
        x_sem = [sem(f"x{t}") for t in range(2)]
        ada_sem = [sem(f"ada{i}") for i in range(4)]

        def V(off, *dims, p0=0, p1=128):
            n = 1
            for d in dims:
                n *= d
            ap = ar[p0:p1, off:off + n]
            if len(dims) == 2:
                ap = ap.rearrange("p (a b) -> p a b", a=dims[0])
            elif len(dims) == 3:
                ap = ap.rearrange("p (a b c) -> p a b c", a=dims[0], b=dims[1])
            return ap

        def sm(name, p1=128):
            o, n = SML[name]
            return ar[0:p1, OFF_SM + o:OFF_SM + o + n]

        def B(ap, shape):
            return ap.to_broadcast(list(shape))

        def bank(i, *dims, off=0):
            n = 1
            for d in dims:
                n *= d
            ap = ps[i][:, off:off + n]
            if len(dims) == 2:
                ap = ap.rearrange("p (a b) -> p a b", a=dims[0])
            elif len(dims) == 3:
                ap = ap.rearrange("p (a b c) -> p a b c", a=dims[0], b=dims[1])
            return ap

        fr = [[] for _ in range(8)]

        st_at = [0]

        def stat(n):
            assert st_at[0] + n <= NST - 32
            o = OFF_ST + st_at[0]
            st_at[0] += n
            return o

        plan = []
        for j, n in enumerate((512, 512, 512, 416)):
            plan += [("w_in", T[f"w_in{j}"][u], 2 * n, 2) for u in range(4)]
        plan += [("w_o", T["w_o"][u], UNIT, 2) for u in range(8)]
        for layer in range(2):
            ff = [("w_ff1", T["w_ff1"][layer, u], UNIT, 2) for u in range(32)]
            ff += [("w_ff2", T["w_ff2"][layer, u], UNIT, 2) for u in range(32)]
            plan += ff
            if layer == 0:
                plan += [("w_glu", T["w_glu"][u], UNIT, 2) for u in range(16)]
        plan += [("w_qkv", T["w_qkv0"][u], UNIT, 2) for u in range(4)]
        plan += [("w_qkv", T["w_qkv1"][u], 512, 2) for u in range(4)]
        plan += [("w_conv", T["w_conv"][u], UNIT, 2) for u in range(12)]
        plan += [("w_out", T["w_out"][u], UNIT, 2) for u in range(8)]
        plan += [("peer_wq", T["peer_wq"][u], UNIT, 2) for u in range(16)]
        plan += [("keys", T["keys"][u], UNIT, 0) for u in range(2)]
        plan += [("peer_u", T["peer_u"][u], UNIT, 2) for u in range(128)]
        plan += [("peer_v", T["peer_v"][u], UNIT, 2) for u in range(128)]
        raw_free = {}
        cuts = [(i, c) for i, x in enumerate(plan) for c in range(x[3])]
        hl_ready, hl_free = {}, {}
        at = dict(plan=0, made=0, taken=0)

        def raw(i):
            o = OFF_RING + (i % NRAW) * UNIT
            return ar[:, o:o + plan[i][2]], (ring_sem[i % NRAW], 16 * (i // NRAW + 1))

        def cut_weights(n):
            i, c = cuts[n]
            src, landed = raw(i)
            w = plan[i][2] // plan[i][3]
            src = src[:, c * w:(c + 1) * w]
            o = (n % NHL) * CUT
            free = hl_free.get(n - NHL)
            hi, lo = wh[:, o:o + w], wl[:, o:o + w]
            A(act(hi, src, ACT.Copy), landed, free)
            D(tt(lo, src, hi.bitcast(F32), ALU.subtract), A.prev, free)
            raw_free[i] = [D.prev]
            hl_ready[n] = [A.prev, D.prev]

        def take(name):
            n = at["taken"]
            at["taken"] += 1
            i, c = cuts[n]
            assert plan[i][0] == name and i == at["plan"], (name, plan[i][0])
            if c == plan[i][3] - 1:
                at["plan"] += 1
            while at["made"] <= min(n + AHEAD, len(cuts) - 1):
                cut_weights(at["made"])
                at["made"] += 1
            o = (n % NHL) * CUT
            w = plan[i][2] // plan[i][3]
            return wh[:, o:o + w], wl[:, o:o + w], hl_ready[n], n

        def take_raw(name):
            i = at["plan"]
            at["plan"] += 1
            assert plan[i][0] == name and not plan[i][3], (name, plan[i][0])
            src, landed = raw(i)
            return src, landed, i

        def mms(lst, after=()):
            tok = None
            for k, (o, l, r, s, e) in enumerate(lst):
                tok = P(lambda eng, o=o, l=l, r=r, s=s, e=e: eng.matmul(o, l, r, start=s, stop=e),
                        *(after if k == 0 else ()), inc=(k == len(lst) - 1))
            return tok

        def p3(o, l, r, s, e):
            return [(o, l[0], r[0], s, False), (o, l[0], r[1], False, False), (o, l[1], r[0], False, e)]

        def tps(lst, after=()):
            tok = None
            for k, (o, i, idn) in enumerate(lst):
                tok = P(lambda eng, o=o, i=i, idn=idn: eng.transpose(o, i, idn),
                        *(after if k == 0 else ()), inc=(k == len(lst) - 1))
            return tok

        ident = sm("ident")
        xr = V(OFF_XR, 2, 1024)
        HH = hth[:, :].rearrange("p (a b) -> p a b", a=8)
        HL = htl[:, :].rearrange("p (a b) -> p a b", a=8)
        HQ = [(hth[:, 512 * q:512 * (q + 1)], htl[:, 512 * q:512 * (q + 1)]) for q in range(4)]

        def cut_act(hi, lo, src, *after):
            A(act(hi, src, ACT.Copy), *after)
            D(tt(lo, src, hi.bitcast(F32), ALU.subtract), A.prev, *after)
            return [A.prev, D.prev]

        hn = V(OFF_HN, 2, 1024)

        def tt(o, a, b, op):
            return lambda e: e.tensor_tensor(o, a, b, op)

        def ts(o, a, s1, s2, op0, op1=None):
            if op1 is None:
                return lambda e: e.tensor_scalar(o, a, s1, None, op0)
            return lambda e: e.tensor_scalar(o, a, s1, s2, op0, op1)

        def stt(o, a, s, b, op0, op1):
            return lambda e: e.scalar_tensor_tensor(out=o, in0=a, scalar=s, in1=b, op0=op0, op1=op1)

        def act(o, a, f, **k):
            return lambda e: e.activation(o, a, f, **k)

        def cp(o, a):
            return lambda e: e.tensor_copy(o, a)

        def rstd(ss, n, dst, *after):
            D(ts(dst, ss, 1.0 / n, EPS, ALU.mult, ALU.add), *after)
            A(act(dst, dst, ACT.Sqrt), D.prev)
            return D(lambda e: e.reciprocal(dst, dst), A.prev)

        norm_tp = {}
        first_half = [None]

        def by_k(h):
            return lambda k: h[0] if k < 4 else h[1]

        def norm_T(gain, ready, at_raw, shift=None, extra=None, cut=True, early_root=True):
            hT = V(at_raw, 8, 256)
            free = P.prev
            toks, his = [], []
            so = stat(3)
            ss = ar[:, so:so + 2]
            if early_root:
                A(act(ar[:, so + 2:so + 3], sm("ones")[:, 0:1], ACT.Sqrt), got_in)
            for t in range(2):
                A(act(hn[:, t, :], xr[:, t, :], ACT.Square, accum_out=ss[:, t:t + 1]), ready[t], extra)
            sq = A.prev
            rstd(ss, 1024, ss, sq)
            rs = D.prev
            def low(n):
                t, b = n % 2, n // 2
                sl = (slice(None), slice(4 * b, 4 * b + 4), slice(t * 128, (t + 1) * 128))
                toks.append(D(tt(HL[sl], hT[sl], HH[sl].bitcast(F32), ALU.subtract), his[n], free))
                if n == 1:
                    first_half[0] = list(toks)

            for n in range(4):
                t, b = n % 2, n // 2
                half = slice(512 * b, 512 * b + 512)
                hd = D(ts(hn[:, t, half], xr[:, t, half], ss[:, t:t + 1], None, ALU.mult), rs)
                bk = 4 + n
                tp = tps([(bank(bk, 4, 128)[:, k, :], hn[:, t, (4 * b + k) * 128:(4 * b + k + 1) * 128], ident)
                          for k in range(4)], [hd, fr[bk], got_in])
                norm_tp[n] = tp
            for n in range(4):
                t, b = n % 2, n // 2
                bk = 4 + n
                sl = (slice(None), slice(4 * b, 4 * b + 4), slice(t * 128, (t + 1) * 128))
                dst = hT[sl]
                g = gain[:, 4 * b:4 * b + 4]
                D(tt(dst, bank(bk, 4, 128), B(g.unsqueeze(2), [128, 4, 128]), ALU.mult), norm_tp[n], free, got_in)
                fr[bk] = [D.prev]
                if shift is not None:
                    h = shift[:, 4 * b:4 * b + 4]
                    D(tt(dst, dst, B(h.unsqueeze(2), [128, 4, 128]), ALU.add), D.prev)
                if cut:
                    A(act(HH[sl], dst, ACT.Copy), D.prev, free)
                    his.append(A.prev)
                    toks.append(A.prev)
                    if n > 0:
                        low(n - 1)
                else:
                    toks.append(D.prev)
            if cut:
                low(3)
                return [first_half[0], toks]
            return toks

        def lin_tok(name, n, lhs, ready, done, b0=0):
            gen = lin_tok_steps(name, n, lhs, ready, done, b0)
            for _ in gen:
                pass
            return P.prev

        def weave(main, side):
            for _ in main:
                next(side, None)

        def lin_tok_steps(name, n, lhs, ready, done, b0=0):
            bks = (b0, b0 + 1)
            ready_of = ready if callable(ready) else lambda k: ready
            for k in range(8):
                h, l, ok, no = take(name)
                lst = []
                for t in range(2):
                    lst += p3(bank(bks[t], n), [x[:, k, t * 128:(t + 1) * 128] for x in lhs], (h, l), k == 0, k == 7)
                tk = mms(lst, [ok, ready_of(k)] + ([fr[bks[0]], fr[bks[1]]] if k == 0 else []))
                hl_free[no] = tk
                if k < 7:
                    yield
            for t in range(2):
                done(t, bks[t], tk)
            yield

        def lin_T(name, bk, half, ready, free=()):
            for _ in lin_T_steps(name, bk, half, ready, free):
                pass
            return P.prev

        def lin_T_steps(name, bk, half, ready, free=()):
            for c in range(2):
                h, l, ok, no = take(name)
                h, l = [x.rearrange("p (k n) -> p k n", k=4) for x in (h, l)]
                lst = []
                for kk in range(4):
                    k = 4 * c + kk
                    lst += p3(bank(bk, 2, 256)[:, half, :], (h[:, kk, :], l[:, kk, :]), (HH[:, k, :], HL[:, k, :]),
                              k == 0, k == 7)
                hl_free[no] = mms(lst, [ok, ready[c]] + list(free))
                yield

        for t in range(2):
            A.dma(lambda e, t=t: e.dma_start(xr[:, t, :], T["x"][128 * t:128 * t + 128, :]), x_sem[t])
        A.dma(lambda e: e.dma_start(V(OFF_SM, SMN), T["small"]), in_sem)
        got_x = [(x_sem[0], 16), (x_sem[1], 16)]
        got_in = (in_sem, 16)
        RANK = 28800
        G.dma(lambda e: e.dma_start(V(RANK, 2, 768), T["w_uq"].rearrange("k p n -> p k n")), rank_sem, got_in)
        G.dma(lambda e: e.dma_start(V(RANK + 1536, 1024), T["w_ukv"]), rank_sem)
        got_rank = (rank_sem, 32)
        G.dma(lambda e: e.dma_start(V(OFF_GB, 2048), T["gb"]), gb_sem)
        got_gb = (gb_sem, 16)

        hT_r = norm_T(sm("mixg")[:, 0:8], got_x, 22528, early_root=False)
        for n, d in (("gqmla", 96), ("gqmoba", 64), ("qng", 64)):
            qg_r = D(ts(sm(n), sm(n), float(d) ** -0.5, None, ALU.mult), got_in)
        PROJ, QM, KV, KF, OO = 0, 3904, 5440, 7488, 9024
        QT1, KT1, QT2, KT2, SC = 11072, 13120, 15168, 17216, 19264
        proj = V(PROJ, 2, 1952)
        pj_tok = {}

        def block(j, b0):
            n = (512, 512, 512, 416)[j]

            def done(t, bk, tk):
                A(act(proj[:, t, 512 * j:512 * j + n], bank(bk, n), ACT.Copy), tk)
                fr[bk] = [A.prev]
                pj_tok[j] = A.prev
            return lin_tok_steps("w_in", n, (HH, HL), by_k(hT_r), done, b0)

        cT = V(SC, 3, 256)
        c_r = []

        def c_norms():
            so = stat(4)
            s4 = ar[:, so:so + 4]
            for t in range(2):
                A(act(V(SC + 768, 256), proj[:, t, 0:256], ACT.Square, accum_out=s4[:, t:t + 1]), pj_tok[0], A.prev)
                A(act(V(SC + 1024, 128), proj[:, t, 256:384], ACT.Square, accum_out=s4[:, 2 + t:3 + t]), A.prev)
            yield
            D(ts(s4[:, 0:2], s4[:, 0:2], 1.0 / 256, EPS, ALU.mult, ALU.add), A.prev)
            D(ts(s4[:, 2:4], s4[:, 2:4], 1.0 / 128, EPS, ALU.mult, ALU.add))
            A(act(s4, s4, ACT.Sqrt), D.prev)
            rooted = A.prev
            yield
            D(lambda e: e.reciprocal(s4, s4), rooted)
            r = D.prev
            for t in range(2):
                D(ts(proj[:, t, 0:256], proj[:, t, 0:256], s4[:, t:t + 1], None, ALU.mult), r)
                D(ts(proj[:, t, 256:384], proj[:, t, 256:384], s4[:, 2 + t:3 + t], None, ALU.mult), r)
            r = D.prev
            yield
            gc = ar[:, OFF_SM + SML["gcq"][0]:OFF_SM + SML["gcq"][0] + 3]
            tk = {}
            for t in range(2):
                tk[t] = tps([(bank(4 + t, 4, 128)[:, k, :], proj[:, t, k * 128:(k + 1) * 128], ident) for k in range(3)],
                            [r, fr[4 + t]])
            yield
            for t in range(2):
                D(tt(cT[:, :, t * 128:(t + 1) * 128], bank(4 + t, 4, 128)[:, 0:3, :], B(gc.unsqueeze(2), [128, 3, 128]),
                     ALU.mult), tk[t])
                fr[4 + t] = [D.prev]
            c_r.append(D.prev)

        for _ in block(0, 0):
            pass
        side = c_norms()
        weave(block(1, 2), side)
        for _ in side:
            pass
        qm = V(QM, 2, 768)
        kv = V(KV, 2, 1024)
        for k in range(2):
            src = V(RANK + 768 * k, 768)
            tk = mms([(bank(2 + 2 * t + hf, 384), cT[:, k, t * 128:(t + 1) * 128], src[:, 384 * hf:384 * hf + 384],
                       k == 0, k == 1) for t in range(2) for hf in range(2)],
                     [got_rank, c_r[0]] + fr[2] + fr[3] + fr[4] + fr[5])
        for t in range(2):
            for hf in range(2):
                bk = 2 + 2 * t + hf
                A(act(qm[:, t, hf * 384:(hf + 1) * 384], bank(bk, 384), ACT.Copy), tk)
                fr[bk] = [A.prev]
        q_r = A.prev
        src = V(RANK + 1536, 1024)
        for hf in range(2):
            tk = mms([(bank(6 * t + hf, 512), cT[:, 2, t * 128:(t + 1) * 128], src[:, 512 * hf:512 * hf + 512],
                       True, True) for t in range(2)], [got_rank, fr[hf], fr[6 + hf]])
            for t in range(2):
                A(act(kv[:, t, hf * 512:(hf + 1) * 512], bank(6 * t + hf, 512), ACT.Copy), tk)
                fr[6 * t + hf] = [A.prev]
        kv_r = A.prev

        cosv = sm("cos").rearrange("p (t a d) -> p t a d", t=2, a=1)
        sinv = sm("sin").rearrange("p (t a d) -> p t a d", t=2, a=1)
        rtmp = [V(SC + 2048 + 256 * m, 2, 8, 16) for m in range(4)]

        def rope(src, dst, nh, *after):
            c, s = B(cosv, [128, 2, nh, 16]), B(sinv, [128, 2, nh, 16])
            x1, x2 = src[:, :, :, 0:16], src[:, :, :, 16:32]
            m = [r[:, :, 0:nh, :] for r in rtmp]
            D(tt(m[0], x1, c, ALU.mult), *after)
            D(tt(m[1], x2, s, ALU.mult))
            D(tt(m[2], x1, s, ALU.mult))
            D(tt(m[3], x2, c, ALU.mult))
            D(tt(dst[:, :, :, 0:16], m[0], m[1], ALU.subtract), D.prev)
            return D(tt(dst[:, :, :, 16:32], m[2], m[3], ALU.add), D.prev)

        sq = V(SC + 3072, 1536)
        hrot = [0]
        heads_banks = [(2, 3, 4, 5)]

        def scale_heads(src, n, d, got, key, *after):
            so = stat(n)
            r = ar[:, so:so + n]
            view = sq[:, 0:n * d].rearrange("p (a b) -> p a b", a=n)
            A(act(view, src, ACT.Square), *after, sq_free[0])
            squared = A.prev
            yield
            D(lambda e: e.tensor_reduce(r, view, AX.X, ALU.add), squared)
            sq_free[0] = D.prev
            D(ts(r, r, 1.0 / d, EPS, ALU.mult, ALU.add), D.prev)
            A(act(r, r, ACT.Sqrt), D.prev)
            rooted = A.prev
            yield
            D(lambda e: e.reciprocal(r, r), rooted)
            got[key] = D(tt(src, src, B(r.unsqueeze(2), [128, n, d]), ALU.mult), D.prev)

        sq_free = [None]

        def heads_T(src, nh, d, t, dst, gain, ready, got, key):
            for b in range((nh + 3) // 4):
                bk = heads_banks[0][hrot[0] % len(heads_banks[0])]
                hrot[0] += 1
                m = min(4, nh - 4 * b)
                tk = tps([(ps[bk][0:d, k * 128:(k + 1) * 128], src[:, (4 * b + k) * d:(4 * b + k + 1) * d], ident)
                          for k in range(m)], [ready, fr[bk]])
                A(act(dst[0:d, 4 * b:4 * b + m, t * 128:(t + 1) * 128],
                      ps[bk][0:d, 0:m * 128].rearrange("p (a b) -> p a b", a=m), ACT.Copy, scale=gain), tk, qg_r)
                fr[bk] = [A.prev]
                got[key] = A.prev
                yield

        q4 = qm.rearrange("p t (h d) -> p t h d", h=8)
        kf4 = V(KF, 2, 8, 96)
        kr4 = proj[:, :, 384:416].rearrange("p t (a d) -> p t a d", a=1)
        kv4 = kv.rearrange("p t (h d) -> p t h d", h=8)
        qt1, kt1, qt2, kt2 = V(QT1, 8, 256), V(KT1, 8, 256), V(QT2, 8, 256), V(KT2, 8, 256)
        prep = {}

        def mla_prep():
            rope(kr4, kr4, 1, pj_tok[0], c_r[0])
            r = D.prev
            for t in range(2):
                A(act(kf4[:, t, :, 64:96], B(kr4[:, t, :, :], [128, 8, 32]), ACT.Copy), r)
                A(act(kf4[:, t, :, 0:64], kv4[:, t, :, 0:64], ACT.Copy), kv_r)
            kf_r = A.prev
            rope(q4[:, :, :, 64:96], q4[:, :, :, 64:96], 8, q_r, D.prev)
            r = D.prev
            yield
            yield from scale_heads(V(KF, 16, 96), 16, 96, prep, "k1", kf_r)
            yield
            yield from scale_heads(V(QM, 16, 96), 16, 96, prep, "q1", r)
            yield
            for t in range(2):
                yield from heads_T(V(KF + 768 * t, 768), 8, 96, t, kt1, sm("gkmla", 96), prep["k1"], prep, "kt1")
            for t in range(2):
                yield from heads_T(V(QM + 768 * t, 768), 8, 96, t, qt1, sm("gqmla", 96), prep["q1"], prep, "qt1")

        def moba_rows(which, t):
            return proj[:, t, 416 + 512 * which:928 + 512 * which]

        def moba_scale():
            for which in (1, 0):
                for t in range(2):
                    yield from scale_heads(moba_rows(which, t).rearrange("p (a b) -> p a b", a=8), 8, 64, prep,
                                           (which, t), pj_tok[2])
                    yield

        def moba_prep():
            for which, dst, g in ((1, kt2, "gkmoba"), (0, qt2, "gqmoba")):
                for t in range(2):
                    src = moba_rows(which, t)
                    yield from heads_T(src, 8, 64, t, dst, sm(g, 64), prep[which, t], prep, "t2")

        def attention(units, ready):
            n = len(units)
            base = ATT_ST
            tok = [dict() for _ in units]
            DN = V(base, n, 2)
            NM = V(base + 2 * n, n, 2)
            SE = V(base + 4 * n, n, 2)
            sbuf = lambda u: V(base + 128 + 512 * (u % 5), 2, units[u]["K"])
            pbuf = lambda u: V(base + 2688 + 512 * (u % 3), units[u]["K"] // 64, 128)

            def scores(u):
                c = units[u]
                bk = u % 2
                tok[u]["s"] = mms([(bank(bk, 2, c["K"])[:, h, :], c["q"][h], c["k"][h], True, True) for h in range(2)],
                                  [ready(u), fr[bk]])

            def mask(u):
                c = units[u]
                K = c["K"]
                bk = u % 2
                sv, sp = sbuf(u), bank(bk, 2, K)
                war = tok[u - 5]["t"] if u >= 5 else None
                if c["bias"] is not None:
                    D(tt(sv, sp, c["bias"], ALU.add), tok[u]["s"], war)
                elif K == 128:
                    D(tt(sv, sp, B(sm("cmask").unsqueeze(1), [128, 2, 128]), ALU.add), tok[u]["s"], war)
                else:
                    D(tt(sv[:, :, 128:256], sp[:, :, 128:256], B(sm("cmask").unsqueeze(1), [128, 2, 128]), ALU.add),
                      tok[u]["s"], war)
                    D(cp(sv[:, :, 0:128], sp[:, :, 0:128]))
                fr[bk] = [D.prev]
                nm = NM[:, u, :]
                D(lambda e: e.tensor_reduce(nm, sv, AX.X, ALU.max, negate=True), D.prev)
                if c["sink"] is not None:
                    se = SE[:, u, :]
                    D(stt(nm, c["sink"], -1.0, nm, ALU.mult, ALU.min), D.prev)
                    D(tt(se, c["sink"], nm, ALU.add), D.prev)
                tok[u]["m"] = D.prev

            def exps(u):
                sv, nm = sbuf(u), NM[:, u, :]
                for h in range(2):
                    A(act(sv[:, h, :], sv[:, h, :], ACT.Exp, bias=nm[:, h:h + 1], accum_out=DN[:, u, h:h + 1]),
                      tok[u]["m"])
                if units[u]["sink"] is not None:
                    A(act(SE[:, u, :], SE[:, u, :], ACT.Exp), tok[u]["m"])
                tok[u]["e"] = A.prev

            def norm(u):
                sv, dn = sbuf(u), DN[:, u, :]
                if units[u]["sink"] is not None:
                    D(tt(dn, dn, SE[:, u, :], ALU.add), tok[u]["e"])
                D(lambda e: e.reciprocal(dn, dn), tok[u]["e"], D.prev)
                r = D.prev
                for h in range(2):
                    D(ts(sv[:, h, :], sv[:, h, :], dn[:, h:h + 1], None, ALU.mult), r)
                tok[u]["n"] = D.prev

            def turn(u):
                nk = units[u]["K"] // 128
                sv = sbuf(u)
                bk = 2 + u % 2
                tok[u]["t"] = tps([(bank(bk, 2 * nk, 128)[:, h * nk + kb, :], sv[:, h, kb * 128:(kb + 1) * 128], ident)
                                   for h in range(2) for kb in range(nk)], [tok[u]["n"], fr[bk]])

            def copy(u):
                bk = 2 + u % 2
                war = tok[u - 3]["o"] if u >= 3 else None
                pt = pbuf(u)
                A(act(pt, bank(bk, units[u]["K"] // 64, 128), ACT.Copy), tok[u]["t"], war)
                tok[u]["pt"] = A.prev
                fr[bk] = [A.prev]

            def values(u):
                c = units[u]
                nk = c["K"] // 128
                bk = 4 + u % 2
                pt = pbuf(u)
                tok[u]["o"] = mms([(ps[bk][64 * h:64 * h + 64, 0:128], c["v"][h][kb], pt[:, h * nk + kb, :],
                                    kb == 0, kb == nk - 1) for h in range(2) for kb in range(nk)],
                                  [tok[u]["pt"], fr[bk]])

            def out_copy(u):
                bk = 4 + u % 2
                A(act(units[u]["o"], ps[bk][:, 0:128], ACT.Copy), tok[u]["o"])
                fr[bk] = [A.prev]
                att_out[u] = A.prev

            stages = [scores, mask, exps, norm, turn, copy, values, out_copy]
            for step in range(n + len(stages) - 1):
                for k in range(len(stages) - 1, -1, -1):
                    if 0 <= step - k < n:
                        stages[k](step - k)
                att_r[0] = A.prev
                yield

        att_r = [None]
        att_out = {}
        ATT_ST = 24576
        oT = V(OO, 8, 256)
        units = []
        for fam in range(2):
            qt, kt, d = ((qt1, kt1, 96), (qt2, kt2, 64))[fam]
            for hp in range(4):
                for t in range(2):
                    K = 128 * (t + 1)
                    hs = (2 * hp, 2 * hp + 1)
                    if fam == 0:
                        vv = [[kv4[:, kb, h, 64:128] for kb in range(2)] for h in hs]
                    else:
                        vv = [[proj[:, kb, 1440 + 64 * h:1504 + 64 * h] for kb in range(2)] for h in hs]
                    units.append(dict(K=K, q=[qt[0:d, h, t * 128:(t + 1) * 128] for h in hs],
                                      k=[kt[0:d, h, 0:K] for h in hs], v=vv, bias=None, sink=None,
                                      o=oT[:, 4 * fam + hp, t * 128:(t + 1) * 128]))

        def att_ready(u):
            if u < 8:
                return [prep["kt1"], prep["qt1"], kv_r, got_in]
            return [prep["t2"], pj_tok[3], got_in]

        def mixer0():
            moba = moba_prep()
            steps = attention(units, att_ready)
            for step in range(8):
                next(steps)
                next(moba, None)
                yield
            for _ in moba:
                pass
            yield from steps

        def prepare():
            yield from mla_prep()
            yield from moba_scale()

        side = prepare()
        weave(block(2, 6), side)
        weave(block(3, 6), side)
        for _ in side:
            pass
        heads_banks[0] = (6, 7)
        for _ in mixer0():
            pass
        heads_banks[0] = (2, 3, 4, 5)
        att = att_r[0]

        def mix_out(wname, ready, gate=None, side=iter(())):
            for j in range(2):
                def done(t, bk, tk, j=j):
                    xs = xr[:, t, 512 * j:512 * (j + 1)]
                    if gate is None:
                        D(tt(xs, bank(bk, 512), xs, ALU.add), tk)
                    else:
                        tmp = V(OFF_HN + 512 * t, 512)
                        D(tt(tmp, bank(bk, 512), gate[:, 512 * j:512 * (j + 1)], ALU.mult), tk)
                        D(tt(xs, tmp, xs, ALU.add), D.prev)
                    fr[bk] = [D.prev]
                weave(lin_tok_steps(wname, 512, (HH, HL), ready, done, 6 if gate is not None and j == 0 else 2 * j), side)
            return [D.prev, D.prev]

        oT_r = []
        for c in range(4):
            oT_r += cut_act(HH[:, 2 * c:2 * c + 2, :], HL[:, 2 * c:2 * c + 2, :], oT[:, 2 * c:2 * c + 2, :], att, P.prev)
        x_r = mix_out("w_o", oT_r)

        EO, BO, WO, CI = 16384, 8192, 10240, 13312
        CO = stat(16)
        cond = ar[:, CO:CO + 8]
        ct2 = ar[:, CO + 8:CO + 16]
        MT = OFF_ST + NST - 32
        modT = V(MT, 4, 8)
        gb = V(OFF_GB, 2, 1024)

        def ada_setup():
            A(act(ct2, sm("c"), ACT.Exp, scale=-1.0), got_in)
            D(ts(ct2, ct2, 1.0, None, ALU.add), A.prev)
            D(lambda e: e.reciprocal(ct2, ct2), D.prev)
            D(tt(cond, ct2, sm("c"), ALU.mult), D.prev)

        ADA = [OFF_X + 15872, OFF_X + 16128]
        ada_mm = [None, None]
        ada_at = dict(n=0, loaded=0, stop=0, pending=None)
        ada_used = {}

        def ada_slot(n):
            return V((CI, CI + 512, OFF_HN + 1024, OFF_HN + 1536)[n % 4], 512)

        def ada_fetch(n, *after):
            if n < ada_at["stop"]:
                A.dma(lambda e, n=n: e.dma_start(ada_slot(n), T["w_ada"][n]), ada_sem[n % 4], ada_used.get(n - 4),
                      *after)

        def ada_part(stop, *after):
            ada_at["stop"] = stop
            for n in range(ada_at["n"], ada_at["n"] + 3):
                ada_fetch(n, *after)

        def ada_load():
            n = ada_at["n"]
            if n >= ada_at["stop"]:
                return
            ada_fetch(n + 3, hn_free[0])
            ada_at["n"] += 1
            col, part = n // 4, n % 4
            landed = (ada_sem[n % 4], 16 * (n // 4 + 1))
            w = ada_slot(n).rearrange("p (k n) -> p k n", k=2)
            acc = V(ADA[col % 2], 256)
            for k in range(2):
                c = cond[:, 2 * part + k:2 * part + k + 1]
                if part == 0 and k == 0:
                    D(ts(acc, w[:, 0, :], c, None, ALU.mult), landed, ada_mm[col % 2], D.prev)
                else:
                    D(stt(acc, w[:, k, :], c, acc, ALU.mult, ALU.add), landed, D.prev)
            ada_used[n] = D.prev
            if part == 3:
                ada_at["pending"] = (col, acc, D.prev)

        hn_free = [None]

        def ada_use():
            if ada_at["pending"] is None:
                return
            n, acc, tok = ada_at["pending"]
            ada_at["pending"] = None
            part, j = n // 4, n % 4
            if part in (2, 5):
                tk = mms([(bank(7, 256), sm("ones"), acc, True, True)], [tok, fr[7]])
                g = gb[:, 0 if part == 2 else 1, 256 * j:256 * (j + 1)]
                D(tt(g, bank(7, 256), g, ALU.add), tk, got_gb)
            else:
                row = {0: 0, 1: 1, 3: 2, 4: 3}[part]
                tk = mms([(ps[7][:, m:m + 1], acc[:, 128 * m:128 * (m + 1)], sm("ones")[:, 0:1], True, True)
                          for m in range(2)], [tok, fr[7]])
                b0 = OFF_SM + SML["bada"][0] + 8 * row + 2 * j
                D(tt(modT[:, row, 2 * j:2 * j + 2], ps[7][:, 0:2], ar[:, b0:b0 + 2], ALU.add), tk)
            fr[7] = [D.prev]
            ada_mm[n % 2] = tk

        ada_setup()

        def cut_pair(src, n, *after):
            q = n % 4
            hi, lo = HQ[q]
            tok = cut_act(hi, lo, src, hq_free.get(q), *after)
            return [x.rearrange("p (m t) -> p m t", m=2) for x in (hi, lo)], tok

        hq_free = {}

        def down(name, units, src_of, ready_of, ada=False):
            nxt = None
            for q in range(4):
                hq_free[q] = P.prev
            nxt = cut_pair(src_of(0), 0, ready_of(0))
            for j in range(units // 2):
                (hi, lo), ok2 = nxt
                for m in range(2):
                    for hf in range(2):
                        h, l, ok, no = take(name)
                        lst = []
                        for t in range(2):
                            lst += p3(bank(2 + 2 * t + hf, 512), [x[:, m, t * 128:(t + 1) * 128] for x in (hi, lo)],
                                      (h, l), j == 0 and m == 0, j == units // 2 - 1 and m == 1)
                        tk = mms(lst, [ok, ok2] + (fr[2] + fr[3] + fr[4] + fr[5] if j == 0 and m == 0 else []))
                        hl_free[no] = tk
                        if m == 0 and hf == 0 and j + 1 < units // 2:
                            nxt = cut_pair(src_of(j + 1), j + 1, ready_of(j + 1))
                    if ada:
                        ada_use()
                        ada_load()
                hq_free[j % 4] = tk
            return tk

        def ffn(layer, x_ready, war, ada=False, side=None):
            hr = norm_T(sm("ffng")[:, 8 * layer:8 * layer + 8], x_ready, 0)
            if ada:
                hn_free[0] = P.prev
                ada_part(ada, hn_free[0])
            aT = V(0, 32, 256)
            done = {}
            for j in range(16):
                bk = j % 2
                for m in range(2):
                    tk = lin_T("w_ff1", bk, m, hr, fr[bk] if m == 0 else ())
                    if ada:
                        ada_use()
                        ada_load()
                    if side is not None:
                        next(side, None)
                d = aT[:, 2 * j:2 * j + 2, :]
                A(act(d, bank(bk, 2, 256), ACT.Relu), tk, war, hr)
                fr[bk] = [A.prev]
                done[j] = D(tt(d, d, d, ALU.mult), A.prev)
            tk = down("w_ff2", 32, lambda j: V(512 * j, 512), lambda j: done[j], ada)
            while ada and (ada_at["n"] < ada or ada_at["pending"]):
                ada_load()
                ada_use()
            toks = []
            for t in range(2):
                for hf in range(2):
                    b = 2 + 2 * t + hf
                    xs = xr[:, t, 512 * hf:512 * (hf + 1)]
                    D(tt(xs, bank(b, 512), xs, ALU.add), tk)
                    fr[b] = [D.prev]
                toks.append(D.prev)
            return toks, tk


        Er, Ei = V(EO, 32, 256), V(EO + 8192, 32, 256)
        s5t = V(CI + 1024, 40, 32)
        row = lambda k: s5t[:, k, :]

        def s5_prep(war):
            L, LI, LT = sm("lre"), sm("lim"), sm("ldt")
            (dt, xx, nn, rr, pp, s2n, em, ex, th, kk, sn, cs, hs, cm1, are, aim, den, cr, ci, t1, t2, pr, pi) = [
                row(k) for k in range(23)]
            LOG2E = 1.0 / math.log(2.0)

            A.dma(lambda e: e.dma_start(V(4096, 1024), T["b5"]), key_sem, war)
            A.dma(lambda e: e.dma_start(V(5120, 1024), T["c5"]), key_sem)
            bc_r = (key_sem, 32)

            def expo(x, want_em):
                D(ts(x, x, -87.0, 88.0, ALU.max, ALU.min), D.prev, war)
                D(ts(nn, x, LOG2E, 12582912.0, ALU.mult, ALU.add), D.prev)
                D(ts(nn, nn, 12582912.0, None, ALU.subtract), D.prev)
                D(stt(rr, nn, -0.693359375, x, ALU.mult, ALU.add), D.prev)
                D(stt(rr, nn, 2.12194440e-4, rr, ALU.mult, ALU.add), D.prev)
                D(ts(pp, rr, 1.0 / 5040, 1.0 / 720, ALU.mult, ALU.add), D.prev)
                for c in (1.0 / 120, 1.0 / 24, 1.0 / 6, 0.5, 1.0):
                    D(tt(pp, pp, rr, ALU.mult), D.prev)
                    D(ts(pp, pp, c, None, ALU.add), D.prev)
                D(tt(pp, pp, rr, ALU.mult), D.prev)
                D(ts(nn, nn, 127.0, 8388608.0, ALU.add, ALU.mult), D.prev)
                D(cp(s2n.bitcast(I32), nn), D.prev)
                D(tt(pp, pp, s2n, ALU.mult), D.prev)
                D(tt(ex, pp, s2n, ALU.add), D.prev)
                if want_em:
                    D(ts(em, s2n, 1.0, None, ALU.subtract))
                    D(tt(em, em, pp, ALU.add), D.prev)

            D(cp(xx, LT), got_in, D.prev, war)
            expo(xx, False)
            yield
            D(cp(dt, ex), D.prev)
            D(tt(xx, L, dt, ALU.mult), D.prev)
            expo(xx, True)
            yield
            D(tt(th, LI, dt, ALU.mult), D.prev)
            D(ts(kk, th, 1.0 / (2 * math.pi), 12582912.0, ALU.mult, ALU.add), D.prev)
            D(ts(kk, kk, 12582912.0, None, ALU.subtract), D.prev)
            c1 = 6.28125
            c2 = float(np.float32(2 * math.pi - c1))
            c3 = 2 * math.pi - c1 - c2
            for c in (c1, c2, c3):
                D(stt(th, kk, -c, th, ALU.mult, ALU.add), D.prev)
            D(ts(th, th, -3.1415925, 3.1415925, ALU.max, ALU.min), D.prev)
            D(stt(t1, th, -1.0, th, ALU.mult, ALU.max), D.prev)
            yield
            D(ts(t1, t1, -1.0, math.pi / 2, ALU.mult, ALU.add), D.prev)
            D(ts(t2, th, 0.5, None, ALU.mult), D.prev)
            A(act(sn, th, ACT.Sin), D.prev)
            A(act(cs, t1, ACT.Sin))
            A(act(hs, t2, ACT.Sin))
            D(tt(cm1, hs, hs, ALU.mult), A.prev)
            D(ts(cm1, cm1, -2.0, None, ALU.mult), D.prev)
            D(tt(are, em, cs, ALU.mult), D.prev)
            yield
            D(tt(are, are, cm1, ALU.add), D.prev)
            D(tt(aim, ex, sn, ALU.mult))
            D(tt(den, L, L, ALU.mult))
            D(tt(t1, LI, LI, ALU.mult))
            D(tt(den, den, t1, ALU.add), D.prev)
            yield
            D(lambda e: e.reciprocal(den, den), D.prev)
            D(tt(cr, are, L, ALU.mult))
            D(tt(t1, aim, LI, ALU.mult), D.prev)
            D(tt(cr, cr, t1, ALU.add), D.prev)
            D(tt(cr, cr, den, ALU.mult), D.prev)
            yield
            D(tt(ci, aim, L, ALU.mult))
            D(tt(t2, are, LI, ALU.mult), D.prev)
            D(tt(ci, ci, t2, ALU.subtract), D.prev)
            base = D(tt(ci, ci, den, ALU.mult), D.prev)
            G(lambda e: e.memset(Er[:, :, 0:1], 1.0), war)
            G(lambda e: e.memset(Ei[:, :, 0:1], 0.0))
            G(cp(pr, cs), base)
            G(cp(pi, sn))
            qr, qi, q1 = row(23), row(24), row(25)
            n = 1
            while n < 256:
                for o in range(0, n, 32):
                    w = min(32, n)
                    tm = V(OFF_HN, 32, w)
                    a, b = B(pr.unsqueeze(2), [128, 32, w]), B(pi.unsqueeze(2), [128, 32, w])
                    lo, up = slice(o, o + w), slice(n + o, n + o + w)
                    G(tt(tm, Ei[:, :, lo], b, ALU.mult), G.prev)
                    G(tt(Er[:, :, up], Er[:, :, lo], a, ALU.mult))
                    G(tt(Er[:, :, up], Er[:, :, up], tm, ALU.subtract), G.prev)
                    G(tt(tm, Er[:, :, lo], b, ALU.mult), G.prev)
                    G(tt(Ei[:, :, up], Ei[:, :, lo], a, ALU.mult))
                    G(tt(Ei[:, :, up], Ei[:, :, up], tm, ALU.add), G.prev)
                G(tt(qr, pr, pr, ALU.mult))
                G(tt(q1, pi, pi, ALU.mult))
                G(tt(qi, pr, pi, ALU.mult))
                G(tt(pr, qr, q1, ALU.subtract), G.prev)
                G(tt(pi, qi, qi, ALU.add), G.prev)
                n *= 2
            S5["e"] = G.prev
            yield
            bl = V(4096, 2, 8, 64)
            cl = V(5120, 2, 32, 16)
            hp = sm("hpar")
            for ri, dst in ((0, BTr), (1, BTi)):
                for h in range(2):
                    D(ts(dst[:, :, 64 * h:64 * h + 64], bl[:, ri, :, :], hp[:, h:h + 1], None, ALU.mult), bc_r)
                yield
            m1, m2 = V(6144, 32, 16), V(6656, 32, 16)
            c1, c2 = V(7168, 32, 16), V(7680, 32, 16)
            crb, cib = B(cr.unsqueeze(2), [128, 32, 16]), B(ci.unsqueeze(2), [128, 32, 16])
            D(tt(m1, cl[:, 0], crb, ALU.mult), bc_r, base)
            D(tt(m2, cl[:, 1], cib, ALU.mult))
            D(tt(c1, m1, m2, ALU.subtract), D.prev)
            yield
            D(tt(m1, cl[:, 0], cib, ALU.mult), D.prev)
            D(tt(m2, cl[:, 1], crb, ALU.mult), D.prev)
            D(tt(c2, m1, m2, ALU.add), D.prev)
            yield
            for h in range(2):
                mask = sm("bones")[:, 64 * h:64 * h + 1]
                D(ts(W1[:, :, 16 * h:16 * h + 16], c1, mask, 64.0, ALU.mult, ALU.mult), D.prev)
                D(ts(W1n[:, :, 16 * h:16 * h + 16], c1, mask, -64.0, ALU.mult, ALU.mult), D.prev)
                D(ts(W2[:, :, 16 * h:16 * h + 16], c2, mask, -64.0, ALU.mult, ALU.mult), D.prev)
                yield
            S5["tab"] = D.prev
            S5["r"] = ex

        S5 = {}
        BTr, BTi = V(BO, 8, 128), V(BO + 1024, 8, 128)
        W1, W1n, W2 = V(WO, 32, 32), V(WO + 1024, 32, 32), V(WO + 2048, 32, 32)
        side = s5_prep([att, x_r[1]])
        x_r, ff_last = ffn(0, x_r, att, ada=64, side=side)
        assert next(side, None) is None and "tab" in S5
        tab_r, e_ready, r_ap = S5["tab"], S5["e"], S5["r"]

        hr = norm_T(sm("mixg")[:, 8:16], x_r, 6144, extra=e_ready, cut=False)
        hT = V(6144, 8, 256)
        def ring5(base, n, m):
            return lambda q: [V(b + 256 * k, 256) for b in [base[q % m]] for k in range(n)]

        turned = ring5([0, 1024], 4, 2)
        vbuf = ring5([2048, 2560], 2, 2)
        hbuf = ring5([3072, 3584], 2, 2)
        backed = ring5([4096, 5120, CI], 4, 3)
        pe_c = {}
        ybank = [4, 5]
        bu = {}
        tq = [dict() for _ in range(32)]

        def s5_in(q):
            c, j = q // 4, q % 4
            bk = q % 4
            rows = slice(32 * j, 32 * j + 32)
            bu[q] = mms([(bank(bk, 2, 256)[:, 0, :], BTr[rows, c, :], hT[rows, c, :], True, True),
                         (bank(bk, 2, 256)[:, 1, :], BTi[rows, c, :], hT[rows, c, :], True, True)],
                        [hr, tab_r, fr[bk]])

        def s5_turn(q):
            bk = q % 4
            er, ei = Er[:, q, :], Ei[:, q, :]
            br, bi = bank(bk, 2, 256)[:, 0, :], bank(bk, 2, 256)[:, 1, :]
            a1, a2, a3, a4 = turned(q)
            v1, v2 = vbuf(q)
            war = tq[q - 2]["v"] if q > 1 else ff_last
            D(tt(a1, br, er, ALU.mult), bu[q], e_ready, war)
            D(tt(a2, bi, ei, ALU.mult))
            D(tt(a3, bi, er, ALU.mult))
            D(tt(a4, br, ei, ALU.mult))
            fr[bk] = [D.prev]
            dm = D.prev
            G(tt(v1, a1, a2, ALU.add), dm, tq[q - 2]["h"] if q > 1 else None)
            G(tt(v2, a3, a4, ALU.subtract))
            tq[q]["v"] = G.prev

        def s5_scan(q):
            v1, v2 = vbuf(q)
            h1, h2 = hbuf(q)
            rb = B(r_ap[:, q:q + 1], [128, 256])
            D(lambda e: e.tensor_tensor_scan(h1, rb, v1, 0.0, ALU.mult, ALU.add), tq[q]["v"],
              tq[q - 2]["a"] if q > 1 else None)
            D(lambda e: e.tensor_tensor_scan(h2, rb, v2, 0.0, ALU.mult, ALU.add))
            tq[q]["h"] = D.prev

        def s5_back(q):
            er, ei = Er[:, q, :], Ei[:, q, :]
            a1, a2, a3, a4 = backed(q)
            h1, h2 = hbuf(q)
            D(tt(a1, h1, er, ALU.mult), tq[q]["h"], pe_c.get(q - 3))
            D(tt(a4, h2, er, ALU.mult))
            G(tt(a2, h2, ei, ALU.mult), tq[q]["h"], pe_c.get(q - 3))
            G(tt(a3, h1, ei, ALU.mult))
            tq[q]["a"] = [D.prev, G.prev]

        def s5_out(q):
            c, j = q // 4, q % 4
            a1, a2, a3, a4 = backed(q)
            yb = ybank[c % 2]
            yo = ps[yb][32 * j:32 * j + 32, 0:256]
            pe_c[q] = mms([(yo, W1[:, q, :], a1, True, False), (yo, W1n[:, q, :], a2, False, False),
                           (yo, W2[:, q, :], a3, False, False), (yo, W2[:, q, :], a4, False, True)],
                          [tq[q]["a"], fr[yb] if j == 0 else None])

        def s5_gelu(q):
            c, j = q // 4, q % 4
            if j != 3:
                return
            yb = ybank[c % 2]
            ds = sm("dskip")[:, c:c + 1]
            g = V(OFF_HN + 256 * (c % 4), 256)
            D(stt(g, hT[:, c, :], ds, ps[yb][:, 0:256], ALU.mult, ALU.add), pe_c[q], gT_free.get(c - 4))
            fr[yb] = [D.prev]
            A(act(g, g, ACT.Gelu_apprx_tanh), D.prev)
            tk = cut_act(HH[:, c, :], HL[:, c, :], g, A.prev, ff_last)
            gT_free[c] = tk
            g_tok.extend(tk)

        gT_free = {}
        g_tok = []
        stages = [s5_in, s5_turn, s5_scan, s5_back, s5_out, s5_gelu]
        delay = [0, 2, 3, 4, 4, 5]
        for step in range(32 + delay[-1]):
            for f, d in zip(stages, delay):
                if 0 <= step - d < 32:
                    f(step - d)
        glu_free = {}
        for j in range(2):
            keep = {}
            def vals(t, bk, tk):
                keep[t] = (bk, tk)
            def gates(t, bk, tk, j=j):
                s = V(OFF_HN + 512 * t, 512)
                A(act(s, bank(bk, 512), ACT.Sigmoid), tk, glu_free.get(t))
                vb, vt = keep[t]
                D(tt(s, bank(vb, 512), s, ALU.mult), A.prev, vt)
                fr[vb] = [D.prev]
                fr[bk] = [A.prev]
                xs = xr[:, t, 512 * j:512 * (j + 1)]
                D(tt(xs, xs, s, ALU.add), D.prev)
                glu_free[t] = D.prev
            lin_tok("w_glu", 512, (HH, HL), g_tok, vals, 0 if j == 0 else 4)
            tk = lin_tok("w_glu", 512, (HH, HL), g_tok, gates, 2)
        x_r, ff_last = ffn(1, [D.prev, D.prev], [tk, D.prev], ada=96)

        gs = stat(8)
        gsc = ar[:, gs:gs + 8]
        D(stt(gsc, modT[:, 1, :], 1.0, sm("n1g"), ALU.add, ALU.mult), D.prev)
        hr = norm_T(gsc, x_r, 20480, shift=modT[:, 0, :], extra=D.prev)
        WB = 16384
        A.dma(lambda e: e.dma_start(V(WB, 2048), T["wbias"]), key_sem, ff_last, x_r)
        A.dma(lambda e: e.dma_start(V(WB + 2048, 256), T["wmask"]), key_sem)
        wb_in = (key_sem, 64)
        wb = V(WB, 8, 256)
        wb_r = D(tt(wb, wb, B(V(WB + 2048, 256).unsqueeze(1), [128, 8, 256]), ALU.add), wb_in)
        pj2 = V(4096, 2, 768)
        pj2_t = []
        for j, n in enumerate((512, 256)):
            def done(t, bk, tk, j=j, n=n):
                A(act(pj2[:, t, 512 * j:512 * j + n], bank(bk, n), ACT.Copy), tk, ff_last, x_r)
                fr[bk] = [A.prev]
            lin_tok("w_qkv", n, (HH, HL), by_k(hr), done, 2 * j)
            pj2_t.append(A.prev)
        CV, YC = 0, 14336
        cw = sm("convw").rearrange("p (j c) -> p j c", j=3)
        cvT = V(CV, 12, 256)
        cv = lambda k: cvT[:, k, :]
        yT = V(YC, 4, 256)
        y_r = {}

        def conv_chunk(c, ready):
            cg, hh, bg = cv(3 * c), cv(3 * c + 1), cv(3 * c + 2)
            y = yT[:, c, :]
            G(tt(cg, cg, hh, ALU.mult), ready)
            D(ts(y, cg, cw[:, 2, c:c + 1], None, ALU.mult), G.prev)
            D(stt(y[:, 1:256], cg[:, 0:255], cw[:, 1, c:c + 1], y[:, 1:256], ALU.mult, ALU.add), D.prev)
            D(stt(y[:, 2:256], cg[:, 0:254], cw[:, 0, c:c + 1], y[:, 2:256], ALU.mult, ALU.add), D.prev)
            y_r[c] = G(tt(y, y, bg, ALU.mult), D.prev)

        def conv_steps():
            for j in range(6):
                bk = 6 + j % 2
                for m in range(2):
                    for _ in lin_T_steps("w_conv", bk, m, hr, fr[bk] if m == 0 else ()):
                        yield
                A(act(cvT[:, 2 * j:2 * j + 2, :], bank(bk, 2, 256), ACT.Copy), P.prev, ff_last, x_r)
                fr[bk] = [A.prev]
                ready = A.prev
                yield
                if j in (1, 2, 4, 5):
                    conv_chunk({1: 0, 2: 1, 4: 2, 5: 3}[j], ready)

        sq = V(12288, 1536)
        KT3, QT3 = 6144, 7168
        qt3, kt3 = V(QT3, 8, 256), V(KT3, 2, 256)
        OO2 = 9216
        oT2 = V(OO2, 4, 256)
        units = []
        for hp in range(4):
            for t in range(2):
                K = 128 * (t + 1)
                hs = (2 * hp, 2 * hp + 1)
                kh = hp // 2
                so = OFF_SM + SML["sinks"][0] + 2 * hp
                units.append(dict(K=K, q=[qt3[0:64, h, t * 128:(t + 1) * 128] for h in hs],
                                  k=[kt3[0:64, kh, 0:K]] * 2,
                                  v=[[pj2[:, kb, 640 + 64 * kh:704 + 64 * kh] for kb in range(2)]] * 2,
                                  bias=wb[:, 2 * hp:2 * hp + 2, 128 * (1 - t):256], sink=ar[:, so:so + 2],
                                  o=oT2[:, hp, t * 128:(t + 1) * 128]))

        def window():
            sq_free[0] = [ff_last, x_r]
            for t in range(2):
                q = pj2[:, t, 0:512]
                yield from scale_heads(q.rearrange("p (a b) -> p a b", a=8), 8, 64, prep, ("q", t), pj2_t[0])
                yield
                k = pj2[:, t, 512:640]
                yield from scale_heads(k.rearrange("p (a b) -> p a b", a=2), 2, 64, prep, ("k", t), pj2_t[1])
                yield
                yield from heads_T(q, 8, 64, t, qt3, sm("qng", 64), prep["q", t], prep, "q3")
                yield from heads_T(k, 2, 64, t, kt3, sm("kng", 64), prep["k", t], prep, "k3")
            yield from attention(units, lambda u: [prep["q3"], prep["k3"], wb_r])

        w_ready = {}

        def group_rms(c, src, gain, sq_at, *after):
            s2 = V(sq_at, 2, 256)
            A(act(s2, src, ACT.Square), *after)
            bk = (6, 7, 0, 1)[c // 2]
            cols = sm("bones").rearrange("p (g n) -> p g n", g=2)[:, :, 0]
            tk = mms([(bank(bk, 2, 2, 2)[:, m, t, :], s2[:, m, 128 * t:128 * t + 128], cols, True, True)
                      for m in range(2) for t in range(2)], [A.prev, fr[bk]])
            yield
            so = stat(8)
            r = ar[:, so:so + 8]
            D(ts(r, bank(bk, 8), 1.0, EPS, ALU.mult, ALU.add), tk)
            fr[bk] = [D.prev]
            A(act(r, r, ACT.Sqrt), D.prev)
            rooted = A.prev
            yield
            D(lambda e, r=r: e.reciprocal(r, r), rooted)
            wide = V(sq_at, 8, 64)
            D(cp(wide, B(r.unsqueeze(2), [128, 8, 64])), D.prev)
            wide = V(sq_at, 4, 128)
            tk = mms([(bank(bk, 4, 128)[:, n, :], wide[:, n, :], ident, True, True) for n in range(4)],
                     [D.prev, fr[bk]])
            yield
            spread_r = bank(bk, 2, 256)
            for m in range(2):
                D(stt(src[:, m, :], src[:, m, :], gain[:, m:m + 1], spread_r[:, m, :], ALU.mult, ALU.mult), tk)
            A(act(HH[:, c:c + 2, :], src, ACT.Copy), D.prev, hT_free)
            hi = A.prev
            fr[bk] = [D.prev]
            D(tt(HL[:, c:c + 2, :], src, HH[:, c:c + 2, :].bitcast(F32), ALU.subtract), hi, hT_free)
            w_ready[c] = w_ready[c + 1] = [hi, D.prev]

        att_out.clear()
        side = window()
        weave(conv_steps(), side)
        hT_free = P.prev
        gens = [group_rms(c, yT[:, c:c + 2, :], sm("convg")[:, c:c + 2], 3072 + 256 * c, y_r[c], y_r[c + 1])
                for c in (0, 2)]
        for _ in side:
            for g in gens:
                next(g, None)
        for g in gens:
            for _ in g:
                pass
        gens = [group_rms(4 + c, oT2[:, c:c + 2, :], sm("attng")[:, c:c + 2], 10240 + 256 * c,
                          *[att_out[u] for u in range(2 * c, 2 * c + 4)]) for c in (0, 2)]

        def rest():
            for _ in range(4):
                for g in gens:
                    next(g, None)
                yield

        x_r = mix_out("w_out", lambda k: w_ready[k], gate=gb[:, 0, :], side=rest())

        gs = stat(8)
        gsc = ar[:, gs:gs + 8]
        D(stt(gsc, modT[:, 3, :], 1.0, sm("n2g"), ALU.add, ALU.mult), D.prev)
        hr = norm_T(gsc, x_r, 20480, shift=modT[:, 2, :], extra=D.prev)
        X = V(0, 128, 256)
        QP, SCO = 28672, 24576
        qp = V(QP, 16, 256)
        scs = V(SCO, 2, 16, 128)
        att_all = [D.prev, A.prev, P.prev]
        for j in range(8):
            bk = j % 2
            for m in range(2):
                tk = lin_T("peer_wq", bk, m, hr, fr[bk] if m == 0 else ())
            A(act(qp[:, 2 * j:2 * j + 2, :], bank(bk, 2, 256), ACT.Copy), tk, att_all)
            fr[bk] = [A.prev]
        qp_r = A.prev
        kw = [take_raw("keys") for _ in range(2)]
        sc_t = {}
        for b in range(4):
            src, landed, i = kw[b // 2]
            k8 = src.rearrange("p (a b) -> p a b", a=8)
            for t in range(2):
                bk = 2 + (4 * t + b) % 4
                tk = mms([(bank(bk, 4, 128)[:, m, :], qp[:, 4 * b + m, t * 128:(t + 1) * 128], k8[:, 4 * (b % 2) + m, :],
                           True, True) for m in range(4)], [landed, qp_r, fr[bk]])
                A(act(scs[:, t, 4 * b:4 * b + 4, :], bank(bk, 4, 128), ACT.Copy), tk)
                fr[bk] = [A.prev]
                sc_t[t] = A.prev
            raw_free[i] = [tk]
        scores_done = tk

        u_tok = {}
        u_scr = {}

        def u_pair(j):
            for m in range(2):
                yield from lin_T_steps("peer_u", j % 2, m, hr, fr[j % 2] if m == 0 else ())
            u_done[j] = P.prev

        u_done = {}

        def u_out(j, spread_to=0, ready=None):
            bk, tk = j % 2, u_done[j]
            xs = X[:, 2 * j:2 * j + 2, :]
            toks = []
            if spread_to < 256:
                A(act(xs[:, :, spread_to:256], bank(bk, 2, 256)[:, :, spread_to:256], ACT.Gelu_apprx_tanh), tk, ready,
                  att_all)
                toks.append(A.prev)
            if spread_to > 0:
                w = V(OFF_SCR, 2, 256)[:, :, 0:spread_to]
                A(act(w, bank(bk, 2, 256)[:, :, 0:spread_to], ACT.Gelu_apprx_tanh), tk, u_scr.get(0))
                fr[bk] = [A.prev]
                D(tt(xs[:, :, 0:spread_to], xs[:, :, 0:spread_to], w, ALU.mult), A.prev, ready)
                u_scr[0] = D.prev
                toks.append(D.prev)
            fr[bk] = [A.prev]
            u_tok[j] = toks

        SEL = QP
        TVa, TIa, TIf = V(SEL, 16, 16), V(SEL + 256, 16, 16), V(SEL + 512, 16, 16)
        CAND = V(SEL + 768, 8, 16, 16)
        CAND2 = V(SEL + 768, 8, 256)
        EQ = V(SEL + 768, 128, 16)
        EQ4 = V(SEL + 768, 8, 256).rearrange("p h (k i) -> p h k i", k=16)
        TV, TI = V(SEL + 2816, 8, 16), V(SEL + 2944, 8, 16)
        PI, PJ = V(SEL + 3072, 128), V(SEL + 3200, 128)
        PIf, PJf = V(SEL + 3328, 128), V(SEL + 3456, 128)
        RIA = [V(SEL + 3584 + 128 * m, 128) for m in range(3)]
        SUM = V(SEL + 3968, 8)
        TMP = [V(OFF_HN + 256 * m, 256) for m in range(2)]
        picked = {}

        def top16(jobs, *after):
            tok = [list(after), list(after)]
            ops = [lambda e, src, tv, ti, tmp: e.max(tv[:, 0:8], src),
                   lambda e, src, tv, ti, tmp: e.max_index(ti[:, 0:8].bitcast(U32), tv[:, 0:8], src),
                   lambda e, src, tv, ti, tmp: e.match_replace(tmp, tv[:, 0:8], src, NEG * 10),
                   lambda e, src, tv, ti, tmp: e.max(tv[:, 8:16], tmp),
                   lambda e, src, tv, ti, tmp: e.max_index(ti[:, 8:16].bitcast(U32), tv[:, 8:16], tmp)]
            n = 0
            for op in ops:
                for m, job in enumerate(jobs):
                    tok[m] = D(lambda e, op=op, job=job: op(e, *job), tok[m])
                    n += 1
                    if n == 5:
                        yield

        def select():
            for t in range(2):
                for m in range(0, 16, 2):
                    yield from top16([(scs[:, t, i, :], TVa[:, i, :], TIa[:, i, :], TMP[i % 2][:, 0:128])
                                      for i in (m, m + 1)], sc_t[t], D.prev, scores_done)
                    yield
                D(cp(TIf, TIa.bitcast(U32)), D.prev)
                va = TVa.rearrange("p (h a) k -> p h a k", a=2)
                for q in (slice(0, 4), slice(4, 8)):
                    D(tt(CAND[:, q], B(va[:, q, 0, :].unsqueeze(3), [128, 4, 16, 16]),
                         B(va[:, q, 1, :].unsqueeze(2), [128, 4, 16, 16]), ALU.add), D.prev)
                    yield
                for h in range(0, 8, 2):
                    yield from top16([(CAND2[:, i, :], TV[:, i, :], TI[:, i, :], TMP[i % 2]) for i in (h, h + 1)],
                                     D.prev)
                    yield
                tiu = V(SEL + 2944, 128).bitcast(U32)
                D(lambda e: e.tensor_scalar(PI.bitcast(U32), tiu, 4, None, ALU.logical_shift_right), D.prev)
                D(lambda e: e.tensor_scalar(PJ.bitcast(U32), tiu, 15, None, ALU.bitwise_and))
                D(cp(PIf, PI.bitcast(U32)), D.prev)
                D(cp(PJf, PJ.bitcast(U32)), D.prev)
                yield
                fi = TIf.rearrange("p (h a) k -> p h a k", a=2)
                for which, pf in ((0, PIf), (1, PJf)):
                    for q in range(2):
                        r, h4 = slice(64 * q, 64 * q + 64), slice(4 * q, 4 * q + 4)
                        D(tt(EQ[:, r, :], B(pf[:, r].unsqueeze(2), [128, 64, 16]),
                             B(sm("iota16").unsqueeze(1), [128, 64, 16]), ALU.is_equal), D.prev)
                        yield
                        D(tt(EQ4[:, h4], EQ4[:, h4], B(fi[:, h4, which, :].unsqueeze(2), [128, 4, 16, 16]), ALU.mult),
                          D.prev)
                        yield
                        D(lambda e, which=which, r=r: e.tensor_reduce(RIA[which][:, r], EQ[:, r, :], AX.X, ALU.add),
                          D.prev, picked.get(t - 1))
                        yield
                R3 = RIA[2].rearrange("p (h k) -> p h k", h=8)
                D(tt(R3, TV, B(TV[:, :, 0:1], [128, 8, 16]), ALU.subtract), D.prev)
                A(act(R3, R3, ACT.Exp), D.prev)
                yield
                D(lambda e, R3=R3: e.tensor_reduce(SUM, R3, AX.X, ALU.add), A.prev)
                D(lambda e: e.reciprocal(SUM, SUM), D.prev)
                D(tt(R3, R3, B(SUM.unsqueeze(2), [128, 8, 16]), ALU.mult), D.prev)
                sel_done = D.prev
                yield
                tk = tps([(bank(6, 4, 128)[:, m, :], RIA[m], ident) for m in range(3)], [sel_done, fr[6]])
                picked[t] = tk
                itv = V(OFF_GB, 3, 256)[:, :, t * 128:(t + 1) * 128]
                D(cp(itv, bank(6, 4, 128)[:, 0:3, :]), tk, att_all)
                fr[6] = [D.prev]
                picked["all"] = D.prev
                yield

        side = select()
        for j in range(NGA // 2):
            for n, _ in enumerate(u_pair(j)):
                if n % 2:
                    next(side, None)
            u_out(j)
        for _ in side:
            pass
        it_r = picked["all"]
        iaT, ibT, gT_ = V(OFF_GB, 256), V(OFF_GB + 256, 256), V(OFF_GB + 512, 256)
        nib, ng = V(OFF_GB + 768, 64, 2), V(OFF_GB + 896, 64, 2)
        D(ts(nib, ibT.rearrange("p (s k) -> p s k", k=4)[:, :, 2:4], -1.0, None, ALU.mult), it_r)
        D(ts(ng, gT_.rearrange("p (s k) -> p s k", k=4)[:, :, 2:4], -1.0, None, ALU.mult), it_r)
        it_r = [it_r, D.prev]
        iota = sm("iota")
        oh_free = {}
        spread_q = []

        def evac_g(s, bk, tk, cols):
            gv = bank(bk, 4, 128).rearrange("p t b -> p b t")
            xs = X[:, 0:cols, 4 * s:4 * s + 4]
            D(tt(xs, gv[:, 0:cols, :], xs, ALU.mult), tk, *[u_tok[j] for j in range(cols // 2)])
            fr[bk] = [D.prev]
            copies.append((s, bk, cols, D.prev))

        copies = []

        def evac_rest():
            for s, bk, cols, tok in copies:
                if cols < 128:
                    gv = bank(bk, 4, 128).rearrange("p t b -> p b t")
                    A(act(X[:, cols:128, 4 * s:4 * s + 4], gv[:, cols:128, :], ACT.Copy), tok, it_r)
                    fr[bk] = [A.prev]
            copies.clear()

        def spread_ones(s):
            oa = V(OFF_HN + 1024 * (s % 2), 4, 128)
            ob = V(OFF_HN + 1024 * (s % 2) + 512, 4, 128)
            before = [it_r, oh_free.get(s - 2)]
            ia4 = B(iaT[:, 4 * s:4 * s + 4].unsqueeze(2), [128, 4, 128])
            D(tt(oa, ia4, B(iota.unsqueeze(1), [128, 4, 128]), ALU.is_equal), *before)
            made = [D.prev]
            for k in range(4):
                n = 4 * s + k
                g1 = gT_[:, n:n + 1]
                if k == 0:
                    made.append(D(ts(ob[:, k, :], iota, ibT[:, n:n + 1], g1, ALU.is_equal, ALU.mult), *before))
                elif k == 1 or k == 2 and s % 2:
                    made.append(G(ts(ob[:, k, :], iota, ibT[:, n:n + 1], g1, ALU.is_equal, ALU.mult), *before))
                else:
                    A(act(ob[:, k, :], iota, ACT.Abs, bias=nib[:, s, k - 2:k - 1]), *before)
                    made.append(A(act(ob[:, k, :], ob[:, k, :], ACT.Relu, bias=g1, scale=ng[:, s, k - 2:k - 1]), A.prev))
            return oa, ob, made

        def spread_mm(s, oa, ob, made):
            bk = 2 + s % 4
            tk = mms([(bank(bk, 4, 128)[:, k, :], oa[:, k, :], ob[:, k, :], True, True) for k in range(4)],
                     made + [fr[bk]])
            oh_free[s] = tk
            spread_q.append((s, bk, tk))

        cuts_left = ((j, n) for j in range(NGA // 2, 64) for n in range(4))
        total = 4 * (64 - NGA // 2)
        s, evaced, known, late, gen, ones = 0, 0, NGA // 2, None, None, None
        for i, (j, n) in enumerate(cuts_left):
            due = s < 64 and (i + 1) * 64 >= (s + 1) * (total - 4)
            if n == 0:
                gen = u_pair(j)
            next(gen)
            if n == 3:
                next(gen, None)
            evac_rest()
            if due:
                if ones is not None:
                    spread_mm(*ones)
                ones = (s, *spread_ones(s))
                s += 1
                if len(spread_q) > 1:
                    evac_g(*spread_q.pop(0), 2 * known)
                    evaced += 1
            if late is not None:
                evac_rest()
                u_out(late, 4 * evaced, [it_r, A.prev, D.prev])
                known += 1
                late = None
            if n == 3:
                late = j
        assert s == 64
        spread_mm(*ones)
        while spread_q:
            evac_g(*spread_q.pop(0), 2 * known)
            evac_rest()
            evaced += 1
        u_out(late, 256, [A.prev, D.prev])
        spread = [D.prev, A.prev]
        tk = down("peer_v", 128, lambda j: V(512 * j, 512), lambda j: [spread, u_tok[j]])
        outd = out.rearrange("a (t p) d -> p (a t) d", p=128)
        for t in range(2):
            for hf in range(2):
                b = 2 + 2 * t + hf
                xs = xr[:, t, 512 * hf:512 * (hf + 1)]
                tmp = V(OFF_HN + 512 * (2 * t + hf), 512)
                D(tt(tmp, bank(b, 512), gb[:, 1, 512 * hf:512 * (hf + 1)], ALU.mult), tk, spread)
                D(tt(xs, tmp, xs, ALU.add), D.prev)
            A.dma(lambda e, t=t: e.dma_start(outd[:, t, :], xr[:, t, :]), out_sem, D.prev)
        A.wait((out_sem, 32))

        assert at["plan"] == len(plan)
        loads = Line(nc.sync, None)
        loads.wait(got_x)
        for i, (_, ap, words, _) in enumerate(plan):
            loads.dma(lambda e, ap=ap, i=i: e.dma_start(raw(i)[0], ap), ring_sem[i % NRAW], raw_free.get(i - NRAW))

        block = ctx.enter_context(nc.Block())

        @block.sync
        def _(e):
            loads.run()

        @block.scalar
        def _(e):
            A.run()

        @block.gpsimd
        def _(e):
            G.run()

        @block.vector
        def _(e):
            D.run()

        @block.tensor
        def _(e):
            P.run()



def _cols(v, n):
    return np.ascontiguousarray(v.reshape(n, 128).T)


def _rows(v):
    o = np.zeros((128, 1), np.float32)
    o[:len(v), 0] = v
    return o


def _units_T(w):
    n = w.shape[1] // 128
    return w.reshape(8, 128, n, 128).transpose(2, 1, 0, 3).reshape(n, 128, 1024)


def _units_tok(w, width=512):
    n = w.shape[1] // width
    return w.reshape(4, 2, 128, n, width).transpose(3, 0, 2, 1, 4).reshape(4 * n, 128, 2 * width)


def _bucket(dist):
    d = np.maximum(dist, 1).astype(np.float32)
    large = 16 + (np.log(d / np.float32(16)) / np.float32(math.log(8.0)) * np.float32(16)).astype(np.int32)
    return np.where(dist < 16, dist, np.minimum(large, 31))


def _arrays(a):
    f = np.float32
    p = np.arange(128)
    sml = {}
    sml["ident"] = np.eye(128, dtype=f)
    sml["cmask"] = np.where(p[None, :] <= p[:, None], 0.0, NEG).astype(f)
    sml["iota"] = np.broadcast_to(p.astype(f), (128, 128))
    sml["bones"] = np.where(p[None, :] // 64 == p[:, None] // 64, 1.0 / 64, 0.0).astype(f)
    sml["ones"] = np.ones((128, 128), f)
    inv = f(10000.0) ** (-np.arange(16, dtype=f) / f(16))
    ang = np.arange(256, dtype=f)[:, None] * inv[None, :]
    for n, fn in (("cos", np.cos), ("sin", np.sin)):
        sml[n] = fn(ang).astype(f).reshape(2, 128, 16).transpose(1, 0, 2).reshape(128, 32)
    h = (p // 16) % 2
    sml["hpar"] = np.stack([h == 0, h == 1], 1).astype(f)
    sml["iota16"] = np.broadcast_to(np.arange(16, dtype=f), (128, 16))
    sml["mixg"] = np.concatenate([_cols(a["mix_norm_g"][l], 8) for l in range(2)], 1)
    sml["ffng"] = np.concatenate([_cols(a["ffn_norm_g"][l], 8) for l in range(2)], 1)
    sml["n1g"] = _cols(a["norm1_g_2"][0], 8)
    sml["n2g"] = _cols(a["norm2_g_2"][0], 8)
    sml["gcq"] = _cols(a["g_cq"][0], 2)
    sml["gckv"] = _cols(a["g_ckv"][0], 1)
    for n, k in (("gqmla", "g_qn_mla"), ("gkmla", "g_kn_mla"), ("gqmoba", "g_qn_moba"), ("gkmoba", "g_kn_moba"),
                 ("qng", "q_norm_g_2"), ("kng", "k_norm_g_2")):
        sml[n] = _rows(a[k][0])
    sml["c"] = _cols(a["c_2"][0], 8)
    ba = a["b_ada_2"][0].reshape(6, 1024)
    sml["bada"] = np.concatenate([_cols(ba[r], 8) for r in (0, 1, 3, 4)], 1)
    sml["convw"] = np.concatenate([_cols(a["conv_w_2"][0][j], 4) for j in range(3)], 1)
    sml["convg"] = _cols(a["conv_out_g_2"][0], 4)
    sml["attng"] = _cols(a["attn_out_g_2"][0], 4)
    sml["dskip"] = _cols(a["d_skip"][0], 8)
    sml["sinks"] = np.broadcast_to(a["sinks_2"][0], (128, 8))
    st = lambda v: v.reshape(32, 128).T
    sml["lre"] = st(a["lam_re"][0])
    sml["lim"] = st(a["lam_im"][0])
    sml["ldt"] = st(np.repeat(a["log_dt"][0][:, None], 64, 1))
    small = np.concatenate([np.broadcast_to(sml[n], (128, w)).astype(f) for n, (_, w) in SML.items()], 1)
    r = {"small": small, "x": a["x"][0]}
    r["gb"] = np.broadcast_to(np.concatenate([ba[2], ba[5]]), (128, 2048))
    w = a["w_in"][0]
    for j in range(3):
        r[f"w_in{j}"] = _units_tok(w[:, 512 * j:512 * j + 512])
    r["w_in3"] = _units_tok(w[:, 1536:], 416)
    r["w_uq"] = a["w_uq"][0].reshape(2, 128, 768)
    r["w_ukv"] = a["w_ukv"][0]
    r["w_o"] = _units_tok(a["w_o"][0])
    r["w_ff1"] = np.stack([_units_T(a["w_ff1"][l]) for l in range(2)])
    r["w_ff2"] = a["w_ff2"].reshape(2, 32, 128, 1024)
    r["w_ada"] = a["w_ada_2"][0].reshape(4, 2, 128, 24, 256).transpose(3, 0, 2, 1, 4).reshape(96, 128, 512)
    glu = _units_tok(a["w_glu"][0])
    r["w_glu"] = np.concatenate([glu[4 * n:4 * n + 4] for n in (0, 2, 1, 3)])
    b = np.stack([a["b_re"][0], a["b_im"][0]])
    r["b5"] = b.reshape(2, 8, 4, 2, 64, 16).transpose(2, 3, 5, 0, 1, 4).reshape(128, 1024)
    c = np.stack([a["c_re"][0], a["c_im"][0]])
    r["c5"] = c.reshape(2, 32, 2, 16, 64).transpose(2, 4, 0, 1, 3).reshape(128, 1024)
    w = a["w_in_2"][0]
    order = [w[:, off + 128 * k:off + 128 * k + 128] for k in range(4) for off in (512, 1024, 0)]
    r["w_conv"] = _units_T(np.concatenate(order, 1))
    r["w_qkv0"] = _units_tok(w[:, 1536:2048])
    r["w_qkv1"] = _units_tok(w[:, 2048:], 256)
    r["w_out"] = _units_tok(a["w_out_2"][0])
    dist = p[:, None] + 128 - np.arange(256)[None, :]
    r["wbias"] = a["rel_bias_2"][_bucket(np.maximum(dist, 0))].transpose(0, 2, 1).reshape(128, 2048)
    r["wmask"] = np.where((dist >= 0) & (dist < 128), 0.0, NEG).astype(f)
    r["peer_wq"] = _units_T(a["peer_wq_2"][0])
    r["keys"] = a["peer_keys_2"][0].transpose(3, 1, 0, 2).reshape(128, 2, 1024).transpose(1, 0, 2)
    u = a["peer_u_2"][0].reshape(128, 128, 8, 128)
    r["peer_u"] = u.transpose(1, 3, 2, 0).reshape(128, 128, 1024)
    r["peer_v"] = a["peer_v_2"][0].reshape(128, 128, 1024).transpose(1, 0, 2)
    return {k: np.ascontiguousarray(v) for k, v in r.items()}


def kernel(**inputs):
    import concourse.bacc as _bacc
    from concourse import mybir as _mybir
    from concourse.bass_utils import run_bass_kernel_spmd as _run

    nc = _bacc.Bacc("TRN2", target_bir_lowering=False, num_devices=1)
    arrays = _arrays({k: np.asarray(v) for k, v in inputs.items()})
    T = {}
    feed = {}
    for name, v in arrays.items():
        feed[f"in_{name}"] = v
        T[name] = nc.dram_tensor(f"in_{name}", v.shape, _mybir.dt.from_np(v.dtype), kind="ExternalInput").ap()
    out = nc.dram_tensor("out_0", (1, 256, 1024), F32, kind="ExternalOutput").ap()
    build(nc, T, out)
    r = _run(nc, [feed], core_ids=[0])
    return r.results[0]["out_0"]
```
